# Optimizing a Trainium2 kernel written in Bass

```python
import math
import jax, jax.numpy as jnp
from jax import lax
import numpy as np

D_MODEL = 1024
BATCH = 1
SEQ = 512
DEPTH = 1

EPS = 1e-6
D_MIX = D_MODEL
RET_HEADS = 4
RET_DK = 128
RET_DV = 128
RET_WIDTH = RET_HEADS * RET_DV
RET_CHUNK = 128
RET_ROPE_THETA = 10000.0
DIFF_HEADS = 4
DIFF_DH = 64
DIFF_DV = 2 * DIFF_DH
DIFF_WIDTH = DIFF_HEADS * DIFF_DV
Q_BLOCK = 128
ROPE_THETA = 500000.0
ROT_DIM = DIFF_DH // 4
RET_Q = RET_HEADS * RET_DK
RET_K = RET_HEADS * RET_DK
RET_V = RET_HEADS * RET_DV
RET_G = RET_WIDTH
DIFF_Q = DIFF_HEADS * 2 * DIFF_DH
DIFF_K = DIFF_HEADS * 2 * DIFF_DH
DIFF_V = DIFF_HEADS * DIFF_DV
SPLITS = [RET_Q, RET_K, RET_V, RET_G, DIFF_Q, DIFF_K, DIFF_V]
D_IN_PROJ = sum(SPLITS)
N_EXPERTS = 32
TOP_K = 4
D_FF = D_MODEL
SWIGLU_LIMIT = 7.0
SWIGLU_ALPHA = 1.702
MOE_BLOCK = 128

kernel_name = "hybrid_retention_diffattn_moe_encoder"

def rms_norm(x, w):
    xf = x.astype(jnp.float32)
    y = xf * lax.rsqrt(jnp.mean(xf * xf, axis=-1, keepdims=True) + EPS)
    return (y * w.astype(jnp.float32)).astype(x.dtype)

def rotary_cos_sin(positions, inv_freq):
    ang = positions.astype(jnp.float32)[..., None] * inv_freq
    return jnp.cos(ang), jnp.sin(ang)

def apply_rotary(x, cos, sin):
    xf = x.astype(jnp.float32)
    half = xf.shape[-1] // 2
    x1, x2 = xf[..., :half], xf[..., half:]
    out = jnp.concatenate([x1 * cos - x2 * sin, x2 * cos + x1 * sin], axis=-1)
    return out.astype(x.dtype)

def retention_one_direction(q, k, v, log_decay, include_diag):
    B, H, S, dk = q.shape
    dv = v.shape[-1]
    C = RET_CHUNK
    NC = S // C
    qc = q.reshape(B, H, NC, C, dk)
    kc = k.reshape(B, H, NC, C, dk)
    vc = v.reshape(B, H, NC, C, dv)
    idx = jnp.arange(C, dtype=jnp.float32)
    dist = idx[:, None] - idx[None, :]
    mask = (dist >= 0) if include_diag else (dist > 0)
    ld = log_decay.astype(jnp.float32)
    decay_mat = jnp.where(mask[None], jnp.exp(ld[:, None, None] * jnp.where(mask, dist, 0.0)[None]), 0.0)
    scores = jnp.einsum("bhcnd,bhcmd->bhcnm", qc, kc) * decay_mat[None, :, None]
    intra = jnp.einsum("bhcnm,bhcme->bhcne", scores, vc)
    k_decay = jnp.exp(ld[:, None] * (C - 1 - idx)[None])
    kv = jnp.einsum("bhcmd,hm,bhcme->bhcde", kc, k_decay, vc)
    chunk_decay = jnp.exp(ld * C)[None, :, None, None]

    def step(state, kv_i):
        return state * chunk_decay + kv_i, state

    _, prev = lax.scan(step, jnp.zeros((B, H, dk, dv), jnp.float32), jnp.moveaxis(kv, 2, 0))
    prev = jnp.moveaxis(prev, 0, 2)
    q_decay = jnp.exp(ld[:, None] * (idx + 1.0)[None])
    cross = jnp.einsum("bhcnd,bhcde->bhcne", qc, prev) * q_decay[None, :, None, :, None]
    return (intra + cross).reshape(B, H, S, dv)

def retention_group(q_raw, k_raw, v_raw, g_raw, positions, log_decay_fwd, log_decay_bwd, norm_w):
    B, S, _ = q_raw.shape
    inv_freq = RET_ROPE_THETA ** (-jnp.linspace(0.0, 1.0, RET_DK // 2, dtype=jnp.float32))
    cos, sin = rotary_cos_sin(positions, inv_freq)
    cos, sin = cos[:, :, None, :], sin[:, :, None, :]
    q = apply_rotary(q_raw.reshape(B, S, RET_HEADS, RET_DK), cos, sin)
    k = apply_rotary(k_raw.reshape(B, S, RET_HEADS, RET_DK), cos, sin) * (RET_DK ** -0.5)
    v = v_raw.reshape(B, S, RET_HEADS, RET_DV)
    q = jnp.transpose(q, (0, 2, 1, 3)).astype(jnp.float32)
    k = jnp.transpose(k, (0, 2, 1, 3)).astype(jnp.float32)
    v = jnp.transpose(v, (0, 2, 1, 3)).astype(jnp.float32)
    y_fwd = retention_one_direction(q, k, v, log_decay_fwd, True)
    y_bwd = jnp.flip(retention_one_direction(jnp.flip(q, 2), jnp.flip(k, 2), jnp.flip(v, 2), log_decay_bwd, False), 2)
    y = jnp.transpose(y_fwd + y_bwd, (0, 2, 1, 3))
    y = rms_norm(y, norm_w.reshape(RET_HEADS, RET_DV))
    y = y.reshape(B, S, RET_WIDTH) * jax.nn.silu(g_raw.astype(jnp.float32))
    return y.astype(q_raw.dtype)

def diff_attention_group(q_raw, k_raw, v_raw, positions, q_norm_w, k_norm_w,
                         lq1, lk1, lq2, lk2, sub_norm_w, lambda_init):
    B, S, _ = q_raw.shape
    q = rms_norm(q_raw.reshape(B, S, DIFF_HEADS, 2, DIFF_DH), q_norm_w)
    k = rms_norm(k_raw.reshape(B, S, DIFF_HEADS, 2, DIFF_DH), k_norm_w)
    inv_freq = ROPE_THETA ** (-jnp.arange(0, ROT_DIM, 2, dtype=jnp.float32) / ROT_DIM)
    cos, sin = rotary_cos_sin(positions, inv_freq)
    cos, sin = cos[:, :, None, None, :], sin[:, :, None, None, :]
    q = jnp.concatenate([apply_rotary(q[..., :ROT_DIM], cos, sin), q[..., ROT_DIM:]], axis=-1)
    k = jnp.concatenate([apply_rotary(k[..., :ROT_DIM], cos, sin), k[..., ROT_DIM:]], axis=-1)
    q = jnp.transpose(q, (0, 2, 3, 1, 4))
    k = jnp.transpose(k, (0, 2, 3, 1, 4))
    v = jnp.transpose(v_raw.reshape(B, S, DIFF_HEADS, DIFF_DV), (0, 2, 1, 3)).astype(jnp.float32)
    lam = (jnp.exp(jnp.sum(lq1.astype(jnp.float32) * lk1.astype(jnp.float32)))
           - jnp.exp(jnp.sum(lq2.astype(jnp.float32) * lk2.astype(jnp.float32))) + lambda_init)
    scale = DIFF_DH ** -0.5
    n_blocks = S // Q_BLOCK
    q_blocks = jnp.moveaxis(q.reshape(B, DIFF_HEADS, 2, n_blocks, Q_BLOCK, DIFF_DH), 3, 0)

    def attend(q_blk):
        s = jnp.einsum("bhcqd,bhckd->bhcqk", q_blk, k).astype(jnp.float32) * scale
        p = jax.nn.softmax(s, axis=-1)
        a = p[:, :, 0] - lam * p[:, :, 1]
        return jnp.einsum("bhqk,bhkd->bhqd", a, v)

    o = lax.map(attend, q_blocks)
    o = jnp.transpose(o, (1, 0, 3, 2, 4)).reshape(B, S, DIFF_HEADS, DIFF_DV)
    o = rms_norm(o, sub_norm_w) * (1.0 - lambda_init)
    return o.reshape(B, S, DIFF_WIDTH).astype(q_raw.dtype)

def moe_ffn(h, w_router, b_router, w1, b1, w2, b2):
    B, S, D = h.shape
    T = B * S
    ht = h.reshape(T, D)
    logits = (ht @ w_router + b_router).astype(jnp.float32)
    top_val, top_idx = lax.top_k(logits, TOP_K)
    gates = jax.nn.softmax(top_val, axis=-1)
    A = T * TOP_K
    e_flat = top_idx.reshape(A).astype(jnp.int32)
    tok_flat = jnp.arange(A, dtype=jnp.int32) // TOP_K
    g_flat = gates.reshape(A)
    order = jnp.argsort(e_flat, stable=True)
    e_sorted, tok_sorted, g_sorted = e_flat[order], tok_flat[order], g_flat[order]
    counts = jnp.zeros((N_EXPERTS,), jnp.int32).at[e_flat].add(1)
    starts = jnp.cumsum(counts) - counts
    padded = ((counts + MOE_BLOCK - 1) // MOE_BLOCK) * MOE_BLOCK
    pad_end = jnp.cumsum(padded)
    pad_start = pad_end - padded
    dest = pad_start[e_sorted] + (jnp.arange(A, dtype=jnp.int32) - starts[e_sorted])
    P = A + N_EXPERTS * MOE_BLOCK
    NB = P // MOE_BLOCK
    tok_buf = jnp.full((P,), T, jnp.int32).at[dest].set(tok_sorted)
    gate_buf = jnp.zeros((P,), jnp.float32).at[dest].set(g_sorted)
    block_e = jnp.minimum(jnp.searchsorted(pad_end, jnp.arange(NB, dtype=jnp.int32) * MOE_BLOCK, side="right"),
                          N_EXPERTS - 1).astype(jnp.int32)
    h_pad = jnp.concatenate([ht, jnp.zeros((1, D), ht.dtype)], axis=0)
    x_blocks = h_pad[tok_buf].reshape(NB, MOE_BLOCK, D)

    def expert_block(args):
        xb, e = args
        u = xb @ w1[e] + b1[e]
        glu = jnp.minimum(u[:, :D_FF], SWIGLU_LIMIT)
        lin = jnp.clip(u[:, D_FF:], -SWIGLU_LIMIT, SWIGLU_LIMIT)
        act = glu * jax.nn.sigmoid(SWIGLU_ALPHA * glu) * (lin + 1.0)
        return act @ w2[e] + b2[e]

    y_blocks = lax.map(expert_block, (x_blocks, block_e))
    y = y_blocks.reshape(P, D).astype(jnp.float32) * gate_buf[:, None]
    out = jax.ops.segment_sum(y, tok_buf, num_segments=T + 1)[:T]
    return out.reshape(B, S, D).astype(h.dtype)

def setup_inputs(seed: int = 0) -> dict:
    key = jax.random.key(seed)
    ks = jax.random.split(key, 24)
    f32 = jnp.float32
    nrm = lambda k, shape, s: jax.random.normal(k, shape, f32) * s
    x = jax.random.normal(ks[0], (BATCH, SEQ, D_MODEL), f32)
    offsets = jax.random.randint(ks[1], (BATCH, 1), 0, 1024, dtype=jnp.int32)
    positions = (jnp.arange(SEQ, dtype=jnp.int32)[None, :] + offsets).astype(jnp.int32)
    base_decay = jnp.log(1.0 - 2.0 ** (-5.0 - jnp.arange(RET_HEADS, dtype=f32)))
    ret_log_decay_fwd = base_decay[None] * (1.0 + 0.05 * jax.random.normal(ks[2], (DEPTH, RET_HEADS), f32))
    ret_log_decay_bwd = base_decay[None] * (1.0 + 0.05 * jax.random.normal(ks[3], (DEPTH, RET_HEADS), f32))
    return {
        "x": x,
        "positions": positions,
        "norm1_w": 1.0 + nrm(ks[4], (DEPTH, D_MODEL), 0.02),
        "w_in": nrm(ks[5], (DEPTH, D_MODEL, D_IN_PROJ), D_MODEL ** -0.5),
        "ret_log_decay_fwd": ret_log_decay_fwd,
        "ret_log_decay_bwd": ret_log_decay_bwd,
        "ret_norm_w": 1.0 + nrm(ks[6], (DEPTH, RET_WIDTH), 0.02),
        "q_norm_w": 1.0 + nrm(ks[7], (DEPTH, DIFF_DH), 0.02),
        "k_norm_w": 1.0 + nrm(ks[8], (DEPTH, DIFF_DH), 0.02),
        "lambda_q1": nrm(ks[9], (DEPTH, DIFF_DH), 0.1),
        "lambda_k1": nrm(ks[10], (DEPTH, DIFF_DH), 0.1),
        "lambda_q2": nrm(ks[11], (DEPTH, DIFF_DH), 0.1),
        "lambda_k2": nrm(ks[12], (DEPTH, DIFF_DH), 0.1),
        "diff_norm_w": 1.0 + nrm(ks[13], (DEPTH, DIFF_DV), 0.02),
        "w_out": nrm(ks[14], (DEPTH, D_MIX, D_MODEL), D_MIX ** -0.5),
        "norm2_w": 1.0 + nrm(ks[15], (DEPTH, D_MODEL), 0.02),
        "w_router": nrm(ks[16], (DEPTH, D_MODEL, N_EXPERTS), D_MODEL ** -0.5),
        "b_router": nrm(ks[17], (DEPTH, N_EXPERTS), 0.01),
        "w1": nrm(ks[18], (DEPTH, N_EXPERTS, D_MODEL, 2 * D_FF), D_MODEL ** -0.5),
        "b1": nrm(ks[19], (DEPTH, N_EXPERTS, 2 * D_FF), 0.01),
        "w2": nrm(ks[20], (DEPTH, N_EXPERTS, D_FF, D_MODEL), D_FF ** -0.5),
        "b2": nrm(ks[21], (DEPTH, N_EXPERTS, D_MODEL), 0.01),
    }

def reference(x, positions, norm1_w, w_in, ret_log_decay_fwd, ret_log_decay_bwd, ret_norm_w,
              q_norm_w, k_norm_w, lambda_q1, lambda_k1, lambda_q2, lambda_k2, diff_norm_w,
              w_out, norm2_w, w_router, b_router, w1, b1, w2, b2):
    split_points = list(np.cumsum(SPLITS)[:-1])
    for l in range(DEPTH):
        lambda_init = 0.8 - 0.6 * math.exp(-0.3 * l)
        h = rms_norm(x, norm1_w[l])
        proj = h @ w_in[l]
        rq, rk, rv, rg, dq, dk, dv = jnp.split(proj, split_points, axis=-1)
        y_ret = retention_group(rq, rk, rv, rg, positions, ret_log_decay_fwd[l], ret_log_decay_bwd[l], ret_norm_w[l])
        y_diff = diff_attention_group(dq, dk, dv, positions, q_norm_w[l], k_norm_w[l],
                                      lambda_q1[l], lambda_k1[l], lambda_q2[l], lambda_k2[l],
                                      diff_norm_w[l], lambda_init)
        mixed = jnp.concatenate([y_ret, y_diff], axis=-1)
        x = x + (mixed @ w_out[l]).astype(x.dtype)
        h2 = rms_norm(x, norm2_w[l])
        x = x + moe_ffn(h2, w_router[l], b_router[l], w1[l], b1[l], w2[l], b2[l])
    return x


_drawn_inputs = setup_inputs


def setup_inputs(seed=0):
    import zlib

    import numpy as np

    out = dict(_drawn_inputs(seed))
    spreads = {}
    factors = {'ret_norm_w': 11.084,
     'lambda_k1': 6.234,
     'b_router': 8.816,
     'b1': 23.205,
     'b2': 26.69,
     'q_norm_w': 2.929,
     'k_norm_w': 3.428,
     'diff_norm_w': 3.378,
     'norm2_w': 2.809}
    for name, (base, spread) in spreads.items():
        noise = np.random.default_rng([zlib.crc32(name.encode()), seed]).standard_normal(out[name].shape)
        drawn = base * np.exp(spread * noise) if base else spread * noise
        out[name] = __import__('jax').numpy.asarray(drawn.astype(out[name].dtype))
    for name, factor in factors.items():
        out[name] = (out[name] * factor).astype(out[name].dtype)
    return out
```

```python
from contextlib import ExitStack

import concourse.bass as bass
from concourse import mybir
import numpy as np

P = 128
D = 1024
T = 512
NB = T // P
KD = D // P
HEADS = 4
DV = 128
DH = 64
ROT = DH // 4
NF8 = ROT // 2
NE = 32
TOPK = 4
W = 512
EPS = 1e-6
LIMIT = 7.0
ALPHA = 1.702
LAMBDA_INIT = 0.2
RING = 12
SLOT = 2048
CAP = 96
MAX_CHUNK = -(-T // CAP)
MAX_OVER = 24
CHUNKS = 6
W1_COLS = [0, D, W, D + W]
ORDER = [0, 3, 5, 4, 1, 2]
FRONT_LOADS = [3, 3, 3, 0, 0, 0]
DIST = 896

PK = {}
_at = 0
for _n, _w in (("n1w", KD), ("n2w", KD), ("retw", HEADS), ("diffw", 1), ("invcol", 1), ("inv8", NF8), ("ldf", HEADS),
               ("ldb", HEADS), ("qw", DH), ("kw", DH), ("lam", 4 * DH), ("brt", NE)):
    PK[_n] = (_at, _at + _w)
    _at += _w
NPAR = _at

GROUPS = [("Qd", 2048), ("Kd", 2560), ("Vd", 3072), ("Vr", 1024), ("G", 1536), ("Qr", 0), ("Kr", 512)]

TWO_PI = 2 * np.pi
C1 = 6.28125
C2 = float(np.float32(np.round((TWO_PI - C1) * 2**17) / 2**17))
C3 = float(np.float32(TWO_PI - C1 - C2))
MAGIC = 1.5 * 2.0**23
PI_LOW = 3.1415925


def build_layer(nc, x, w_in, w_out, w_router, w1, b1t, w2, b2t, par, pos, h2_rows, out):
    f32, i32, u32 = mybir.dt.float32, mybir.dt.int32, mybir.dt.uint32
    f32r = mybir.dt.float32r
    ALU, ACT, AX = mybir.AluOpType, mybir.ActivationFunctionType, mybir.AxisListType

    ctx = ExitStack()
    with ctx:
        def sb(name, shape, dt=f32):
            return ctx.enter_context(nc.sbuf_tensor(name, shape, dt))

        def sem(name):
            return ctx.enter_context(nc.semaphore(name))

        ring = sb("ring", [P, RING, SLOT])
        X = sb("X", [P, NB, D])
        HT = sb("HT", [P, KD * T])
        hT = HT[:, :].rearrange("p (k t) -> p k t", k=KD)
        h2 = HT[:, :].rearrange("p (b d) -> p b d", b=NB)
        par_sb = sb("par_sb", [P, NPAR])
        ident = sb("ident", [P, P])
        before = sb("before", [P, P])
        ones = sb("ones", [P, P])
        swap = sb("swap", [P, P])
        iota_s = sb("iota_s", [P, P])
        wr_sb = sb("wr_sb", [P, KD, NE])
        small = sb("small", [P, 1000])
        small_used = [0]

        def tiny(*shape):
            n = int(np.prod(shape))
            a = small[:, small_used[0]:small_used[0] + n]
            small_used[0] += n
            if len(shape) == 2:
                a = a.rearrange("p (a b) -> p a b", a=shape[0])
            if len(shape) == 3:
                a = a.rearrange("p (a b c) -> p a b c", a=shape[0], b=shape[1])
            return a

        ssx, msx, rsx = tiny(2 * NB), tiny(2 * NB), tiny(2 * NB)
        ssq, msq, rsq = tiny(2, 32), tiny(2, 32), tiny(2, 32)
        negmax, rowsum, rowinv, lamc = tiny(32), tiny(32), tiny(32), tiny(16)
        sso, mso, rso = tiny(2, 16), tiny(2, 16), tiny(2, 16)
        lamt, lam2, neglam, dw = tiny(2), tiny(2), tiny(1), tiny(1)
        top8, topf, ev, gate4, esum = tiny(NB, 8), tiny(NB, 8), tiny(NB, TOPK), tiny(NB, TOPK), tiny(NB)
        idx8 = sb("idx8", [P, NB, 8], u32)
        gate_y = tiny(1)
        gate_s = tiny(2)
        over_top = tiny(MAX_OVER)
        over_n = tiny(1)
        over_some = tiny(MAX_OVER)
        over_at = sb("over_at", [P, MAX_OVER + 1], i32)
        over_e = sb("over_e", [P, MAX_OVER], i32)
        place_idx = sb("place_idx", [P, 2], u32)

        arena = sb("arena", [P, 15872])

        def cut(at, n, *split):
            a = arena[:, at:at + n]
            if len(split) == 2:
                return a.rearrange("p (a b) -> p a b", a=split[0])
            if len(split) == 3:
                return a.rearrange("p (a b c) -> p a b c", a=split[0], b=split[1])
            return a

        def slots(s, n, parts):
            return ring[:, s:s + n, :].rearrange("p s c -> p (s c)").rearrange("p (a b) -> p a b", a=parts)

        NANG = T + NB * NF8
        rq, rk = cut(0, 2048, NB, W), cut(2048, 2048, NB, W)
        qrT, krT = cut(0, 2048, HEADS, T), cut(2048, 2048, HEADS, T)
        decay = cut(4096, HEADS * DIST, HEADS, DIST)
        h2T = cut(4096, 2048, 2, D)
        cosT, sinT = cut(7680, W), cut(8192, W)
        xs = cut(8704, 2048, 2, D)
        prob = cut(8704, 2048, 4, W)
        yrow = cut(8704, 2048, NB, W)
        ang, turns, red = cut(10752, NANG), cut(10752 + NANG, NANG), cut(10752 + 2 * NANG, 2 * NANG, 2, NANG)
        dist = cut(10752 + 4 * NANG, DIST)
        dtmp = cut(10752 + 4 * NANG + DIST, DIST)
        pos_sb = cut(4096, T + NB).bitcast(i32)
        ropet = cut(10752, 1024, 4, NB * 8 * NF8)
        amix = cut(10752, 1024, 2, W)
        std = cut(10752, 1024, 2, W)
        aT = cut(11776, 1024, 2, W)
        qsb = cut(12800, 1024, 2, W)
        roped = cut(13824, 1024, 2, W)
        sig = cut(12800, 2048)
        sqs = cut(14848, 1024)
        cs_row = sb("cs_row", [P, 2, NB * NF8])
        orow = slots(6, 1, NB)
        qdT = slots(7, 1, HEADS)
        kdT = slots(8, 1, HEADS)
        vd = slots(9, 1, NB)
        mixT = slots(8, 2, KD)
        vr = slots(10, 1, NB)
        gg = slots(11, 1, NB)
        posm = cut(0, MAX_CHUNK * NE * NB, MAX_CHUNK, NE, NB)
        b1_sb = cut(768, NE * 16, NE, 16)
        b2_sb = cut(1280, NE * KD, NE, KD)
        idgate = cut(1536, NE * NB * 2, NE, NB, 2)
        logits, mask = cut(1792, NB * NE, NB, NE), cut(1920, NB * NE, NB, NE)
        eq, gts = cut(2048, NB * NE, NB, NE), cut(2176, NB * NE, NB, NE)
        over_key = cut(2048, (MAX_CHUNK - 1) * NE, MAX_CHUNK - 1, NE)
        ub, sg = cut(2304, 8 * CAP, 2, 4 * CAP), cut(3072, 4 * CAP, 2, 2 * CAP)
        actT = cut(3456, KD * CAP, KD, CAP)
        ybT = cut(6144, KD * CAP, KD, CAP)
        htE = cut(6912, 2 * KD * CAP, 2, KD * CAP)
        onehot = cut(8448, NB * CAP, NB, CAP)
        hrow = HT[0:CAP, 0:2 * D].rearrange("p (q d) -> p q d", q=2)
        cmat = sb("cmat", [CAP, 2, T], f32r)
        yhi, ylo = sb("yhi", [CAP, D], f32r), sb("ylo", [CAP, D], f32r)

        ps = ctx.enter_context(nc.psum_tensor("ps", [P, 8, W], f32))

        x_in = [sem(f"x_in{b}") for b in range(NB)]
        par_in, pos_in, wr_in, b1_in, b2_in = sem("par_in"), sem("pos_in"), sem("wr_in"), sem("b1_in"), sem("b2_in")
        ring_in = [sem(f"ring_in{s}") for s in range(RING)]
        consts, consts0 = sem("consts"), sem("consts0")
        dve, act_own = sem("dve_chain"), sem("act_chain")
        sq_x, ms_x, sd_x, rs_x, xs_ready, xT_done, hT_ready = (sem(n) for n in (
            "sq_x", "ms_x", "sd_x", "rs_x", "xs_ready", "xT_done", "hT_ready"))
        red_ready, trig_ready, dexp_in, dexp_ready, lam_in, lam_exp = (sem(n) for n in (
            "red_ready", "trig_ready", "dexp_in", "dexp_ready", "lam_in", "lam_exp"))
        proj_done, proj_evac, sq_used, ms_q, sd_q, qk_ready = (sem(n) for n in (
            "proj_done", "proj_evac", "sq_used", "ms_q", "sd_q", "qk_ready"))
        qkT_done, qkT_evac, rot_done, rope_done = (sem(n) for n in ("qkT_done", "qkT_evac", "rot_done", "rope_done"))
        sc_done, max_ready, exp_done, comb_done, aT_done, aT_evac, av_done, o_evac, o_sq = (sem(n) for n in (
            "sc_done", "max_ready", "exp_done", "comb_done", "aT_done", "aT_evac", "av_done", "o_evac", "o_sq"))
        ms_o, sd_o, o_ready, mixT_done, mixT_ready = (sem(n) for n in ("ms_o", "sd_o", "o_ready", "mixT_done", "mixT_ready"))
        sig_g, st_done, std_ready, yv_done, y_evac, y_sq = (sem(n) for n in (
            "sig_g", "st_done", "std_ready", "yv_done", "y_evac", "y_sq"))
        op_done, res_ready, h2_ready, h2T_done, h2T_ready, lg_done, lg_ready = (sem(n) for n in (
            "op_done", "res_ready", "h2_ready", "h2T_done", "h2T_ready", "lg_done", "lg_ready"))
        ev_in, ev_ready, mask_ready, rank_done, pos_ready, h2_stored = (sem(n) for n in (
            "ev_in", "ev_ready", "mask_ready", "rank_done", "pos_ready", "h2_stored"))
        over_ready = sem("over_ready")
        b_in, gate_ready, fetches = sem("b_in"), sem("gate_ready"), sem("fetches")
        row_in = [sem(f"row_in{q}") for q in range(2)]
        (hot_ready, idx_done, idx_ready, hrT_done, htE_ready, up_done, ub_ready, glu_ready, lin_ready, gl_ready,
         sg_ready, act_ready, chunk_used, down_done, yb_ready, yT_done, yhi_ready, y_ready, ct_done, c_ready, cmb_done,
         cmb_added, out_done) = (sem(n) for n in (
             "hot_ready", "idx_done", "idx_ready", "hrT_done", "htE_ready", "up_done", "ub_ready", "glu_ready",
             "lin_ready", "gl_ready", "sg_ready", "act_ready", "chunk_used", "down_done", "yb_ready", "yT_done",
             "yhi_ready", "y_ready", "ct_done", "c_ready", "cmb_done", "cmb_added", "out_done"))

        def pcols(name):
            a, b = PK[name]
            return par_sb[:, a:b]

        def bank(b, a=0, n=W):
            return ps[:, b, a:a + n]

        def wide(b):
            return ps[:, b:b + 2, :]

        def spread(ap, n):
            return ap.unsqueeze(len(ap.shape)).to_broadcast(list(ap.shape) + [n])

        x_v = x.rearrange("a (b p) d -> (a b) p d", p=P)
        out_v = out.rearrange("a (b p) d -> (a b) p d", p=P)
        w_in_v = w_in.rearrange("a (k p) n -> p (a k) n", p=P)
        w_out_v = w_out.rearrange("a (k p) n -> p (a k) n", p=P)
        w1_v = w1.rearrange("a e (k p) n -> (a e) p k n", p=P)
        w2_v = w2.rearrange("a e (k p) n -> (a e) p k n", p=P)
        h2_v = h2_rows.rearrange("(b p) d -> b p d", p=P)

        def pair(s):
            return ring[:, s:s + 2, :].rearrange("p s (k n) -> p (s k) n", n=W)

        def over_count(eng):
            return eng.value_load(over_at[0:1, MAX_OVER:MAX_OVER + 1], min_val=0, max_val=MAX_OVER)

        def further(eng, one_pass):
            eng.wait_ge(over_ready, 1)
            n_over = over_count(eng)
            with eng.If(n_over > 0):
                with eng.Fori(0, n_over) as j:
                    at = eng.value_load(over_at[0:1, bass.ds(j, 1)], min_val=0, max_val=MAX_CHUNK * NE - 1)
                    e = eng.value_load(over_e[0:1, bass.ds(j, 1)], min_val=0, max_val=NE - 1)
                    one_pass(j + NE, e, at)

        block = ctx.enter_context(nc.Block())

        @block.sync
        def _(sp):
            for b in range(NB):
                sp.dma_start(X[:, b, :], x_v[b]).then_inc(x_in[b], 16)
            for g, (_, c) in enumerate(GROUPS):
                if g >= 3:
                    sp.wait_ge(proj_done, 4 * (g - 2))
                sp.dma_start(pair(2 * (g % 3)), w_in_v[:, :, c:c + W]).then_inc(ring_in[2 * (g % 3)], 16)
            for n in range(2):
                sp.wait_ge(proj_done, 4 * (5 + n))
                sp.dma_start(pair(2 + 2 * n), w_out_v[:, :, n * W:(n + 1) * W]).then_inc(ring_in[2 + 2 * n], 16)

            def load(e, c):
                if c < 4:
                    src = w1_v[bass.ds(e, 1), :, :, W1_COLS[c]:W1_COLS[c] + W]
                else:
                    src = w2_v[bass.ds(e, 1), :, :, (c - 4) * W:(c - 3) * W]
                sp.dma_start(pair(2 * ORDER[c]), src.rearrange("a p k n -> p (a k) n")).then_inc(ring_in[2 * ORDER[c]], 16)

            for c in range(CHUNKS):
                s = ORDER[c]
                if c == 0:
                    sp.wait_ge(proj_done, 4 * 7)
                if s == 3:
                    sp.wait_ge(mixT_done, NB)
                    sp.wait_ge(sc_done, 2 * NB * HEADS)
                if s == 4:
                    sp.wait_ge(op_done, 2 * NB)
                if s == 5:
                    sp.wait_ge(yv_done, NB * HEADS)
                    sp.wait_ge(o_ready, 2)
                if s == 1:
                    sp.wait_ge(op_done, 2 * NB)
                load(0, c)

            def weights(n, e):
                for c in range(CHUNKS):
                    if c in (0, 2):
                        sp.wait_ge(chunk_used, 2 * n + (c // 2 - 1))
                    elif c < 4:
                        sp.wait_ge(up_done, 4 * n + (c - 3))
                    else:
                        sp.wait_ge(down_done, 2 * n + (c - 5))
                    load(e, c)

            with sp.Fori(1, NE) as n:
                weights(n, n)
            further(sp, lambda n, e, at: weights(n, e))
            n_over = over_count(sp)
            for b in range(NB):
                sp.wait_ge(cmb_added, 8 * n_over + (8 * (NE - 1) + 2 * (b + 1)))
                sp.dma_start(out_v[b], X[:, b, :]).then_inc(out_done, 16)
            sp.wait_ge(out_done, 16 * NB)

        @block.gpsimd
        def _(pool):
            nc.gpsimd.memset(ident[:, :], 0.0).then_inc(consts0, 1)
            nc.gpsimd.memset(before[:, :], 1.0).then_inc(consts0, 1)
            nc.gpsimd.memset(swap[:, :], 0.0).then_inc(consts0, 1)
            nc.gpsimd.memset(ones[:, :], 1.0).then_inc(consts0, 1)
            pool.wait_ge(consts0, 4)
            nc.gpsimd.affine_select(out=ident[:, :], in_=ident[:, :], compare_op=ALU.not_equal, fill=1.0, base=0,
                                    pattern=[[-1, P]], channel_multiplier=1).then_inc(consts, 1)
            nc.gpsimd.affine_select(out=before[:, :], in_=before[:, :], compare_op=ALU.is_gt, fill=0.0, base=0,
                                    pattern=[[1, P]], channel_multiplier=-1).then_inc(consts, 1)
            nc.gpsimd.affine_select(out=swap[:, :], in_=swap[:, :], compare_op=ALU.not_equal, fill=-1.0, base=-DH,
                                    pattern=[[-1, P]], channel_multiplier=1).then_inc(consts0, 1)
            pool.wait_ge(consts0, 5)
            nc.gpsimd.affine_select(out=swap[:, :], in_=swap[:, :], compare_op=ALU.not_equal, fill=1.0, base=DH,
                                    pattern=[[-1, P]], channel_multiplier=1).then_inc(consts, 1)
            nc.gpsimd.iota(iota_s[:, :], pattern=[[1, P]], base=0, channel_multiplier=0,
                           allow_small_or_imprecise_dtypes=True).then_inc(consts, 1)
            nc.gpsimd.iota(dist, pattern=[[1, DIST]], base=-(T - P), channel_multiplier=-1,
                           allow_small_or_imprecise_dtypes=True).then_inc(consts, 1)
            pool.wait_ge(yv_done, NB * HEADS)
            nc.gpsimd.iota(idgate[:, :, :, 0], pattern=[[0, NE], [P, NB]], base=0, channel_multiplier=1,
                           allow_small_or_imprecise_dtypes=True).then_inc(consts, 1)

            def fetch(n, q):
                pool.wait_ge(idx_ready, n + 1)
                pool.sem_inc(fetches, 1)
                nc.gpsimd.indirect_dma_start(hrow[:, q, :], None, h2_rows,
                                             bass.IndirectOffsetOnAxis(ap=place_idx[0:CAP, q:q + 1], axis=0)
                                             ).then_inc(row_in[q], 16)

            pool.wait_ge(h2_stored, 16 * NB)
            fetch(0, 0)
            with pool.Fori(0, NE // 2 - 1) as i:
                fetch(2 * i + 1, 1)
                fetch(2 * i + 2, 0)
            fetch(NE - 1, 1)
            further(pool, lambda n, e, at: fetch(n, 0))

        @block.scalar
        def _(act):
            own = [0]

            def link(ins):
                own[0] += 1
                ins.then_inc(act_own, 1)
                act.wait_ge(act_own, own[0])

            act.dma_start(par_sb[:, :], par).then_inc(par_in, 16)
            act.dma_start(pos_sb, pos).then_inc(pos_in, 16)
            act.dma_start(wr_sb[:, :, :], w_router.rearrange("a (k p) e -> p (a k) e", p=P)).then_inc(wr_in, 16)
            for b in range(NB):
                act.wait_ge(x_in[b], 16)
                nc.scalar.activation(sqs, X[:, b, :], ACT.Square, accum_out=ssx[:, b:b + 1]).then_inc(sq_x, 1)
                act.wait_ge(sq_x, b + 1)
                act.wait_ge(ms_x, b + 1)
                nc.scalar.activation(msx[:, b:b + 1], msx[:, b:b + 1], ACT.Sqrt).then_inc(sd_x, 1)
                act.wait_ge(rs_x, b + 1)
                if b >= 2:
                    act.wait_ge(xT_done, b - 1)
                nc.scalar.activation(xs[:, b % 2, :], X[:, b, :], ACT.Copy, scale=rsx[:, b:b + 1]).then_inc(xs_ready, 1)
            act.wait_ge(red_ready, 1)
            nc.scalar.activation(sinT, red[:, 0, 0:T], ACT.Sin)
            nc.scalar.activation(cosT, red[:, 1, 0:T], ACT.Sin)
            nc.scalar.activation(cs_row[:, :, :], red[:, :, T:NANG], ACT.Sin).then_inc(trig_ready, 1)
            act.wait_ge(dexp_in, 1)
            act.wait_ge(lam_in, 1)
            nc.scalar.activation(decay, decay, ACT.Exp).then_inc(dexp_ready, 1)
            nc.scalar.activation(lam2, lamt, ACT.Exp).then_inc(lam_exp, 1)

            def evac(j):
                g, i = divmod(j, 4)
                name = GROUPS[g][0]
                act.wait_ge(proj_done, j + 1)
                src = bank(j % 2)
                if name in ("Qd", "Kd"):
                    if j >= 2:
                        act.wait_ge(sq_used, j - 1)
                    nc.scalar.activation((rq if name == "Qd" else rk)[:, i, :], src, ACT.Copy)
                    nc.scalar.activation(sqs[:, (j % 2) * W:(j % 2 + 1) * W], src, ACT.Square).then_inc(proj_evac, 1)
                elif name in ("Qr", "Kr"):
                    r = j - 20
                    if r >= 2:
                        act.wait_ge(rope_done, r - 1)
                    nc.scalar.activation(qsb[:, j % 2, :], src, ACT.Copy,
                                         scale=1.0 if name == "Qr" else P ** -0.5).then_inc(proj_evac, 1)
                else:
                    dst = {"Vd": vd, "Vr": vr, "G": gg}[name]
                    nc.scalar.activation(dst[:, i, :], src, ACT.Copy).then_inc(proj_evac, 1)

            for j in range(8):
                evac(j)
            act.wait_ge(ms_q, 1)
            nc.scalar.activation(msq[:, 0, :], msq[:, 0, :], ACT.Sqrt).then_inc(sd_q, 1)
            act.wait_ge(ms_q, 2)
            nc.scalar.activation(msq[:, 1, :], msq[:, 1, :], ACT.Sqrt).then_inc(sd_q, 1)
            for j in range(8, 12):
                evac(j)
            for g, dst in enumerate((qdT, kdT)):
                for i in range(NB):
                    act.wait_ge(qkT_done, 4 * g + i + 1)
                    nc.scalar.activation(dst[:, :, i * P:(i + 1) * P],
                                         bank(3 + i).rearrange("p (h t) -> p h t", h=HEADS), ACT.Copy,
                                         scale=DH ** -0.5 if g == 0 else 1.0).then_inc(qkT_evac, 1)

            def a_out(u):
                act.wait_ge(aT_done, u + 1)
                if u >= 2:
                    act.wait_ge(av_done, u - 1)
                nc.scalar.activation(aT[:, u % 2, :], bank(7), ACT.Copy).then_inc(aT_evac, 1)

            def o_out(i):
                act.wait_ge(av_done, HEADS * (i + 1))
                nc.scalar.activation(orow[:, i, :], bank(2), ACT.Copy)
                if i >= 1:
                    act.wait_ge(o_sq, i)
                nc.scalar.activation(sqs[:, 0:W], bank(2), ACT.Square).then_inc(o_evac, 1)

            for u in range(NB * HEADS):
                for s in range(2):
                    k = 2 * u + s
                    act.wait_ge(max_ready, k + 1)
                    if u >= 2:
                        act.wait_ge(comb_done, u - 1)
                    nc.scalar.activation(prob[:, 2 * (u % 2) + s, :], bank(3 + 2 * (u % 2) + s), ACT.Exp,
                                         bias=negmax[:, k:k + 1], accum_out=rowsum[:, k:k + 1]).then_inc(exp_done, 1)
                if u >= 1:
                    a_out(u - 1)
                evac(12 + u)
                if u >= 4 and u % 4 == 0:
                    o_out(u // 4 - 1)
            a_out(15)
            o_out(3)
            act.wait_ge(rope_done, 8)
            nc.scalar.activation(sig, gg, ACT.Sigmoid).then_inc(sig_g, 1)
            act.wait_ge(ms_o, 1)
            nc.scalar.activation(mso[:, 0, :], mso[:, 0, :], ACT.Sqrt).then_inc(sd_o, 1)
            for i in range(NB):
                act.wait_ge(yv_done, NB * HEADS)
                if i == 0:
                    act.wait_ge(comb_done, NB * HEADS)
                nc.scalar.activation(yrow[:, i, :], bank(2 + i), ACT.Copy)
                if i >= 2:
                    act.wait_ge(y_sq, i - 1)
                nc.scalar.activation(sqs[:, (i % 2) * W:(i % 2 + 1) * W], bank(2 + i), ACT.Square).then_inc(y_evac, 1)
            act.wait_ge(ms_o, 2)
            nc.scalar.activation(mso[:, 1, :], mso[:, 1, :], ACT.Sqrt).then_inc(sd_o, 1)
            act.dma_start(b1_sb, b1t.rearrange("p (e n) -> p e n", e=NE)).then_inc(b_in, 16)
            act.dma_start(b2_sb, b2t.rearrange("p (e n) -> p e n", e=NE)).then_inc(b_in, 16)
            for b in range(NB):
                act.wait_ge(res_ready, 2 * (b + 1))
                nc.scalar.activation(sqs, X[:, b, :], ACT.Square, accum_out=ssx[:, NB + b:NB + b + 1]).then_inc(sq_x, 1)
                act.wait_ge(sq_x, NB + b + 1)
                act.wait_ge(ms_x, NB + b + 1)
                nc.scalar.activation(msx[:, NB + b:NB + b + 1], msx[:, NB + b:NB + b + 1], ACT.Sqrt).then_inc(sd_x, 1)
                act.wait_ge(rs_x, NB + b + 1)
                nc.scalar.activation(h2[:, b, :], X[:, b, :], ACT.Copy, scale=rsx[:, NB + b:NB + b + 1]).then_inc(h2_ready, 1)
            for b in range(NB):
                act.wait_ge(h2_ready, b + 1)
                act.dma_start(h2_v[b], h2[:, b, :]).then_inc(h2_stored, 16)
            act.wait_ge(ev_in, 1)
            nc.scalar.activation(ev, ev, ACT.Exp).then_inc(ev_ready, 1)

            def gate_sigmoid(n, t):
                act.wait_ge(glu_ready, 4 * n + (t + 1))
                nc.scalar.activation(sg[:, t % 2, :], ub[:, t % 2, 0:2 * CAP], ACT.Sigmoid, scale=ALPHA).then_inc(sg_ready, 1)

            def y_high(n):
                act.wait_ge(yT_done, n + 1)
                nc.scalar.activation(yhi[:, :], ps[0:CAP, 6:8, :], ACT.Copy, scale=gate_y[0:CAP, 0:1]
                                     ).then_inc(yhi_ready, 1)

            def c_out(n, q):
                act.wait_ge(ct_done, n + 1)
                nc.scalar.activation(cmat[:, q, :], ps[0:CAP, 7, :], ACT.Copy).then_inc(c_ready, 1)

            def expert(n, q, first=False, last=False):
                gate_sigmoid(n, 0)
                if not first:
                    y_high(n - 1)
                for t in range(1, 4):
                    gate_sigmoid(n, t)
                if not last:
                    c_out(n + 1, 1 - q)

            c_out(0, 0)
            expert(0, 0, first=True)
            with act.Fori(0, NE // 2 - 1) as i:
                expert(2 * i + 1, 1)
                expert(2 * i + 2, 0)
            expert(NE - 1, 1, last=True)
            y_high(NE - 1)

            def over_pass(n, e, at):
                c_out(n, 0)
                for t in range(4):
                    gate_sigmoid(n, t)
                y_high(n)

            further(act, over_pass)

        @block.vector
        def _(v):
            own = [0]

            def link(ins):
                own[0] += 1
                ins.then_inc(dve, 1)
                v.wait_ge(dve, own[0])

            TS, TT, STT = nc.vector.tensor_scalar, nc.vector.tensor_tensor, nc.vector.scalar_tensor_tensor

            def norm_x(b, k):
                v.wait_ge(sq_x, k + 1)
                TS(msx[:, k:k + 1], ssx[:, k:k + 1], 1.0 / D, EPS, ALU.mult, ALU.add).then_inc(ms_x, 1)
                v.wait_ge(sd_x, k + 1)
                nc.vector.reciprocal(rsx[:, k:k + 1], msx[:, k:k + 1]).then_inc(rs_x, 1)

            def norm_T(b):
                v.wait_ge(xT_done, b + 1)
                if b == 0:
                    v.wait_ge(par_in, 16)
                TT(hT[:, :, b * P:(b + 1) * P], wide(2 * b).rearrange("p s (k t) -> p (s k) t", t=P),
                   spread(pcols("n1w"), P), ALU.mult).then_inc(hT_ready, 1)

            for b in range(NB):
                norm_x(b, b)
                if b >= 1:
                    norm_T(b - 1)
            norm_T(NB - 1)

            v.wait_ge(pos_in, 16)
            v.wait_ge(consts, 5)
            link(nc.vector.tensor_copy(ang[:, 0:T], pos_sb[:, 0:T]))
            link(nc.vector.tensor_copy(esum, pos_sb[:, T:T + NB]))
            link(TS(ang[:, 0:T], ang[:, 0:T], pcols("invcol"), None, ALU.mult))
            for b in range(NB):
                link(TS(ang[:, T + b * NF8:T + (b + 1) * NF8], pcols("inv8"), esum[:, b:b + 1], None, ALU.mult))
            for s, shift in enumerate((0.0, 0.25)):
                r = red[:, s, :]
                link(TS(turns, ang, 1.0 / TWO_PI, shift, ALU.mult, ALU.add))
                link(TS(turns, turns, MAGIC, MAGIC, ALU.add, ALU.subtract))
                link(STT(r, turns, -C1, ang, ALU.mult, ALU.add))
                link(STT(r, turns, -C2, r, ALU.mult, ALU.add))
                link(STT(r, turns, -C3, r, ALU.mult, ALU.add))
                if s:
                    link(TS(r, r, float(np.pi / 2), None, ALU.add))
                ins = TS(r, r, PI_LOW, -PI_LOW, ALU.min, ALU.max)
                if s:
                    ins.then_inc(red_ready, 1)
                else:
                    link(ins)
            for h in range(HEADS):
                link(TS(dtmp, dist, 0.0, pcols("ldb")[:, h:h + 1], ALU.min, ALU.mult))
                link(TS(decay[:, h, :], dist, 0.0, pcols("ldf")[:, h:h + 1], ALU.max, ALU.mult))
                ins = TT(decay[:, h, :], decay[:, h, :], dtmp, ALU.subtract)
                if h == HEADS - 1:
                    ins.then_inc(dexp_in, 1)
                else:
                    link(ins)
            lam = pcols("lam").rearrange("p (a b c) -> p a b c", a=2, b=2)
            prod = turns[:, 0:2 * DH].rearrange("p (a c) -> p a c", a=2)
            link(TT(prod, lam[:, :, 0, :], lam[:, :, 1, :], ALU.mult))
            nc.vector.reduce_sum(lamt, prod, AX.X).then_inc(lam_in, 1)
            v.wait_ge(lam_exp, 1)
            link(TT(neglam, lam2[:, 1:2], lam2[:, 0:1], ALU.subtract))
            link(TS(neglam, neglam, LAMBDA_INIT, None, ALU.subtract))
            link(TS(dw, pcols("diffw"), 1.0 - LAMBDA_INIT, None, ALU.mult))

            def qk_sums(g):
                for i in range(NB):
                    j = 4 * g + i
                    v.wait_ge(proj_evac, j + 1)
                    nc.vector.reduce_sum(ssq[:, g, 8 * i:8 * i + 8],
                                         sqs[:, (j % 2) * W:(j % 2 + 1) * W].rearrange("p (a c) -> p a c", a=8),
                                         AX.X).then_inc(sq_used, 1)
                v.wait_ge(sq_used, 4 * g + 4)
                TS(msq[:, g, :], ssq[:, g, :], 1.0 / DH, EPS, ALU.mult, ALU.add).then_inc(ms_q, 1)

            def qk_rest(g):
                r, w = (rq, pcols("qw")) if g == 0 else (rk, pcols("kw"))
                v.wait_ge(sd_q, g + 1)
                link(nc.vector.reciprocal(rsq[:, g, :], msq[:, g, :]))
                for i in range(NB):
                    cell = r[:, i, :].rearrange("p (a c) -> p a c", a=8)
                    link(TT(cell, cell, spread(rsq[:, g, 8 * i:8 * i + 8], DH), ALU.mult))
                    link(TT(cell, cell, w.unsqueeze(1).to_broadcast([P, 8, DH]), ALU.mult))
                cells = r.rearrange("p b (a c) -> p b a c", a=8)
                x1, x2 = cells[:, :, :, 0:NF8], cells[:, :, :, NF8:ROT]
                s, c = (cs_row[:, k, :].rearrange("p (b f) -> p b f", b=NB).unsqueeze(2).to_broadcast([P, NB, 8, NF8])
                        for k in range(2))
                t = [ropet[:, k, :].rearrange("p (b a f) -> p b a f", b=NB, a=8) for k in range(4)]
                if g == 0:
                    v.wait_ge(trig_ready, 1)
                link(TT(t[0], x1, c, ALU.mult))
                link(TT(t[1], x2, s, ALU.mult))
                link(TT(t[2], x2, c, ALU.mult))
                link(TT(t[3], x1, s, ALU.mult))
                link(TT(x1, t[0], t[1], ALU.subtract))
                TT(x2, t[2], t[3], ALU.add).then_inc(qk_ready, 1)
                v.wait_ge(qk_ready, g + 1)

            qk_sums(0)
            qk_sums(1)
            qk_rest(0)
            qk_rest(1)

            def comb(u):
                v.wait_ge(exp_done, 2 * u + 2)
                link(nc.vector.reciprocal(rowinv[:, 2 * u:2 * u + 2], rowsum[:, 2 * u:2 * u + 2]))
                link(TT(lamc[:, u:u + 1], rowinv[:, 2 * u + 1:2 * u + 2], neglam, ALU.mult))
                p1, p2 = prob[:, 2 * (u % 2), :], prob[:, 2 * (u % 2) + 1, :]
                if u >= 2:
                    v.wait_ge(aT_done, u - 1)
                link(TS(amix[:, u % 2, :], p2, lamc[:, u:u + 1], None, ALU.mult))
                STT(amix[:, u % 2, :], p1, rowinv[:, 2 * u:2 * u + 1], amix[:, u % 2, :], ALU.mult, ALU.add
                    ).then_inc(comb_done, 1)

            def rope(r):
                q = r % 2
                dst = (qrT if r < 4 else krT)[:, r % 4, :]
                v.wait_ge(proj_evac, 20 + r + 1)
                if r == 0:
                    v.wait_ge(qkT_done, 8)
                link(TT(roped[:, 0, :], qsb[:, q, :], cosT, ALU.mult))
                v.wait_ge(rot_done, r + 1)
                link(TT(roped[:, 1, :], bank(q), sinT, ALU.mult))
                TT(dst, roped[:, 0, :], roped[:, 1, :], ALU.add).then_inc(rope_done, 1)
                v.wait_ge(rope_done, r + 1)

            def o_sum(i):
                v.wait_ge(o_evac, i + 1)
                nc.vector.reduce_sum(sso[:, 0, 4 * i:4 * i + 4], sqs[:, 0:W].rearrange("p (h c) -> p h c", h=HEADS),
                                     AX.X).then_inc(o_sq, 1)

            for u in range(NB * HEADS):
                for s in range(2):
                    v.wait_ge(sc_done, 2 * u + s + 1)
                    nc.vector.tensor_reduce(negmax[:, 2 * u + s:2 * u + s + 1], bank(3 + 2 * (u % 2) + s), AX.X, ALU.max,
                                            negate=True).then_inc(max_ready, 1)
                if u >= 9:
                    rope(u - 9)
                comb(u)
                if u >= 4 and u % 4 == 0:
                    o_sum(u // 4 - 1)
            rope(7)
            o_sum(3)

            def finish_heads(k, rows, count, size):
                v.wait_ge(o_sq if k == 0 else y_sq, NB)
                TS(mso[:, k, :], sso[:, k, :], 1.0 / DV, EPS, ALU.mult, ALU.add).then_inc(ms_o, 1)
                v.wait_ge(sd_o, k + 1)
                link(nc.vector.reciprocal(rso[:, k, :], mso[:, k, :]))
                flat = rows.rearrange("p b (h c) -> p (b h) c", h=HEADS)
                return TT(flat, flat, spread(rso[:, k, :], DV), ALU.mult)

            finish_heads(0, orow, 16, DV).then_inc(o_ready, 1)

            v.wait_ge(dexp_ready, 1)
            for q in range(NB * HEADS):
                h, m = divmod(q, NB)
                v.wait_ge(st_done, q + 1)
                if q >= 2:
                    v.wait_ge(yv_done, q - 1)
                a = (T - P) - P * m
                TT(std[:, q % 2, :], bank((0, 1, 6, 7)[q % 4]), decay[:, h, a:a + T], ALU.mult).then_inc(std_ready, 1)
            v.wait_ge(sig_g, 1)
            gflat = gg.rearrange("p b c -> p (b c)")
            link(TT(gflat, gflat, sig, ALU.mult))
            for i in range(NB):
                v.wait_ge(y_evac, i + 1)
                nc.vector.reduce_sum(sso[:, 1, 4 * i:4 * i + 4],
                                     sqs[:, (i % 2) * W:(i % 2 + 1) * W].rearrange("p (h c) -> p h c", h=HEADS),
                                     AX.X).then_inc(y_sq, 1)
            link(finish_heads(1, yrow, 16, DV))
            TT(yrow, yrow, gg, ALU.mult).then_inc(o_ready, 1)
            for k, half in enumerate((1, 0)):
                for i in range(NB):
                    t = 4 * k + i
                    v.wait_ge(mixT_done, t + 1)
                    src = bank(6 + t % 2).rearrange("p (h t) -> p h t", h=HEADS)
                    dst = mixT[:, 4 * half:4 * half + 4, i * P:(i + 1) * P]
                    if half:
                        TS(dst, src, dw, None, ALU.mult).then_inc(mixT_ready, 1)
                    else:
                        TT(dst, src, spread(pcols("retw"), P), ALU.mult).then_inc(mixT_ready, 1)

            def h2_T(b):
                v.wait_ge(h2T_done, b + 1)
                if b >= 2:
                    v.wait_ge(lg_done, b - 1)
                TT(h2T[:, b % 2, :].rearrange("p (k t) -> p k t", k=KD),
                   wide(4 + 2 * (b % 2)).rearrange("p s (k t) -> p (s k) t", t=P),
                   spread(pcols("n2w"), P), ALU.mult).then_inc(h2T_ready, 1)

            def choose(b):
                v.wait_ge(lg_done, b + 1)
                TT(logits[:, b, :], bank(b, 0, NE), pcols("brt"), ALU.add).then_inc(lg_ready, 1)
                v.wait_ge(lg_ready, b + 1)
                link(nc.vector.max(top8[:, b, :], logits[:, b, :]))
                link(nc.vector.max_index(idx8[:, b, :], top8[:, b, :], logits[:, b, :]))

            for b in range(NB):
                for s in range(2):
                    w = 2 * b + s
                    v.wait_ge(op_done, w + 1)
                    cell = X[:, b, s * W:(s + 1) * W]
                    TT(cell, bank(w % 4), cell, ALU.add).then_inc(res_ready, 1)
                norm_x(b, NB + b)
                if b >= 1:
                    h2_T(b - 1)
            h2_T(NB - 1)
            for b in range(NB):
                choose(b)
            link(TT(ev, top8[:, :, 0:TOPK], top8[:, :, 0:1].to_broadcast([P, NB, TOPK]), ALU.subtract))
            nc.vector.tensor_copy(topf, idx8[:, :, :]).then_inc(ev_in, 1)
            v.wait_ge(ev_in, 1)
            iota_e = iota_s[:, 0:NE].unsqueeze(1).to_broadcast([P, NB, NE])
            for k in range(TOPK):
                at = topf[:, :, k:k + 1].to_broadcast([P, NB, NE])
                if k == 0:
                    link(TT(mask, iota_e, at, ALU.is_equal))
                else:
                    link(TT(eq, iota_e, at, ALU.is_equal))
                    ins = TT(mask, mask, eq, ALU.add)
                    if k == TOPK - 1:
                        ins.then_inc(mask_ready, 1)
                    else:
                        link(ins)
            v.wait_ge(ev_ready, 1)
            link(nc.vector.reduce_sum(esum, ev, AX.X))
            link(nc.vector.reciprocal(esum, esum))
            link(TT(gate4, ev, spread(esum, TOPK), ALU.mult))
            for k in range(TOPK):
                at = topf[:, :, k:k + 1].to_broadcast([P, NB, NE])
                link(TT(eq, iota_e, at, ALU.is_equal))
                if k == 0:
                    link(TT(gts, eq, gate4[:, :, k:k + 1].to_broadcast([P, NB, NE]), ALU.mult))
                else:
                    link(TT(eq, eq, gate4[:, :, k:k + 1].to_broadcast([P, NB, NE]), ALU.mult))
                    link(TT(gts, gts, eq, ALU.add))
            link(nc.vector.tensor_copy(idgate[:, :, :, 1], gts.rearrange("p b e -> p e b")))
            v.wait_ge(rank_done, 1)
            v.wait_ge(consts, 6)
            link(TS(eq, bank(1, 0, NB * NE).rearrange("p (b e) -> p b e", b=NB), 1.0, None, ALU.add))
            link(TT(eq, eq, mask, ALU.mult))
            for c in range(MAX_CHUNK):
                ins = TS(posm[:, c, :, :], eq.rearrange("p b e -> p e b"), -1.0 - CAP * c, None, ALU.add)
                if c == MAX_CHUNK - 1:
                    ins.then_inc(pos_ready, 1)
                else:
                    link(ins)
            v.wait_ge(pos_ready, 1)

            def hot(n, at):
                TT(onehot, iota_s[:, 0:CAP].unsqueeze(1).to_broadcast([P, NB, CAP]),
                   spread(posm.rearrange("p c e b -> p (c e) b")[:, bass.ds(at, 1), :].rearrange("p a b -> p (a b)"), CAP), ALU.is_equal
                   ).then_inc(hot_ready, 1)

            def places(n, q):
                v.wait_ge(idx_done, n + 1)
                nc.vector.tensor_copy(place_idx[0:CAP, q:q + 1], ps[0:CAP, 5, 480:481])
                nc.vector.tensor_copy(gate_s[0:CAP, q:q + 1], ps[0:CAP, 5, 481:482]).then_inc(idx_ready, 1)

            def columns(n, q):
                v.wait_ge(hrT_done, n + 1)
                TT(htE[:, q, :].rearrange("p (k t) -> p k t", k=KD),
                   ps[:, 4:6, 0:4 * CAP].rearrange("p s (k t) -> p s k t", t=CAP),
                   spread(pcols("n2w").rearrange("p (s k) -> p s k", s=2), CAP), ALU.mult).then_inc(htE_ready, 1)

            def swiglu(n, e, t, first=False):
                v.wait_ge(up_done, 4 * n + (t + 1))
                if t >= 2 or not first:
                    v.wait_ge(act_ready, 4 * n + (t - 1))
                TT(ub[:, t % 2, :].rearrange("p (m t) -> p m t", t=CAP), ps[:, t, 0:4 * CAP].rearrange("p (m t) -> p m t", t=CAP),
                   spread(b1_sb[:, bass.ds(e, 1), 4 * t:4 * t + 4].rearrange("p a m -> p (a m)"), CAP), ALU.add
                   ).then_inc(ub_ready, 1)
                glu, lin = ub[:, t % 2, 0:2 * CAP], ub[:, t % 2, 2 * CAP:4 * CAP]
                v.wait_ge(ub_ready, 4 * n + (t + 1))
                TS(glu, glu, LIMIT, None, ALU.min).then_inc(glu_ready, 1)
                TS(lin, lin, LIMIT, -LIMIT, ALU.min, ALU.max).then_inc(lin_ready, 1)
                v.wait_ge(lin_ready, 4 * n + (t + 1))
                STT(lin, lin, 1.0, glu, ALU.add, ALU.mult).then_inc(gl_ready, 1)
                v.wait_ge(gl_ready, 4 * n + (t + 1))
                v.wait_ge(sg_ready, 4 * n + (t + 1))
                TT(actT[:, 2 * t:2 * t + 2, :], lin.rearrange("p (m t) -> p m t", t=CAP),
                   sg[:, t % 2, :].rearrange("p (m t) -> p m t", t=CAP), ALU.mult).then_inc(act_ready, 1)

            def y_bias(n, e):
                for s in range(2):
                    v.wait_ge(down_done, 2 * n + (s + 1))
                    TT(ybT[:, 4 * s:4 * s + 4, :], ps[:, 4 + s, 0:4 * CAP].rearrange("p (m t) -> p m t", t=CAP),
                       spread(b2_sb[:, bass.ds(e, 1), 4 * s:4 * s + 4].rearrange("p a m -> p (a m)"), CAP), ALU.add
                       ).then_inc(yb_ready, 1)

            def y_gate(n, q):
                nc.vector.tensor_copy(gate_y[0:CAP, 0:1], gate_s[0:CAP, q:q + 1]).then_inc(gate_ready, 1)

            def y_low(n):
                v.wait_ge(yhi_ready, n + 1)
                STT(ylo[:, :].rearrange("p (s c) -> p s c", s=2), ps[0:CAP, 6:8, :], gate_y[0:CAP, 0:1],
                    yhi[:, :].bitcast(f32).rearrange("p (s c) -> p s c", s=2), ALU.mult, ALU.subtract
                    ).then_inc(y_ready, 1)

            def add_sum(n, i):
                v.wait_ge(cmb_done, 8 * n + (i + 1))
                b, s = divmod(i, 2)
                cell = X[:, b, s * W:(s + 1) * W]
                TT(cell, bank(6 + i % 2), cell, ALU.add).then_inc(cmb_added, 1)

            def expert(n, q, first=False, last=False):
                if not last:
                    v.wait_ge(ct_done, n + 1)
                    hot(n + 1, n + 1)
                swiglu(n, n, 0, first)
                if not last:
                    places(n + 1, 1 - q)
                if not first:
                    y_low(n - 1)
                swiglu(n, n, 1, first)
                if not first:
                    for i in range(3):
                        add_sum(n - 1, i)
                swiglu(n, n, 2, first)
                if not first:
                    for i in range(3, 6):
                        add_sum(n - 1, i)
                if not last:
                    columns(n + 1, 1 - q)
                if not first:
                    add_sum(n - 1, 6)
                swiglu(n, n, 3, first)
                if not first:
                    add_sum(n - 1, 7)
                y_gate(n, q)
                y_bias(n, n)

            v.wait_ge(b_in, 32)
            hot(0, 0)
            places(0, 0)
            for c in range(1, MAX_CHUNK):
                key = over_key[:, c - 1, :]
                link(TS(key, iota_s[:, 0:NE], 1.0 + NE * c, None, ALU.add))
                link(STT(key, bank(1, NB * NE, NE), float(CAP * c), key, ALU.is_gt, ALU.mult))
            keys = over_key.rearrange("p c e -> p (c e)")
            for i in range(MAX_OVER // 8):
                top = over_top[:, 8 * i:8 * i + 8]
                link(nc.vector.max(top, keys))
                if i < MAX_OVER // 8 - 1:
                    link(nc.vector.match_replace(out=keys, in_to_replace=top, in_values=keys, imm_value=0.0))
            link(TS(over_some, over_top, 0.0, None, ALU.is_gt))
            link(nc.vector.reduce_sum(over_n, over_some, AX.X))
            link(nc.vector.tensor_copy(over_at[:, MAX_OVER:MAX_OVER + 1], over_n))
            link(TS(over_at[:, 0:MAX_OVER], over_top, -1.0, None, ALU.add))
            TS(over_e[:, :], over_at[:, 0:MAX_OVER], NE - 1, None, ALU.bitwise_and).then_inc(over_ready, 1)
            columns(0, 0)
            expert(0, 0, first=True)
            with v.Fori(0, NE // 2 - 1) as i:
                expert(2 * i + 1, 1)
                expert(2 * i + 2, 0)
            expert(NE - 1, 1, last=True)
            y_low(NE - 1)
            for i in range(2 * NB):
                add_sum(NE - 1, i)

            def over_pass(n, e, at):
                v.wait_ge(ct_done, n)
                hot(n, at)
                places(n, 0)
                columns(n, 0)
                for t in range(4):
                    swiglu(n, e, t)
                y_gate(n, 0)
                y_bias(n, e)
                y_low(n)
                for i in range(2 * NB):
                    add_sum(n, i)

            further(v, over_pass)

        @block.tensor
        def _(pe):
            MM, TR = nc.tensor.matmul, nc.tensor.transpose
            pe.wait_ge(consts, 5)
            for b in range(NB):
                pe.wait_ge(xs_ready, b + 1)
                for k in range(KD):
                    t = TR(bank(2 * b + k // 4, (k % 4) * P, P), xs[:, b % 2, k * P:(k + 1) * P], ident[:, :])
                t.then_inc(xT_done, 1)

            def project(j):
                g, i = divmod(j, 4)
                if g == 0:
                    pe.wait_ge(hT_ready, i + 1)
                if i == 0:
                    pe.wait_ge(ring_in[2 * (g % 3)], 16 * (g // 3 + 1))
                if j >= 2:
                    pe.wait_ge(proj_evac, j - 1)
                if j >= 22:
                    pe.wait_ge(rope_done, j - 21)
                wt = pair(2 * (g % 3))
                for k in range(KD):
                    if g < 5:
                        lhs, rhs = hT[:, k, i * P:(i + 1) * P], wt[:, k, :]
                    else:
                        lhs, rhs = wt[:, k, i * P:(i + 1) * P], hT[:, k, :]
                    m = MM(bank(j % 2), lhs, rhs, start=k == 0, stop=k == KD - 1)
                m.then_inc(proj_done, 1)

            def rotate(r):
                pe.wait_ge(proj_evac, 20 + r + 1)
                MM(bank(r % 2), swap[:, :], qsb[:, r % 2, :], start=True, stop=True).then_inc(rot_done, 1)

            for j in range(12):
                project(j)
            pe.wait_ge(hT_ready, NB)
            for g, r in enumerate((rq, rk)):
                pe.wait_ge(qk_ready, g + 1)
                for i in range(NB):
                    if g == 1:
                        pe.wait_ge(qkT_evac, i + 1)
                    for h in range(HEADS):
                        t = TR(bank(3 + i, h * P, P), r[:, i, h * P:(h + 1) * P], ident[:, :])
                    t.then_inc(qkT_done, 1)

            def scores(u):
                i, h = divmod(u, HEADS)
                if u == 0:
                    pe.wait_ge(qkT_evac, 8)
                if u >= 2:
                    pe.wait_ge(exp_done, 2 * u - 2)
                for s in range(2):
                    MM(bank(3 + 2 * (u % 2) + s), qdT[s * DH:(s + 1) * DH, h, i * P:(i + 1) * P],
                       kdT[s * DH:(s + 1) * DH, h, :], start=True, stop=True).then_inc(sc_done, 1)

            def turn(u):
                pe.wait_ge(comb_done, u + 1)
                if u >= 1:
                    pe.wait_ge(aT_evac, u)
                for k in range(NB):
                    t = TR(bank(7, k * P, P), amix[:, u % 2, k * P:(k + 1) * P], ident[:, :])
                t.then_inc(aT_done, 1)

            def values(u):
                i, h = divmod(u, HEADS)
                pe.wait_ge(aT_evac, u + 1)
                if h == 0 and i >= 1:
                    pe.wait_ge(o_evac, i)
                for k in range(NB):
                    m = MM(bank(2, h * DV, DV), aT[:, u % 2, k * P:(k + 1) * P], vd[:, k, h * DV:(h + 1) * DV],
                           start=k == 0, stop=k == NB - 1)
                m.then_inc(av_done, 1)

            for u in range(NB * HEADS):
                scores(u)
                if u >= 1:
                    turn(u - 1)
                project(12 + u)
                if u >= 1:
                    values(u - 1)
                if u >= 9:
                    rotate(u - 9)
            turn(15)
            values(15)
            rotate(7)

            def ret_scores(q):
                h, m = divmod(q, NB)
                if q == 0:
                    pe.wait_ge(rope_done, 8)
                    pe.wait_ge(exp_done, 32)
                    pe.wait_ge(aT_evac, 16)
                if q >= 4:
                    pe.wait_ge(std_ready, q - 3)
                MM(bank((0, 1, 6, 7)[q % 4]), krT[:, h, m * P:(m + 1) * P], qrT[:, h, :], start=True, stop=True
                   ).then_inc(st_done, 1)

            def ret_values(q):
                h, m = divmod(q, NB)
                if q == 0:
                    pe.wait_ge(o_evac, NB)
                pe.wait_ge(std_ready, q + 1)
                for i in range(NB):
                    t = MM(bank(2 + i, h * DV, DV), std[:, q % 2, i * P:(i + 1) * P], vr[:, m, h * DV:(h + 1) * DV],
                           start=m == 0, stop=m == NB - 1)
                t.then_inc(yv_done, 1)

            ret_scores(0)
            ret_scores(1)
            for q in range(NB * HEADS):
                if q + 2 < NB * HEADS:
                    ret_scores(q + 2)
                ret_values(q)

            for k, rows in enumerate((orow, yrow)):
                pe.wait_ge(o_ready, k + 1)
                for i in range(NB):
                    t = 4 * k + i
                    if t == 0:
                        pe.wait_ge(std_ready, NB * HEADS)
                    if t >= 2:
                        pe.wait_ge(mixT_ready, t - 1)
                    for h in range(HEADS):
                        m = TR(bank(6 + t % 2, h * P, P), rows[:, i, h * P:(h + 1) * P], ident[:, :])
                    m.then_inc(mixT_done, 1)

            def out_project(b):
                for s in range(2):
                    w = 2 * b + s
                    if b == 0:
                        pe.wait_ge(ring_in[2 + 2 * s], 16 * 3)
                        pe.wait_ge(y_evac, NB)
                    pe.wait_ge(mixT_ready, NB + b + 1)
                    if w >= 4:
                        pe.wait_ge(res_ready, w - 3)
                    for k in range(KD):
                        m = MM(bank(w % 4), mixT[:, k, b * P:(b + 1) * P], pair(2 + 2 * s)[:, k, :],
                               start=k == 0, stop=k == KD - 1)
                    m.then_inc(op_done, 1)

            def h2_turn(b):
                pe.wait_ge(h2_ready, b + 1)
                if b == 0:
                    pe.wait_ge(mixT_ready, 8)
                if b >= 2:
                    pe.wait_ge(h2T_ready, b - 1)
                for k in range(KD):
                    m = TR(bank(4 + 2 * (b % 2) + k // 4, (k % 4) * P, P), h2[:, b, k * P:(k + 1) * P], ident[:, :])
                m.then_inc(h2T_done, 1)

            def route(b):
                pe.wait_ge(h2T_ready, b + 1)
                if b == 0:
                    pe.wait_ge(wr_in, 16)
                pe.wait_ge(res_ready, 2 * NB)
                for k in range(KD):
                    m = MM(bank(b, 0, NE), h2T[:, b % 2, k * P:(k + 1) * P], wr_sb[:, k, :],
                           start=k == 0, stop=k == KD - 1)
                m.then_inc(lg_done, 1)

            for b in range(NB):
                out_project(b)
                if b >= 1:
                    h2_turn(b - 1)
            h2_turn(NB - 1) if NB == 1 else None
            route(0)
            route(1)
            h2_turn(NB - 1)
            route(2)
            route(3)
            pe.wait_ge(lg_ready, NB)
            pe.wait_ge(mask_ready, 1)
            for b in range(NB):
                for c in range(b + 1):
                    m = MM(bank(1, b * NE, NE), (before if c == b else ones)[:, :], mask[:, c, :],
                           start=c == 0, stop=c == b)
            for c in range(NB):
                m = MM(bank(1, NB * NE, NE), ones[:, :], mask[:, c, :], start=c == 0, stop=c == NB - 1)
            m.then_inc(rank_done, 1)

            def index(n, e, q):
                pe.wait_ge(hot_ready, n + 1)
                for b in range(NB):
                    m = MM(ps[0:CAP, 5, 480:482], onehot[:, b, :],
                           idgate[:, bass.ds(e, 1), b, :].rearrange("p a c -> p (a c)"), start=b == 0, stop=b == NB - 1)
                m.then_inc(idx_done, 1)

            def turn_rows(n, q, k_th):
                pe.wait_ge(row_in[q], k_th)
                for k in range(KD):
                    m = TR(bank(4 + k // 4, (k % 4) * CAP, CAP), hrow[:, q, k * P:(k + 1) * P], ident[0:CAP, 0:CAP])
                m.then_inc(hrT_done, 1)

            def turn_hot(n):
                for b in range(NB):
                    m = TR(ps[0:CAP, 7, b * P:(b + 1) * P], onehot[:, b, :], ident[:, :])
                m.then_inc(ct_done, 1)

            def weights(n, c):
                s = ORDER[c]
                pe.wait_ge(ring_in[2 * s], 16 * n + 16 * (FRONT_LOADS[s] + 1))

            def up(n, q, r):
                t, j = divmod(r, 4)
                c = 2 * (t // 2) + j // 2
                if r % 8 == 0:
                    weights(n, c)
                    if r == 0:
                        pe.wait_ge(htE_ready, n + 1)
                if r % 8 == 2:
                    weights(n, c)
                col = (2 * (t % 2) + j % 2) * P
                for k in range(KD):
                    m = MM(bank(t, j * CAP, CAP), pair(2 * ORDER[c])[:, k, col:col + P],
                           htE[:, q, k * CAP:(k + 1) * CAP], start=k == 0, stop=k == KD - 1)
                if j == 3:
                    m.then_inc(up_done, 1)
                elif r % 8 == 5:
                    m.then_inc(chunk_used, 1)

            def spread_sum(n, q, i):
                b, s = divmod(i, 2)
                if i == 0:
                    pe.wait_ge(y_ready, n + 1)
                    pe.wait_ge(c_ready, n + 1)
                if i >= 2:
                    pe.wait_ge(cmb_added, 8 * n + (i - 1))
                for part in (yhi, ylo):
                    m = MM(bank(6 + i % 2), cmat[:, q, b * P:(b + 1) * P], part[:, s * W:(s + 1) * W],
                           start=part is yhi, stop=part is ylo)
                m.then_inc(cmb_done, 1)

            def down(n):
                for s in range(2):
                    weights(n, 4 + s)
                    for j in range(4):
                        for k in range(KD):
                            if s == 0 and j == 0 and k % 2 == 0:
                                pe.wait_ge(act_ready, 4 * n + (k // 2 + 1))
                            m = MM(bank(4 + s, j * CAP, CAP), pair(2 * ORDER[4 + s])[:, k, j * P:(j + 1) * P],
                                   actT[:, k, :], start=k == 0, stop=k == KD - 1)
                    m.then_inc(down_done, 1)

            def turn_y(n):
                pe.wait_ge(yb_ready, 2 * n + 2)
                for k in range(KD):
                    m = TR(ps[0:CAP, 6 + k // 4, (k % 4) * P:(k % 4 + 1) * P], ybT[:, k, :], ident[:, :])
                m.then_inc(yT_done, 1)

            def expert(n, q, rows_next, first=False, last=False):
                for r in range(4):
                    up(n, q, r)
                if not last:
                    index(n + 1, n + 1, 1 - q)
                if not first:
                    pe.wait_ge(c_ready, n + 1)
                    turn_y(n - 1)
                for r in range(4, 8):
                    up(n, q, r)
                for r in range(8, 16):
                    up(n, q, r)
                    if not first:
                        spread_sum(n - 1, 1 - q, r - 8)
                    if r == 13 and not last:
                        turn_rows(n + 1, 1 - q, rows_next)
                if not last:
                    if not first:
                        pe.wait_ge(cmb_added, 8 * n)
                    turn_hot(n + 1)
                    pe.wait_ge(htE_ready, n + 2)
                down(n)

            index(0, 0, 0)
            turn_rows(0, 0, 16)
            turn_hot(0)
            pe.wait_ge(c_ready, 1)
            expert(0, 0, 16, first=True)
            with pe.Fori(0, NE // 2 - 1) as i:
                expert(2 * i + 1, 1, 16 * i + 32)
                expert(2 * i + 2, 0, 16 * i + 32)
            expert(NE - 1, 1, None, last=True)
            pe.wait_ge(cmb_added, 8 * (NE - 1))
            turn_y(NE - 1)
            for i in range(2 * NB):
                spread_sum(NE - 1, 1, i)

            def over_pass(n, e, at):
                index(n, e, 0)
                turn_rows(n, 0, 16 * n + (16 - 16 * (NE // 2)))
                pe.wait_ge(cmb_added, 8 * n)
                turn_hot(n)
                for r in range(16):
                    up(n, 0, r)
                down(n)
                pe.wait_ge(c_ready, n + 1)
                turn_y(n)
                for i in range(2 * NB):
                    spread_sum(n, 0, i)

            further(pe, over_pass)


def kernel(x, positions, norm1_w, w_in, ret_log_decay_fwd, ret_log_decay_bwd, ret_norm_w,
           q_norm_w, k_norm_w, lambda_q1, lambda_k1, lambda_q2, lambda_k2, diff_norm_w,
           w_out, norm2_w, w_router, b_router, w1, b1, w2, b2):
    import concourse.bacc as bacc
    from concourse.bass_utils import run_bass_kernel_spmd as run

    def rows(a):
        return np.broadcast_to(np.asarray(a).reshape(1, -1), (P, np.asarray(a).size))

    ramp = np.arange(64, dtype=np.float32) * np.float32(1 / 63)
    inv_ret = (10000.0 ** (-ramp.astype(np.float64))).astype(np.float32)
    inv_diff = (500000.0 ** (-np.arange(0, ROT, 2) / ROT)).astype(np.float32)
    par = np.concatenate([
        np.asarray(norm1_w).reshape(KD, P).T, np.asarray(norm2_w).reshape(KD, P).T,
        np.asarray(ret_norm_w).reshape(HEADS, P).T, np.asarray(diff_norm_w).reshape(1, P).T,
        np.concatenate([inv_ret, inv_ret]).reshape(P, 1), rows(inv_diff),
        rows(ret_log_decay_fwd), rows(ret_log_decay_bwd), rows(q_norm_w), rows(k_norm_w),
        rows(lambda_q1), rows(lambda_k1), rows(lambda_q2), rows(lambda_k2), rows(b_router)], axis=1)
    pos = np.concatenate([rows(positions), np.asarray(positions).reshape(NB, P).T], axis=1)
    b1t = np.asarray(b1).reshape(NE, 2, 4, 2, P).transpose(4, 0, 2, 1, 3).reshape(P, NE * 16)
    b2t = np.asarray(b2).reshape(NE, KD, P).transpose(2, 0, 1).reshape(P, NE * KD)
    arrays = {"x": x, "w_in": w_in, "w_out": w_out, "w_router": w_router, "w1": w1, "w2": w2, "b1t": b1t, "b2t": b2t,
              "par": par, "pos": pos}
    arrays = {n: np.ascontiguousarray(a) for n, a in arrays.items()}
    nc = bacc.Bacc("TRN2", target_bir_lowering=False, num_devices=1, dynamic_dma_scratch_size=4096)
    aps = {n: nc.dram_tensor(f"in_{n}", a.shape, mybir.dt.from_np(a.dtype), kind="ExternalInput").ap()
           for n, a in arrays.items()}
    out = nc.dram_tensor("out", (1, T, D), mybir.dt.float32, kind="ExternalOutput").ap()
    h2_rows = nc.dram_tensor("h2_rows", (T, D), mybir.dt.float32, kind="Internal").ap()
    build_layer(nc, out=out, h2_rows=h2_rows, **aps)
    r = run(nc, [{f"in_{n}": a for n, a in arrays.items()}], core_ids=[0])
    return r.results[0]["out"]
```

```python
from contextlib import ExitStack

import concourse.bass as bass
from concourse import mybir
import numpy as np

P = 128
D = 1024
T = 512
NB = T // P
KD = D // P
HEADS = 4
DV = 128
DH = 64
ROT = DH // 4
NF8 = ROT // 2
NE = 32
TOPK = 4
W = 512
EPS = 1e-6
LIMIT = 7.0
ALPHA = 1.702
LAMBDA_INIT = 0.2
RING = 12
SLOT = 2048
CAP = 96
MAX_CHUNK = -(-T // CAP)
ASSIGNED = T * TOPK
MAX_OVER = 24
CHUNKS = 6
W1_COLS = [0, D, W, D + W]
ORDER = [0, 3, 5, 4, 1, 2]
FRONT_LOADS = [3, 3, 3, 0, 0, 0]
SLICES = 4
DIST = 896

PK = {}
_at = 0
for _n, _w in (("n1w", KD), ("n2w", KD), ("retw", HEADS), ("diffw", 1), ("invcol", 1), ("inv8", NF8), ("ldf", HEADS),
               ("ldb", HEADS), ("qw", DH), ("kw", DH), ("lam", 4 * DH), ("brt", NE)):
    PK[_n] = (_at, _at + _w)
    _at += _w
NPAR = _at

GROUPS = [("Qd", 2048), ("Kd", 2560), ("Vd", 3072), ("Vr", 1024), ("G", 1536), ("Qr", 0), ("Kr", 512)]

TWO_PI = 2 * np.pi
C1 = 6.28125
C2 = float(np.float32(np.round((TWO_PI - C1) * 2**17) / 2**17))
C3 = float(np.float32(TWO_PI - C1 - C2))
MAGIC = 1.5 * 2.0**23
PI_LOW = 3.1415925


def build_layer(nc, x, w_in, w_out, w_router, w1, b1t, w2, b2, par, pos, h2_rows, y_rows, out):
    f32, i32, u32 = mybir.dt.float32, mybir.dt.int32, mybir.dt.uint32
    f32r = mybir.dt.float32r
    ALU, ACT, AX = mybir.AluOpType, mybir.ActivationFunctionType, mybir.AxisListType

    ctx = ExitStack()
    with ctx:
        def sb(name, shape, dt=f32):
            return ctx.enter_context(nc.sbuf_tensor(name, shape, dt))

        def sem(name):
            return ctx.enter_context(nc.semaphore(name))

        ring = sb("ring", [P, RING, SLOT])
        X = sb("X", [P, NB, D])
        HT = sb("HT", [P, KD * T])
        hT = HT[:, :].rearrange("p (k t) -> p k t", k=KD)
        h2 = HT[:, :].rearrange("p (b d) -> p b d", b=NB)
        par_sb = sb("par_sb", [P, NPAR])
        ident = sb("ident", [P, P])
        before = sb("before", [P, P])
        ones = sb("ones", [P, P])
        swap = sb("swap", [P, P])
        iota_s = sb("iota_s", [P, P])
        small = sb("small", [P, 592])
        small_used = [0]

        def tiny(*shape):
            n = int(np.prod(shape))
            a = small[:, small_used[0]:small_used[0] + n]
            small_used[0] += n
            if len(shape) == 2:
                a = a.rearrange("p (a b) -> p a b", a=shape[0])
            if len(shape) == 3:
                a = a.rearrange("p (a b c) -> p a b c", a=shape[0], b=shape[1])
            return a

        ssx, msx, rsx = tiny(2 * NB), tiny(2 * NB), tiny(2 * NB)
        ssq, msq, rsq = tiny(2, 32), tiny(2, 32), tiny(2, 32)
        negmax, rowsum, rowinv, lamc = tiny(32), tiny(32), tiny(32), tiny(16)
        sso, mso, rso = tiny(2, 16), tiny(2, 16), tiny(2, 16)
        lamt, lam2, neglam, dw = tiny(2), tiny(2), tiny(1), tiny(1)
        top8, topf, ev, gate4, esum = tiny(NB, 8), tiny(NB, 8), tiny(NB, TOPK), tiny(NB, TOPK), tiny(NB)
        idx8 = sb("idx8", [P, NB, 8], u32)
        token_row = tiny(NB)
        place_id, vacant = tiny(1), tiny(1)
        over_top = tiny(MAX_OVER)
        over_n = tiny(1)
        over_some = tiny(MAX_OVER)
        over_at = sb("over_at", [P, MAX_OVER + 1], i32)
        over_e = sb("over_e", [P, MAX_OVER], i32)
        place_idx, place_row = sb("place_idx", [P, 2], u32), sb("place_row", [P, 2], u32)

        arena = sb("arena", [P, 15872])

        def cut(at, n, *split):
            a = arena[:, at:at + n]
            if len(split) == 2:
                return a.rearrange("p (a b) -> p a b", a=split[0])
            if len(split) == 3:
                return a.rearrange("p (a b c) -> p a b c", a=split[0], b=split[1])
            return a

        def slots(s, n, parts):
            return ring[:, s:s + n, :].rearrange("p s c -> p (s c)").rearrange("p (a b) -> p a b", a=parts)

        NANG = T + NB * NF8
        rq, rk = cut(0, 2048, NB, W), cut(2048, 2048, NB, W)
        qrT, krT = cut(0, 2048, HEADS, T), cut(2048, 2048, HEADS, T)
        decay = cut(4096, HEADS * DIST, HEADS, DIST)
        h2T = cut(4096, 2048, 2, D)
        cosT, sinT = cut(7680, W), cut(8192, W)
        xs = cut(8704, 2048, 2, D)
        prob = cut(8704, 2048, 4, W)
        yrow = cut(8704, 2048, NB, W)
        ang, turns, red = cut(10752, NANG), cut(10752 + NANG, NANG), cut(10752 + 2 * NANG, 2 * NANG, 2, NANG)
        dist = cut(10752 + 4 * NANG, DIST)
        dtmp = cut(10752 + 4 * NANG + DIST, DIST)
        pos_sb = cut(4096, T + NB).bitcast(i32)
        ropet = cut(10752, 1024, 4, NB * 8 * NF8)
        amix = cut(10752, 1024, 2, W)
        std = cut(10752, 1024, 2, W)
        aT = cut(11776, 1024, 2, W)
        qsb = cut(12800, 1024, 2, W)
        roped = cut(13824, 1024, 2, W)
        sig = cut(12800, 2048)
        sqs = cut(14848, 1024)
        cs_row = sb("cs_row", [P, 2, NB * NF8])
        orow = slots(6, 1, NB)
        qdT = slots(7, 1, HEADS)
        kdT = slots(8, 1, HEADS)
        vd = slots(9, 1, NB)
        mixT = slots(8, 2, KD)
        vr = slots(10, 1, NB)
        gg = slots(11, 1, NB)
        posm = cut(0, MAX_CHUNK * NE * NB, MAX_CHUNK, NE, NB)
        b1_sb = cut(768, NE * 16, NE, 16)
        gatesT = arena[0:NE, 1280:1280 + T]
        logits, mask = cut(1792, NB * NE, NB, NE), cut(1920, NB * NE, NB, NE)
        eq, gts = cut(2048, NB * NE, NB, NE), cut(2176, NB * NE, NB, NE)
        over_key = cut(2304, (MAX_CHUNK - 1) * NE, MAX_CHUNK - 1, NE)
        ub, sg = cut(2304, 8 * CAP, 2, 4 * CAP), cut(3072, 4 * CAP, 2, 2 * CAP)
        actT = cut(3456, KD * CAP, KD, CAP)
        b2_sb = arena[0:NE, 6144:6144 + D]
        wr_sb = cut(7168, KD * NE, KD, NE)
        htE = cut(7168, 2 * KD * CAP, 2, KD * CAP)
        onehot = cut(8704, NB * CAP, NB, CAP)
        tokens = cut(10112, NE * NB * 2, NE, NB, 2)
        choice = cut(2304, NB * NE, NB, NE)
        yrows = arena[0:CAP, 9088:9088 + D]
        hrow = HT[0:CAP, 0:2 * D].rearrange("p (q d) -> p q d", q=2)
        act_hi, act_lo = sb("act_hi", [P, KD, CAP], f32r), sb("act_lo", [P, KD, CAP], f32r)
        w_hi, w_lo = sb("w_hi", [P, SLICES, W], f32r), sb("w_lo", [P, SLICES, W], f32r)
        chosen = ring.rearrange("p s c -> p (s c)")[:, 0:NB * TOPK * D].rearrange("p (b k d) -> p b k d", b=NB, k=TOPK)

        ps = ctx.enter_context(nc.psum_tensor("ps", [P, 8, W], f32))

        x_in = [sem(f"x_in{b}") for b in range(NB)]
        par_in, pos_in, wr_in, b1_in, b2_in = sem("par_in"), sem("pos_in"), sem("wr_in"), sem("b1_in"), sem("b2_in")
        ring_in = [sem(f"ring_in{s}") for s in range(RING)]
        consts, consts0 = sem("consts"), sem("consts0")
        dve, act_own = sem("dve_chain"), sem("act_chain")
        sq_x, ms_x, sd_x, rs_x, xs_ready, xT_done, hT_ready = (sem(n) for n in (
            "sq_x", "ms_x", "sd_x", "rs_x", "xs_ready", "xT_done", "hT_ready"))
        red_ready, trig_ready, dexp_in, dexp_ready, lam_in, lam_exp = (sem(n) for n in (
            "red_ready", "trig_ready", "dexp_in", "dexp_ready", "lam_in", "lam_exp"))
        proj_done, proj_evac, sq_used, ms_q, sd_q, qk_ready = (sem(n) for n in (
            "proj_done", "proj_evac", "sq_used", "ms_q", "sd_q", "qk_ready"))
        qkT_done, qkT_evac, rot_done, rope_done = (sem(n) for n in ("qkT_done", "qkT_evac", "rot_done", "rope_done"))
        sc_done, max_ready, exp_done, comb_done, aT_done, aT_evac, av_done, o_evac, o_sq = (sem(n) for n in (
            "sc_done", "max_ready", "exp_done", "comb_done", "aT_done", "aT_evac", "av_done", "o_evac", "o_sq"))
        ms_o, sd_o, o_ready, mixT_done, mixT_ready = (sem(n) for n in ("ms_o", "sd_o", "o_ready", "mixT_done", "mixT_ready"))
        sig_g, st_done, std_ready, yv_done, y_evac, y_sq = (sem(n) for n in (
            "sig_g", "st_done", "std_ready", "yv_done", "y_evac", "y_sq"))
        op_done, res_ready, h2_ready, h2T_done, h2T_ready, lg_done, lg_ready = (sem(n) for n in (
            "op_done", "res_ready", "h2_ready", "h2T_done", "h2T_ready", "lg_done", "lg_ready"))
        ev_in, ev_ready, mask_ready, rank_done, pos_ready, h2_stored = (sem(n) for n in (
            "ev_in", "ev_ready", "mask_ready", "rank_done", "pos_ready", "h2_stored"))
        over_ready = sem("over_ready")
        b_in, fetches, tokens_ready = sem("b_in"), sem("fetches"), sem("tokens_ready")
        y_stored = [sem(f"y_stored{q}") for q in range(2)]
        gts_ready, gT_done, gT_ready, bias_done, bias_added = (sem(n) for n in (
            "gts_ready", "gT_done", "gT_ready", "bias_done", "bias_added"))
        all_stored, vacant_ready = sem("all_stored"), sem("vacant_ready")
        chosen_in = [sem(f"chosen_in{b}") for b in range(NB)]
        row_in = [sem(f"row_in{q}") for q in range(2)]
        (hot_ready, idx_done, idx_ready, hrT_done, htE_ready, up_done, ub_ready, glu_ready, lin_ready, gl_ready,
         sg_ready, act_ready, acthi_ready, actlo_ready, whi_ready, wlo_ready, slice_used, chunk_used, y_ready, sum_ready, out_done) = (sem(n) for n in (
             "hot_ready", "idx_done", "idx_ready", "hrT_done", "htE_ready", "up_done", "ub_ready", "glu_ready",
             "lin_ready", "gl_ready", "sg_ready", "act_ready", "acthi_ready", "actlo_ready", "whi_ready", "wlo_ready",
             "slice_used", "chunk_used", "y_ready", "sum_ready",
             "out_done"))

        def pcols(name):
            a, b = PK[name]
            return par_sb[:, a:b]

        def bank(b, a=0, n=W):
            return ps[:, b, a:a + n]

        def wide(b):
            return ps[:, b:b + 2, :]

        def spread(ap, n):
            return ap.unsqueeze(len(ap.shape)).to_broadcast(list(ap.shape) + [n])

        x_v = x.rearrange("a (b p) d -> (a b) p d", p=P)
        out_v = out.rearrange("a (b p) d -> (a b) p d", p=P)
        w_in_v = w_in.rearrange("a (k p) n -> p (a k) n", p=P)
        w_out_v = w_out.rearrange("a (k p) n -> p (a k) n", p=P)
        w1_v = w1.rearrange("a e (k p) n -> (a e) p k n", p=P)
        w2_v = w2.rearrange("a e (k p) n -> (a e) p k n", p=P)
        h2_v = h2_rows.rearrange("(b p) d -> b p d", p=P)

        def pair(s):
            return ring[:, s:s + 2, :].rearrange("p s (k n) -> p (s k) n", n=W)

        def over_count(eng):
            return eng.value_load(over_at[0:1, MAX_OVER:MAX_OVER + 1], min_val=0, max_val=MAX_OVER)

        def further(eng, one_pass):
            eng.wait_ge(over_ready, 1)
            n_over = over_count(eng)
            with eng.If(n_over > 0):
                with eng.Fori(0, n_over) as j:
                    at = eng.value_load(over_at[0:1, bass.ds(j, 1)], min_val=0, max_val=MAX_CHUNK * NE - 1)
                    e = eng.value_load(over_e[0:1, bass.ds(j, 1)], min_val=0, max_val=NE - 1)
                    one_pass(j + NE, e, at)

        block = ctx.enter_context(nc.Block())

        @block.sync
        def _(sp):
            for b in range(NB):
                sp.dma_start(X[:, b, :], x_v[b]).then_inc(x_in[b], 16)
            for g, (_, c) in enumerate(GROUPS):
                if g >= 3:
                    sp.wait_ge(proj_done, 4 * (g - 2))
                sp.dma_start(pair(2 * (g % 3)), w_in_v[:, :, c:c + W]).then_inc(ring_in[2 * (g % 3)], 16)
            for n in range(2):
                sp.wait_ge(proj_done, 4 * (5 + n))
                sp.dma_start(pair(2 + 2 * n), w_out_v[:, :, n * W:(n + 1) * W]).then_inc(ring_in[2 + 2 * n], 16)

            def load(e, c):
                if c < 4:
                    src = w1_v[bass.ds(e, 1), :, :, W1_COLS[c]:W1_COLS[c] + W]
                else:
                    src = w2_v[bass.ds(e, 1), :, :, (c - 4) * W:(c - 3) * W]
                sp.dma_start(pair(2 * ORDER[c]), src.rearrange("a p k n -> p (a k) n")).then_inc(ring_in[2 * ORDER[c]], 16)

            for c in range(CHUNKS):
                s = ORDER[c]
                if c == 0:
                    sp.wait_ge(proj_done, 4 * 7)
                if s == 3:
                    sp.wait_ge(mixT_done, NB)
                    sp.wait_ge(sc_done, 2 * NB * HEADS)
                if s == 4:
                    sp.wait_ge(op_done, 2 * NB)
                if s == 5:
                    sp.wait_ge(yv_done, NB * HEADS)
                    sp.wait_ge(o_ready, 2)
                if s == 1:
                    sp.wait_ge(op_done, 2 * NB)
                load(0, c)

            def weights(n, e):
                for c in range(CHUNKS):
                    if c in (0, 2):
                        sp.wait_ge(chunk_used, 2 * n + (c // 2 - 1))
                    elif c < 4:
                        sp.wait_ge(up_done, 4 * n + (c - 3))
                    else:
                        sp.wait_ge(wlo_ready, 2 * KD * n + KD * (c - 5))
                    load(e, c)

            with sp.Fori(1, NE) as n:
                weights(n, n)
            further(sp, lambda n, e, at: weights(n, e))
            sp.wait_ge(all_stored, 1)
            for b in range(NB):
                sp.dma_start(chosen[:, b, :, :], y_rows[b * P * TOPK:(b + 1) * P * TOPK, :].rearrange(
                    "(p k) d -> p k d", k=TOPK)).then_inc(chosen_in[b], 16)
            for b in range(NB):
                sp.wait_ge(sum_ready, TOPK * (b + 1))
                sp.dma_start(out_v[b], X[:, b, :]).then_inc(out_done, 16)
            sp.wait_ge(out_done, 16 * NB)

        @block.gpsimd
        def _(pool):
            nc.gpsimd.memset(ident[:, :], 0.0).then_inc(consts0, 1)
            nc.gpsimd.memset(before[:, :], 1.0).then_inc(consts0, 1)
            nc.gpsimd.memset(swap[:, :], 0.0).then_inc(consts0, 1)
            nc.gpsimd.memset(ones[:, :], 1.0).then_inc(consts0, 1)
            pool.wait_ge(consts0, 4)
            nc.gpsimd.affine_select(out=ident[:, :], in_=ident[:, :], compare_op=ALU.not_equal, fill=1.0, base=0,
                                    pattern=[[-1, P]], channel_multiplier=1).then_inc(consts, 1)
            nc.gpsimd.affine_select(out=before[:, :], in_=before[:, :], compare_op=ALU.is_gt, fill=0.0, base=0,
                                    pattern=[[1, P]], channel_multiplier=-1).then_inc(consts, 1)
            nc.gpsimd.affine_select(out=swap[:, :], in_=swap[:, :], compare_op=ALU.not_equal, fill=-1.0, base=-DH,
                                    pattern=[[-1, P]], channel_multiplier=1).then_inc(consts0, 1)
            pool.wait_ge(consts0, 5)
            nc.gpsimd.affine_select(out=swap[:, :], in_=swap[:, :], compare_op=ALU.not_equal, fill=1.0, base=DH,
                                    pattern=[[-1, P]], channel_multiplier=1).then_inc(consts, 1)
            nc.gpsimd.iota(iota_s[:, :], pattern=[[1, P]], base=0, channel_multiplier=0,
                           allow_small_or_imprecise_dtypes=True).then_inc(consts, 1)
            nc.gpsimd.iota(dist, pattern=[[1, DIST]], base=-(T - P), channel_multiplier=-1,
                           allow_small_or_imprecise_dtypes=True).then_inc(consts, 1)
            nc.gpsimd.iota(place_id, pattern=[[0, 1]], base=0, channel_multiplier=1,
                           allow_small_or_imprecise_dtypes=True).then_inc(consts, 1)
            nc.gpsimd.iota(token_row, pattern=[[TOPK * P, NB]], base=-ASSIGNED, channel_multiplier=TOPK,
                           allow_small_or_imprecise_dtypes=True).then_inc(consts, 1)
            pool.wait_ge(mixT_done, 2 * NB)
            nc.gpsimd.iota(tokens[:, :, :, 0], pattern=[[0, NE], [P, NB]], base=0, channel_multiplier=1,
                           allow_small_or_imprecise_dtypes=True).then_inc(consts, 1)

            def fetch(n, q):
                pool.wait_ge(idx_ready, n + 1)
                pool.sem_inc(fetches, 1)
                nc.gpsimd.indirect_dma_start(hrow[:, q, :], None, h2_rows,
                                             bass.IndirectOffsetOnAxis(ap=place_idx[0:CAP, q:q + 1], axis=0)
                                             ).then_inc(row_in[q], 16)

            def put(n, q):
                pool.wait_ge(y_ready, n + 1)
                pool.sem_inc(fetches, 1)
                nc.gpsimd.indirect_dma_start(y_rows, bass.IndirectOffsetOnAxis(ap=place_row[0:CAP, q:q + 1], axis=0),
                                             yrows, None).then_inc(y_stored[q], 16)

            pool.wait_ge(h2_stored, 16 * NB)
            fetch(0, 0)
            fetch(1, 1)
            with pool.Fori(0, NE // 2 - 1) as i:
                put(2 * i, 0)
                fetch(2 * i + 2, 0)
                put(2 * i + 1, 1)
                fetch(2 * i + 3, 1)
            put(NE - 2, 0)
            put(NE - 1, 1)

            def over_pass(n, e, at):
                fetch(n, 0)
                put(n, 0)

            further(pool, over_pass)
            n_over = over_count(pool)
            pool.wait_ge(y_stored[0], 16 * n_over + 8 * NE)
            pool.wait_ge(y_stored[1], 8 * NE)
            pool.sem_inc(all_stored, 1)

        @block.scalar
        def _(act):
            own = [0]

            def link(ins):
                own[0] += 1
                ins.then_inc(act_own, 1)
                act.wait_ge(act_own, own[0])

            act.dma_start(par_sb[:, :], par).then_inc(par_in, 16)
            act.dma_start(pos_sb, pos).then_inc(pos_in, 16)
            for b in range(NB):
                act.wait_ge(x_in[b], 16)
                nc.scalar.activation(sqs, X[:, b, :], ACT.Square, accum_out=ssx[:, b:b + 1]).then_inc(sq_x, 1)
                act.wait_ge(sq_x, b + 1)
                act.wait_ge(ms_x, b + 1)
                nc.scalar.activation(msx[:, b:b + 1], msx[:, b:b + 1], ACT.Sqrt).then_inc(sd_x, 1)
                act.wait_ge(rs_x, b + 1)
                if b >= 2:
                    act.wait_ge(xT_done, b - 1)
                nc.scalar.activation(xs[:, b % 2, :], X[:, b, :], ACT.Copy, scale=rsx[:, b:b + 1]).then_inc(xs_ready, 1)

            def evac(j):
                g, i = divmod(j, 4)
                name = GROUPS[g][0]
                act.wait_ge(proj_done, j + 1)
                src = bank(j % 2)
                if name in ("Qd", "Kd"):
                    if j >= 2:
                        act.wait_ge(sq_used, j - 1)
                    nc.scalar.activation((rq if name == "Qd" else rk)[:, i, :], src, ACT.Copy)
                    nc.scalar.activation(sqs[:, (j % 2) * W:(j % 2 + 1) * W], src, ACT.Square).then_inc(proj_evac, 1)
                elif name in ("Qr", "Kr"):
                    r = j - 20
                    if r >= 2:
                        act.wait_ge(rope_done, r - 1)
                    nc.scalar.activation(qsb[:, j % 2, :], src, ACT.Copy,
                                         scale=1.0 if name == "Qr" else P ** -0.5).then_inc(proj_evac, 1)
                else:
                    dst = {"Vd": vd, "Vr": vr, "G": gg}[name]
                    nc.scalar.activation(dst[:, i, :], src, ACT.Copy).then_inc(proj_evac, 1)

            evac(0)
            act.wait_ge(red_ready, 1)
            nc.scalar.activation(sinT, red[:, 0, 0:T], ACT.Sin)
            nc.scalar.activation(cosT, red[:, 1, 0:T], ACT.Sin)
            nc.scalar.activation(cs_row[:, :, :], red[:, :, T:NANG], ACT.Sin).then_inc(trig_ready, 1)
            for j in range(1, 8):
                evac(j)
            act.wait_ge(ms_q, 1)
            nc.scalar.activation(msq[:, 0, :], msq[:, 0, :], ACT.Sqrt).then_inc(sd_q, 1)
            act.wait_ge(ms_q, 2)
            nc.scalar.activation(msq[:, 1, :], msq[:, 1, :], ACT.Sqrt).then_inc(sd_q, 1)
            for j in range(8, 12):
                evac(j)
            for g, dst in enumerate((qdT, kdT)):
                for i in range(NB):
                    act.wait_ge(qkT_done, 4 * g + i + 1)
                    nc.scalar.activation(dst[:, :, i * P:(i + 1) * P],
                                         bank(3 + i).rearrange("p (h t) -> p h t", h=HEADS), ACT.Copy,
                                         scale=DH ** -0.5 if g == 0 else 1.0).then_inc(qkT_evac, 1)

            act.wait_ge(lam_in, 1)
            nc.scalar.activation(lam2, lamt, ACT.Exp).then_inc(lam_exp, 1)

            def a_out(u):
                act.wait_ge(aT_done, u + 1)
                if u >= 2:
                    act.wait_ge(av_done, u - 1)
                nc.scalar.activation(aT[:, u % 2, :], bank(7), ACT.Copy).then_inc(aT_evac, 1)

            def o_out(i):
                act.wait_ge(av_done, HEADS * (i + 1))
                nc.scalar.activation(orow[:, i, :], bank(2), ACT.Copy)
                if i >= 1:
                    act.wait_ge(o_sq, i)
                nc.scalar.activation(sqs[:, 0:W], bank(2), ACT.Square).then_inc(o_evac, 1)

            for u in range(NB * HEADS):
                for s in range(2):
                    k = 2 * u + s
                    act.wait_ge(max_ready, k + 1)
                    if u >= 2:
                        act.wait_ge(comb_done, u - 1)
                    nc.scalar.activation(prob[:, 2 * (u % 2) + s, :], bank(3 + 2 * (u % 2) + s), ACT.Exp,
                                         bias=negmax[:, k:k + 1], accum_out=rowsum[:, k:k + 1]).then_inc(exp_done, 1)
                evac(12 + u)
                if u >= 1:
                    a_out(u - 1)
                if u >= 5 and u % 4 == 1:
                    o_out(u // 4 - 1)
                if 1 <= u <= HEADS:
                    act.wait_ge(dexp_in, u)
                    nc.scalar.activation(decay[:, u - 1, :], decay[:, u - 1, :], ACT.Exp).then_inc(dexp_ready, 1)
            a_out(15)
            o_out(3)
            act.wait_ge(rope_done, 8)
            nc.scalar.activation(sig, gg, ACT.Sigmoid).then_inc(sig_g, 1)
            act.wait_ge(ms_o, 1)
            nc.scalar.activation(mso[:, 0, :], mso[:, 0, :], ACT.Sqrt).then_inc(sd_o, 1)
            for i in range(NB):
                act.wait_ge(yv_done, NB * HEADS)
                if i == 0:
                    act.wait_ge(comb_done, NB * HEADS)
                nc.scalar.activation(yrow[:, i, :], bank(2 + i), ACT.Copy)
                if i >= 2:
                    act.wait_ge(y_sq, i - 1)
                nc.scalar.activation(sqs[:, (i % 2) * W:(i % 2 + 1) * W], bank(2 + i), ACT.Square).then_inc(y_evac, 1)
            act.wait_ge(ms_o, 2)
            nc.scalar.activation(mso[:, 1, :], mso[:, 1, :], ACT.Sqrt).then_inc(sd_o, 1)
            act.dma_start(b1_sb, b1t.rearrange("p (e n) -> p e n", e=NE)).then_inc(b_in, 16)
            act.dma_start(wr_sb, w_router.rearrange("a (k p) e -> p (a k) e", p=P)).then_inc(wr_in, 16)
            act.dma_start(b2_sb, b2.rearrange("a e d -> (a e) d")).then_inc(b_in, 16)
            for b in range(NB):
                act.wait_ge(res_ready, 2 * (b + 1))
                nc.scalar.activation(sqs, X[:, b, :], ACT.Square, accum_out=ssx[:, NB + b:NB + b + 1]).then_inc(sq_x, 1)
                act.wait_ge(sq_x, NB + b + 1)
                act.wait_ge(ms_x, NB + b + 1)
                nc.scalar.activation(msx[:, NB + b:NB + b + 1], msx[:, NB + b:NB + b + 1], ACT.Sqrt).then_inc(sd_x, 1)
                act.wait_ge(rs_x, NB + b + 1)
                nc.scalar.activation(h2[:, b, :], X[:, b, :], ACT.Copy, scale=rsx[:, NB + b:NB + b + 1]).then_inc(h2_ready, 1)
            for b in range(NB):
                act.wait_ge(h2_ready, b + 1)
                act.dma_start(h2_v[b], h2[:, b, :]).then_inc(h2_stored, 16)
            act.wait_ge(ev_in, 1)
            nc.scalar.activation(ev, ev, ACT.Exp).then_inc(ev_ready, 1)

            def gate_sigmoid(n, t):
                act.wait_ge(glu_ready, 4 * n + (t + 1))
                nc.scalar.activation(sg[:, t % 2, :], ub[:, t % 2, 0:2 * CAP], ACT.Sigmoid, scale=ALPHA).then_inc(sg_ready, 1)

            def y_out(n, q, before):
                act.wait_ge(slice_used, 2 * KD * (n + 1))
                if before is not None:
                    act.wait_ge(y_stored[1 - q], before)
                nc.scalar.activation(yrows, ps[0:CAP, 4:6, :], ACT.Copy).then_inc(y_ready, 1)

            def act_high(n, t):
                act.wait_ge(act_ready, 4 * n + (t + 1))
                nc.scalar.activation(act_hi[:, 2 * t:2 * t + 2, :], actT[:, 2 * t:2 * t + 2, :], ACT.Copy
                                     ).then_inc(acthi_ready, 1)

            def w_high(n, j, first=False):
                s, k = divmod(j, KD)
                if k == 0:
                    act.wait_ge(ring_in[2 * ORDER[4 + s]], 16 * n + 16 * (FRONT_LOADS[ORDER[4 + s]] + 1))
                if j >= SLICES or not first:
                    act.wait_ge(slice_used, 2 * KD * n + (j + 1 - SLICES))
                nc.scalar.activation(w_hi[:, j % SLICES, :], pair(2 * ORDER[4 + s])[:, k, :], ACT.Copy).then_inc(whi_ready, 1)

            def one_pass(n, first=False):
                for t in range(3):
                    gate_sigmoid(n, t)
                    if t:
                        act_high(n, t - 1)
                for j in range(SLICES):
                    w_high(n, j, first)
                act_high(n, 2)
                gate_sigmoid(n, 3)
                w_high(n, SLICES)
                act_high(n, 3)
                for j in range(SLICES + 1, 2 * KD):
                    w_high(n, j)

            def over_pass(n, e, at):
                one_pass(n)
                act.wait_ge(y_stored[1], 8 * NE)
                y_out(n, 1, 16 * n - 8 * NE)

            act.wait_ge(gT_done, 1)
            nc.scalar.activation(gatesT, ps[0:NE, 2, :], ACT.Copy).then_inc(gT_ready, 1)
            one_pass(0, first=True)
            y_out(0, 0, None)
            with act.Fori(0, NE // 2 - 1) as i:
                one_pass(2 * i + 1)
                y_out(2 * i + 1, 1, 16 * i + 16)
                one_pass(2 * i + 2)
                y_out(2 * i + 2, 0, 16 * i + 16)
            one_pass(NE - 1)
            y_out(NE - 1, 1, 8 * NE)
            further(act, over_pass)

        @block.vector
        def _(v):
            own = [0]

            def link(ins):
                own[0] += 1
                ins.then_inc(dve, 1)
                v.wait_ge(dve, own[0])

            TS, TT, STT = nc.vector.tensor_scalar, nc.vector.tensor_tensor, nc.vector.scalar_tensor_tensor

            def norm_x(b, k):
                v.wait_ge(sq_x, k + 1)
                TS(msx[:, k:k + 1], ssx[:, k:k + 1], 1.0 / D, EPS, ALU.mult, ALU.add).then_inc(ms_x, 1)
                v.wait_ge(sd_x, k + 1)
                nc.vector.reciprocal(rsx[:, k:k + 1], msx[:, k:k + 1]).then_inc(rs_x, 1)

            def norm_T(b):
                v.wait_ge(xT_done, b + 1)
                if b == 0:
                    v.wait_ge(par_in, 16)
                TT(hT[:, :, b * P:(b + 1) * P], wide(2 * b).rearrange("p s (k t) -> p (s k) t", t=P),
                   spread(pcols("n1w"), P), ALU.mult).then_inc(hT_ready, 1)

            for b in range(NB):
                norm_x(b, b)
                if b >= 1:
                    norm_T(b - 1)
            v.wait_ge(pos_in, 16)
            v.wait_ge(consts, 5)
            link(nc.vector.tensor_copy(ang[:, 0:T], pos_sb[:, 0:T]))
            link(nc.vector.tensor_copy(esum, pos_sb[:, T:T + NB]))
            link(TS(ang[:, 0:T], ang[:, 0:T], pcols("invcol"), None, ALU.mult))
            for b in range(NB):
                link(TS(ang[:, T + b * NF8:T + (b + 1) * NF8], pcols("inv8"), esum[:, b:b + 1], None, ALU.mult))
            for s, shift in enumerate((0.0, 0.25)):
                r = red[:, s, :]
                link(TS(turns, ang, 1.0 / TWO_PI, shift, ALU.mult, ALU.add))
                link(TS(turns, turns, MAGIC, MAGIC, ALU.add, ALU.subtract))
                link(STT(r, turns, -C1, ang, ALU.mult, ALU.add))
                link(STT(r, turns, -C2, r, ALU.mult, ALU.add))
                link(STT(r, turns, -C3, r, ALU.mult, ALU.add))
                if s:
                    link(TS(r, r, float(np.pi / 2), None, ALU.add))
                ins = TS(r, r, PI_LOW, -PI_LOW, ALU.min, ALU.max)
                if s:
                    ins.then_inc(red_ready, 1)
                else:
                    link(ins)
                    norm_T(NB - 1)
            lam = pcols("lam").rearrange("p (a b c) -> p a b c", a=2, b=2)
            prod = turns[:, 0:2 * DH].rearrange("p (a c) -> p a c", a=2)
            link(TT(prod, lam[:, :, 0, :], lam[:, :, 1, :], ALU.mult))
            nc.vector.reduce_sum(lamt, prod, AX.X).then_inc(lam_in, 1)
            def qk_sums(g):
                for i in range(NB):
                    j = 4 * g + i
                    v.wait_ge(proj_evac, j + 1)
                    nc.vector.reduce_sum(ssq[:, g, 8 * i:8 * i + 8],
                                         sqs[:, (j % 2) * W:(j % 2 + 1) * W].rearrange("p (a c) -> p a c", a=8),
                                         AX.X).then_inc(sq_used, 1)
                v.wait_ge(sq_used, 4 * g + 4)
                TS(msq[:, g, :], ssq[:, g, :], 1.0 / DH, EPS, ALU.mult, ALU.add).then_inc(ms_q, 1)

            def qk_rest(g):
                r, w = (rq, pcols("qw")) if g == 0 else (rk, pcols("kw"))
                v.wait_ge(sd_q, g + 1)
                link(nc.vector.reciprocal(rsq[:, g, :], msq[:, g, :]))
                for i in range(NB):
                    cell = r[:, i, :].rearrange("p (a c) -> p a c", a=8)
                    link(TT(cell, cell, spread(rsq[:, g, 8 * i:8 * i + 8], DH), ALU.mult))
                    link(TT(cell, cell, w.unsqueeze(1).to_broadcast([P, 8, DH]), ALU.mult))
                cells = r.rearrange("p b (a c) -> p b a c", a=8)
                x1, x2 = cells[:, :, :, 0:NF8], cells[:, :, :, NF8:ROT]
                s, c = (cs_row[:, k, :].rearrange("p (b f) -> p b f", b=NB).unsqueeze(2).to_broadcast([P, NB, 8, NF8])
                        for k in range(2))
                t = [ropet[:, k, :].rearrange("p (b a f) -> p b a f", b=NB, a=8) for k in range(4)]
                if g == 0:
                    v.wait_ge(trig_ready, 1)
                link(TT(t[0], x1, c, ALU.mult))
                link(TT(t[1], x2, s, ALU.mult))
                link(TT(t[2], x2, c, ALU.mult))
                link(TT(t[3], x1, s, ALU.mult))
                link(TT(x1, t[0], t[1], ALU.subtract))
                TT(x2, t[2], t[3], ALU.add).then_inc(qk_ready, 1)
                v.wait_ge(qk_ready, g + 1)

            qk_sums(0)
            qk_sums(1)
            qk_rest(0)
            qk_rest(1)
            v.wait_ge(lam_exp, 1)
            link(TT(neglam, lam2[:, 1:2], lam2[:, 0:1], ALU.subtract))
            link(TS(neglam, neglam, LAMBDA_INIT, None, ALU.subtract))
            link(TS(dw, pcols("diffw"), 1.0 - LAMBDA_INIT, None, ALU.mult))

            def decay_exponents(h):
                link(TS(dtmp, dist, 0.0, pcols("ldb")[:, h:h + 1], ALU.min, ALU.mult))
                link(TS(decay[:, h, :], dist, 0.0, pcols("ldf")[:, h:h + 1], ALU.max, ALU.mult))
                TT(decay[:, h, :], decay[:, h, :], dtmp, ALU.subtract).then_inc(dexp_in, 1)
                v.wait_ge(dexp_in, h + 1)

            def comb(u):
                v.wait_ge(exp_done, 2 * u + 2)
                link(nc.vector.reciprocal(rowinv[:, 2 * u:2 * u + 2], rowsum[:, 2 * u:2 * u + 2]))
                link(TT(lamc[:, u:u + 1], rowinv[:, 2 * u + 1:2 * u + 2], neglam, ALU.mult))
                p1, p2 = prob[:, 2 * (u % 2), :], prob[:, 2 * (u % 2) + 1, :]
                if u >= 2:
                    v.wait_ge(aT_done, u - 1)
                link(TS(amix[:, u % 2, :], p2, lamc[:, u:u + 1], None, ALU.mult))
                STT(amix[:, u % 2, :], p1, rowinv[:, 2 * u:2 * u + 1], amix[:, u % 2, :], ALU.mult, ALU.add
                    ).then_inc(comb_done, 1)

            def rope(r):
                q = r % 2
                dst = (qrT if r < 4 else krT)[:, r % 4, :]
                v.wait_ge(proj_evac, 20 + r + 1)
                if r == 0:
                    v.wait_ge(qkT_done, 8)
                link(TT(roped[:, 0, :], qsb[:, q, :], cosT, ALU.mult))
                v.wait_ge(rot_done, r + 1)
                link(TT(roped[:, 1, :], bank(q), sinT, ALU.mult))
                TT(dst, roped[:, 0, :], roped[:, 1, :], ALU.add).then_inc(rope_done, 1)
                v.wait_ge(rope_done, r + 1)

            def o_sum(i):
                v.wait_ge(o_evac, i + 1)
                nc.vector.reduce_sum(sso[:, 0, 4 * i:4 * i + 4], sqs[:, 0:W].rearrange("p (h c) -> p h c", h=HEADS),
                                     AX.X).then_inc(o_sq, 1)

            for u in range(NB * HEADS):
                for s in range(2):
                    v.wait_ge(sc_done, 2 * u + s + 1)
                    nc.vector.tensor_reduce(negmax[:, 2 * u + s:2 * u + s + 1], bank(3 + 2 * (u % 2) + s), AX.X, ALU.max,
                                            negate=True).then_inc(max_ready, 1)
                comb(u)
                if u >= 9:
                    rope(u - 9)
                if u >= 5 and u % 4 == 1:
                    o_sum(u // 4 - 1)
                if u < HEADS:
                    decay_exponents(u)
            rope(7)
            o_sum(3)

            def finish_heads(k, rows, count, size):
                v.wait_ge(o_sq if k == 0 else y_sq, NB)
                TS(mso[:, k, :], sso[:, k, :], 1.0 / DV, EPS, ALU.mult, ALU.add).then_inc(ms_o, 1)
                v.wait_ge(sd_o, k + 1)
                link(nc.vector.reciprocal(rso[:, k, :], mso[:, k, :]))
                flat = rows.rearrange("p b (h c) -> p (b h) c", h=HEADS)
                return TT(flat, flat, spread(rso[:, k, :], DV), ALU.mult)

            finish_heads(0, orow, 16, DV).then_inc(o_ready, 1)

            v.wait_ge(dexp_ready, HEADS)
            for q in range(NB * HEADS):
                h, m = divmod(q, NB)
                v.wait_ge(st_done, q + 1)
                if q >= 2:
                    v.wait_ge(yv_done, q - 1)
                a = (T - P) - P * m
                TT(std[:, q % 2, :], bank((0, 1, 6, 7)[q % 4]), decay[:, h, a:a + T], ALU.mult).then_inc(std_ready, 1)
            v.wait_ge(sig_g, 1)
            gflat = gg.rearrange("p b c -> p (b c)")
            link(TT(gflat, gflat, sig, ALU.mult))
            def mix_columns(k, i):
                t = 4 * k + i
                v.wait_ge(mixT_done, t + 1)
                src = bank(6 + t % 2).rearrange("p (h t) -> p h t", h=HEADS)
                if k == 0:
                    TS(mixT[:, 4:8, i * P:(i + 1) * P], src, dw, None, ALU.mult).then_inc(mixT_ready, 1)
                else:
                    TT(mixT[:, 0:4, i * P:(i + 1) * P], src, spread(pcols("retw"), P), ALU.mult).then_inc(mixT_ready, 1)

            for i in range(NB):
                mix_columns(0, i)
            for i in range(NB):
                v.wait_ge(y_evac, i + 1)
                nc.vector.reduce_sum(sso[:, 1, 4 * i:4 * i + 4],
                                     sqs[:, (i % 2) * W:(i % 2 + 1) * W].rearrange("p (h c) -> p h c", h=HEADS),
                                     AX.X).then_inc(y_sq, 1)
            link(finish_heads(1, yrow, 16, DV))
            TT(yrow, yrow, gg, ALU.mult).then_inc(o_ready, 1)
            for i in range(NB):
                mix_columns(1, i)

            def h2_T(b):
                v.wait_ge(h2T_done, b + 1)
                if b >= 2:
                    v.wait_ge(lg_done, b - 1)
                TT(h2T[:, b % 2, :].rearrange("p (k t) -> p k t", k=KD),
                   wide(4 + 2 * (b % 2)).rearrange("p s (k t) -> p (s k) t", t=P),
                   spread(pcols("n2w"), P), ALU.mult).then_inc(h2T_ready, 1)

            def choose(b):
                v.wait_ge(lg_done, b + 1)
                TT(logits[:, b, :], bank(b, 0, NE), pcols("brt"), ALU.add).then_inc(lg_ready, 1)
                v.wait_ge(lg_ready, b + 1)
                link(nc.vector.max(top8[:, b, :], logits[:, b, :]))
                link(nc.vector.max_index(idx8[:, b, :], top8[:, b, :], logits[:, b, :]))

            for b in range(NB):
                for s in range(2):
                    w = 2 * b + s
                    v.wait_ge(op_done, w + 1)
                    cell = X[:, b, s * W:(s + 1) * W]
                    TT(cell, bank(w % 4), cell, ALU.add).then_inc(res_ready, 1)
                norm_x(b, NB + b)
                if b >= 1:
                    h2_T(b - 1)
            h2_T(NB - 1)
            for b in range(NB):
                choose(b)
            link(TT(ev, top8[:, :, 0:TOPK], top8[:, :, 0:1].to_broadcast([P, NB, TOPK]), ALU.subtract))
            nc.vector.tensor_copy(topf, idx8[:, :, :]).then_inc(ev_in, 1)
            v.wait_ge(ev_in, 1)
            iota_e = iota_s[:, 0:NE].unsqueeze(1).to_broadcast([P, NB, NE])
            for k in range(TOPK):
                at = topf[:, :, k:k + 1].to_broadcast([P, NB, NE])
                if k == 0:
                    link(TT(mask, iota_e, at, ALU.is_equal))
                else:
                    link(TT(eq, iota_e, at, ALU.is_equal))
                    if k == 1:
                        link(nc.vector.tensor_copy(choice, eq))
                    else:
                        link(STT(choice, eq, float(k), choice, ALU.mult, ALU.add))
                    ins = TT(mask, mask, eq, ALU.add)
                    if k == TOPK - 1:
                        ins.then_inc(mask_ready, 1)
                    else:
                        link(ins)
            v.wait_ge(consts, 8)
            link(TT(tokens[:, :, :, 1], choice.rearrange("p b e -> p e b"), token_row.unsqueeze(1).to_broadcast([P, NE, NB]),
                    ALU.add))
            v.wait_ge(rank_done, 1)
            link(TS(eq, bank(1, 0, NB * NE).rearrange("p (b e) -> p b e", b=NB), 1.0, None, ALU.add))
            link(TT(eq, eq, mask, ALU.mult))
            for c in range(MAX_CHUNK):
                ins = TS(posm[:, c, :, :], eq.rearrange("p b e -> p e b"), -1.0 - CAP * c, None, ALU.add)
                if c == MAX_CHUNK - 1:
                    ins.then_inc(pos_ready, 1)
                else:
                    link(ins)
            v.wait_ge(pos_ready, 1)
            v.wait_ge(ev_ready, 1)
            link(nc.vector.reduce_sum(esum, ev, AX.X))
            link(nc.vector.reciprocal(esum, esum))
            link(TT(gate4, ev, spread(esum, TOPK), ALU.mult))

            def chose(k, out):
                link(TT(out, iota_e, topf[:, :, k:k + 1].to_broadcast([P, NB, NE]), ALU.is_equal))

            def all_gates():
                for k in range(TOPK):
                    dst = eq if k else gts
                    chose(k, dst)
                    link(TT(dst, dst, gate4[:, :, k:k + 1].to_broadcast([P, NB, NE]), ALU.mult))
                    if k:
                        ins = TT(gts, gts, eq, ALU.add)
                        if k == TOPK - 1:
                            ins.then_inc(gts_ready, 1)
                        else:
                            link(ins)

            def hot(n, at):
                TT(onehot, iota_s[:, 0:CAP].unsqueeze(1).to_broadcast([P, NB, CAP]),
                   spread(posm.rearrange("p c e b -> p (c e) b")[:, bass.ds(at, 1), :].rearrange("p a b -> p (a b)"), CAP), ALU.is_equal
                   ).then_inc(hot_ready, 1)

            def places(n, q, stored=None):
                v.wait_ge(idx_done, n + 1)
                if stored is not None:
                    v.wait_ge(y_stored[q], stored)
                nc.vector.tensor_copy(place_idx[0:CAP, q:q + 1], ps[0:CAP, 6, 0:1])
                at = ps[0:CAP, 6, 1:2]
                STT(vacant[0:CAP], at, 0.0, place_id[0:CAP], ALU.is_ge, ALU.mult).then_inc(vacant_ready, 1)
                v.wait_ge(vacant_ready, n + 1)
                STT(place_row[0:CAP, q:q + 1], at, float(ASSIGNED), vacant[0:CAP], ALU.add, ALU.add).then_inc(idx_ready, 1)

            def columns(n, q):
                v.wait_ge(hrT_done, n + 1)
                TT(htE[:, q, :].rearrange("p (k t) -> p k t", k=KD),
                   ps[:, 6:8, CAP:5 * CAP].rearrange("p s (k t) -> p s k t", t=CAP),
                   spread(pcols("n2w").rearrange("p (s k) -> p s k", s=2), CAP), ALU.mult).then_inc(htE_ready, 1)

            def swiglu(n, e, t, first=False):
                v.wait_ge(up_done, 4 * n + (t + 1))
                if t >= 2 or not first:
                    v.wait_ge(act_ready, 4 * n + (t - 1))
                TT(ub[:, t % 2, :].rearrange("p (m t) -> p m t", t=CAP), ps[:, t, 0:4 * CAP].rearrange("p (m t) -> p m t", t=CAP),
                   spread(b1_sb[:, bass.ds(e, 1), 4 * t:4 * t + 4].rearrange("p a m -> p (a m)"), CAP), ALU.add
                   ).then_inc(ub_ready, 1)
                glu, lin = ub[:, t % 2, 0:2 * CAP], ub[:, t % 2, 2 * CAP:4 * CAP]
                v.wait_ge(ub_ready, 4 * n + (t + 1))
                TS(glu, glu, LIMIT, None, ALU.min).then_inc(glu_ready, 1)
                TS(lin, lin, LIMIT, -LIMIT, ALU.min, ALU.max).then_inc(lin_ready, 1)
                v.wait_ge(lin_ready, 4 * n + (t + 1))
                STT(lin, lin, 1.0, glu, ALU.add, ALU.mult).then_inc(gl_ready, 1)
                v.wait_ge(gl_ready, 4 * n + (t + 1))
                v.wait_ge(sg_ready, 4 * n + (t + 1))
                TT(actT[:, 2 * t:2 * t + 2, :], lin.rearrange("p (m t) -> p m t", t=CAP),
                   sg[:, t % 2, :].rearrange("p (m t) -> p m t", t=CAP), ALU.mult).then_inc(act_ready, 1)

            def act_low(n, t):
                v.wait_ge(acthi_ready, 4 * n + (t + 1))
                TT(act_lo[:, 2 * t:2 * t + 2, :], actT[:, 2 * t:2 * t + 2, :], act_hi[:, 2 * t:2 * t + 2, :].bitcast(f32),
                   ALU.subtract).then_inc(actlo_ready, 1)

            def w_low(n, j):
                s, k = divmod(j, KD)
                v.wait_ge(whi_ready, 2 * KD * n + (j + 1))
                TT(w_lo[:, j % SLICES, :], pair(2 * ORDER[4 + s])[:, k, :], w_hi[:, j % SLICES, :].bitcast(f32),
                   ALU.subtract).then_inc(wlo_ready, 1)

            def later_half(n, e, first=False, next_rows=None):
                swiglu(n, e, 2, first)
                act_low(n, 1)
                if next_rows is not None:
                    columns(n + 1, next_rows)
                for j in range(SLICES):
                    w_low(n, j)
                act_low(n, 2)
                swiglu(n, e, 3, first)
                for j in range(SLICES, SLICES + 2):
                    w_low(n, j)
                act_low(n, 3)

            def expert(n, q, stored=None, first=False, last=False):
                if not last:
                    v.wait_ge(idx_done, n + 1)
                    hot(n + 1, n + 1)
                swiglu(n, n, 0, first)
                if not last:
                    places(n + 1, 1 - q, stored)
                swiglu(n, n, 1, first)
                act_low(n, 0)
                later_half(n, n, first, None if last else 1 - q)
                for j in range(SLICES + 2, 2 * KD):
                    w_low(n, j)

            v.wait_ge(b_in, 32)
            hot(0, 0)
            all_gates()
            places(0, 0)
            for c in range(1, MAX_CHUNK):
                key = over_key[:, c - 1, :]
                link(TS(key, iota_s[:, 0:NE], 1.0 + NE * c, None, ALU.add))
                link(STT(key, bank(1, NB * NE, NE), float(CAP * c), key, ALU.is_gt, ALU.mult))
            keys = over_key.rearrange("p c e -> p (c e)")
            for i in range(MAX_OVER // 8):
                top = over_top[:, 8 * i:8 * i + 8]
                link(nc.vector.max(top, keys))
                if i < MAX_OVER // 8 - 1:
                    link(nc.vector.match_replace(out=keys, in_to_replace=top, in_values=keys, imm_value=0.0))
            link(TS(over_some, over_top, 0.0, None, ALU.is_gt))
            link(nc.vector.reduce_sum(over_n, over_some, AX.X))
            link(nc.vector.tensor_copy(over_at[:, MAX_OVER:MAX_OVER + 1], over_n))
            link(TS(over_at[:, 0:MAX_OVER], over_top, -1.0, None, ALU.add))
            TS(over_e[:, :], over_at[:, 0:MAX_OVER], NE - 1, None, ALU.bitwise_and).then_inc(over_ready, 1)
            columns(0, 0)
            for w in range(2 * NB):
                v.wait_ge(bias_done, w + 1)
                cell = X[:, w // 2, w % 2 * W:(w % 2 + 1) * W]
                TT(cell, bank((6, 7, 2, 3)[w % 4]), cell, ALU.add).then_inc(bias_added, 1)
            expert(0, 0, first=True)
            with v.Fori(0, NE // 2 - 1) as i:
                expert(2 * i + 1, 1, 16 * i + 16)
                expert(2 * i + 2, 0, 16 * i + 16)
            expert(NE - 1, 1, last=True)

            def over_pass(n, e, at):
                v.wait_ge(idx_done, n)
                hot(n, at)
                places(n, 0, 16 * n - 8 * NE)
                columns(n, 0)
                swiglu(n, e, 0)
                swiglu(n, e, 1)
                act_low(n, 0)
                later_half(n, e)
                for j in range(SLICES + 2, 2 * KD):
                    w_low(n, j)

            further(v, over_pass)
            for b in range(NB):
                v.wait_ge(chosen_in[b], 16)
                for k in range(TOPK):
                    STT(X[:, b, :], chosen[:, b, k, :], gate4[:, b, k:k + 1], X[:, b, :], ALU.mult, ALU.add
                        ).then_inc(sum_ready, 1)
                    v.wait_ge(sum_ready, TOPK * b + k + 1)

        @block.tensor
        def _(pe):
            MM, TR = nc.tensor.matmul, nc.tensor.transpose
            pe.wait_ge(consts, 5)

            def turn_x(b):
                pe.wait_ge(xs_ready, b + 1)
                for k in range(KD):
                    t = TR(bank(2 * b + k // 4, (k % 4) * P, P), xs[:, b % 2, k * P:(k + 1) * P], ident[:, :])
                t.then_inc(xT_done, 1)

            def project(j):
                g, i = divmod(j, 4)
                if g == 0:
                    pe.wait_ge(hT_ready, i + 1)
                if i == 0:
                    pe.wait_ge(ring_in[2 * (g % 3)], 16 * (g // 3 + 1))
                if j >= 2:
                    pe.wait_ge(proj_evac, j - 1)
                if j >= 22:
                    pe.wait_ge(rope_done, j - 21)
                wt = pair(2 * (g % 3))
                for k in range(KD):
                    if g < 5:
                        lhs, rhs = hT[:, k, i * P:(i + 1) * P], wt[:, k, :]
                    else:
                        lhs, rhs = wt[:, k, i * P:(i + 1) * P], hT[:, k, :]
                    m = MM(bank(j % 2), lhs, rhs, start=k == 0, stop=k == KD - 1)
                m.then_inc(proj_done, 1)

            def rotate(r):
                pe.wait_ge(proj_evac, 20 + r + 1)
                MM(bank(r % 2), swap[:, :], qsb[:, r % 2, :], start=True, stop=True).then_inc(rot_done, 1)

            for b in range(NB - 1):
                turn_x(b)
            project(0)
            turn_x(NB - 1)
            for j in range(1, 12):
                project(j)
            for g, r in enumerate((rq, rk)):
                pe.wait_ge(qk_ready, g + 1)
                for i in range(NB):
                    if g == 1:
                        pe.wait_ge(qkT_evac, i + 1)
                    for h in range(HEADS):
                        t = TR(bank(3 + i, h * P, P), r[:, i, h * P:(h + 1) * P], ident[:, :])
                    t.then_inc(qkT_done, 1)

            def scores(u):
                i, h = divmod(u, HEADS)
                if u == 0:
                    pe.wait_ge(qkT_evac, 8)
                if u >= 2:
                    pe.wait_ge(exp_done, 2 * u - 2)
                for s in range(2):
                    MM(bank(3 + 2 * (u % 2) + s), qdT[s * DH:(s + 1) * DH, h, i * P:(i + 1) * P],
                       kdT[s * DH:(s + 1) * DH, h, :], start=True, stop=True).then_inc(sc_done, 1)

            def turn(u):
                pe.wait_ge(comb_done, u + 1)
                if u >= 1:
                    pe.wait_ge(aT_evac, u)
                for k in range(NB):
                    t = TR(bank(7, k * P, P), amix[:, u % 2, k * P:(k + 1) * P], ident[:, :])
                t.then_inc(aT_done, 1)

            def values(u):
                i, h = divmod(u, HEADS)
                pe.wait_ge(aT_evac, u + 1)
                if h == 0 and i >= 1:
                    pe.wait_ge(o_evac, i)
                for k in range(NB):
                    m = MM(bank(2, h * DV, DV), aT[:, u % 2, k * P:(k + 1) * P], vd[:, k, h * DV:(h + 1) * DV],
                           start=k == 0, stop=k == NB - 1)
                m.then_inc(av_done, 1)

            for u in range(NB * HEADS):
                scores(u)
                project(12 + u)
                if u >= 1:
                    turn(u - 1)
                if u >= 2:
                    values(u - 2)
                if u >= 9:
                    rotate(u - 9)
            turn(15)
            values(14)
            values(15)
            rotate(7)

            def ret_scores(q):
                h, m = divmod(q, NB)
                if q == 0:
                    pe.wait_ge(rope_done, 8)
                    pe.wait_ge(exp_done, 32)
                    pe.wait_ge(aT_evac, 16)
                if q >= 4:
                    pe.wait_ge(std_ready, q - 3)
                MM(bank((0, 1, 6, 7)[q % 4]), krT[:, h, m * P:(m + 1) * P], qrT[:, h, :], start=True, stop=True
                   ).then_inc(st_done, 1)

            def ret_values(q):
                h, m = divmod(q, NB)
                if q == 0:
                    pe.wait_ge(o_evac, NB)
                pe.wait_ge(std_ready, q + 1)
                for i in range(NB):
                    t = MM(bank(2 + i, h * DV, DV), std[:, q % 2, i * P:(i + 1) * P], vr[:, m, h * DV:(h + 1) * DV],
                           start=m == 0, stop=m == NB - 1)
                t.then_inc(yv_done, 1)

            ret_scores(0)
            ret_scores(1)
            for q in range(NB * HEADS):
                if q + 2 < NB * HEADS:
                    ret_scores(q + 2)
                ret_values(q)

            def turn_mix(k, rows):
                pe.wait_ge(o_ready, k + 1)
                for i in range(NB):
                    t = 4 * k + i
                    if t == 0:
                        pe.wait_ge(std_ready, NB * HEADS)
                    if t >= 2:
                        pe.wait_ge(mixT_ready, t - 1)
                    for h in range(HEADS):
                        m = TR(bank(6 + t % 2, h * P, P), rows[:, i, h * P:(h + 1) * P], ident[:, :])
                    m.then_inc(mixT_done, 1)

            def out_project(w, half):
                b, s = divmod(w, 2)
                if half and b == 0:
                    pe.wait_ge(ring_in[2 + 2 * s], 16 * 3)
                if half and w in (2, 3):
                    pe.wait_ge(y_evac, w - 1)
                if w >= 4 and half:
                    pe.wait_ge(res_ready, w - 3)
                pe.wait_ge(mixT_ready, b + 1 if half else NB + b + 1)
                for k in range(4 * half, 4 * half + 4):
                    m = MM(bank(w % 4), mixT[:, k, b * P:(b + 1) * P], pair(2 + 2 * s)[:, k, :],
                           start=k == 4, stop=k == 3)
                if not half:
                    m.then_inc(op_done, 1)

            turn_mix(0, orow)
            for w in range(4):
                out_project(w, 1)
            turn_mix(1, yrow)

            def h2_turn(b):
                pe.wait_ge(h2_ready, b + 1)
                if b == 0:
                    pe.wait_ge(mixT_ready, 8)
                if b >= 2:
                    pe.wait_ge(h2T_ready, b - 1)
                for k in range(KD):
                    m = TR(bank(4 + 2 * (b % 2) + k // 4, (k % 4) * P, P), h2[:, b, k * P:(k + 1) * P], ident[:, :])
                m.then_inc(h2T_done, 1)

            def route(b):
                pe.wait_ge(h2T_ready, b + 1)
                if b == 0:
                    pe.wait_ge(wr_in, 16)
                pe.wait_ge(res_ready, 2 * NB)
                for k in range(KD):
                    m = MM(bank(b, 0, NE), h2T[:, b % 2, k * P:(k + 1) * P], wr_sb[:, k, :],
                           start=k == 0, stop=k == KD - 1)
                m.then_inc(lg_done, 1)

            for b in range(NB):
                for w in (2 * b, 2 * b + 1):
                    if b >= 2:
                        out_project(w, 1)
                    out_project(w, 0)
                if b >= 1:
                    h2_turn(b - 1)
            route(0)
            route(1)
            h2_turn(NB - 1)
            route(2)
            route(3)
            pe.wait_ge(lg_ready, NB)
            pe.wait_ge(mask_ready, 1)
            for b in range(NB):
                for c in range(b + 1):
                    m = MM(bank(1, b * NE, NE), (before if c == b else ones)[:, :], mask[:, c, :],
                           start=c == 0, stop=c == b)
            for c in range(NB):
                m = MM(bank(1, NB * NE, NE), ones[:, :], mask[:, c, :], start=c == 0, stop=c == NB - 1)
            m.then_inc(rank_done, 1)

            def index(n, e):
                pe.wait_ge(hot_ready, n + 1)
                for b in range(NB):
                    m = MM(ps[0:CAP, 6, 0:2], onehot[:, b, :],
                           tokens[:, bass.ds(e, 1), b, :].rearrange("p a c -> p (a c)"), start=b == 0, stop=b == NB - 1)
                m.then_inc(idx_done, 1)

            def turn_rows(n, q, k_th):
                pe.wait_ge(row_in[q], k_th)
                for k in range(KD):
                    m = TR(bank(6 + k // 4, (k % 4 + 1) * CAP, CAP), hrow[:, q, k * P:(k + 1) * P], ident[0:CAP, 0:CAP])
                m.then_inc(hrT_done, 1)

            def weights(n, c):
                s = ORDER[c]
                pe.wait_ge(ring_in[2 * s], 16 * n + 16 * (FRONT_LOADS[s] + 1))

            def up(n, q, r):
                t, j = divmod(r, 4)
                c = 2 * (t // 2) + j // 2
                if r % 8 == 0:
                    weights(n, c)
                    if r == 0:
                        pe.wait_ge(htE_ready, n + 1)
                if r % 8 == 2:
                    weights(n, c)
                col = (2 * (t % 2) + j % 2) * P
                for k in range(KD):
                    m = MM(bank(t, j * CAP, CAP), pair(2 * ORDER[c])[:, k, col:col + P],
                           htE[:, q, k * CAP:(k + 1) * CAP], start=k == 0, stop=k == KD - 1)
                if j == 3:
                    m.then_inc(up_done, 1)
                elif r % 8 == 5:
                    m.then_inc(chunk_used, 1)

            def down(n):
                for j in range(2 * KD):
                    s, k = divmod(j, KD)
                    if s == 0 and k % 2 == 0:
                        pe.wait_ge(actlo_ready, 4 * n + (k // 2 + 1))
                    pe.wait_ge(wlo_ready, 2 * KD * n + (j + 1))
                    out, hi = ps[0:CAP, 4 + s, :], w_hi[:, j % SLICES, :]
                    MM(out, act_hi[:, k, :], hi, start=k == 0, stop=False)
                    MM(out, act_hi[:, k, :], w_lo[:, j % SLICES, :], start=False, stop=False)
                    MM(out, act_lo[:, k, :], hi, start=False, stop=k == KD - 1).then_inc(slice_used, 1)

            def expert(n, q, rows_next, first=False, last=False):
                for r in range(4):
                    up(n, q, r)
                if not last:
                    index(n + 1, n + 1)
                for r in range(4, 12):
                    up(n, q, r)
                if not last:
                    turn_rows(n + 1, 1 - q, rows_next)
                for r in range(12, 16):
                    up(n, q, r)
                if not first:
                    pe.wait_ge(y_ready, n)
                down(n)

            def gate_biases():
                for w in range(2 * NB):
                    if w >= 4:
                        pe.wait_ge(bias_added, w - 3)
                    MM(bank((6, 7, 2, 3)[w % 4]), gatesT[:, w // 2 * P:(w // 2 + 1) * P], b2_sb[:, w % 2 * W:(w % 2 + 1) * W],
                       start=True, stop=True).then_inc(bias_done, 1)

            index(0, 0)
            pe.wait_ge(gts_ready, 1)
            for b in range(NB):
                m = TR(ps[0:NE, 2, b * P:(b + 1) * P], gts[:, b, :], ident[:, :])
            m.then_inc(gT_done, 1)
            turn_rows(0, 0, 16)
            pe.wait_ge(gT_ready, 1)
            pe.wait_ge(b_in, 32)
            pe.wait_ge(htE_ready, 1)
            gate_biases()
            pe.wait_ge(bias_added, 2 * NB)
            expert(0, 0, 16, first=True)
            with pe.Fori(0, NE // 2 - 1) as i:
                expert(2 * i + 1, 1, 16 * i + 32)
                expert(2 * i + 2, 0, 16 * i + 32)
            expert(NE - 1, 1, None, last=True)

            def over_pass(n, e, at):
                index(n, e)
                turn_rows(n, 0, 16 * n + (16 - 16 * (NE // 2)))
                for r in range(16):
                    up(n, 0, r)
                pe.wait_ge(y_ready, n)
                down(n)

            further(pe, over_pass)


def kernel(x, positions, norm1_w, w_in, ret_log_decay_fwd, ret_log_decay_bwd, ret_norm_w,
           q_norm_w, k_norm_w, lambda_q1, lambda_k1, lambda_q2, lambda_k2, diff_norm_w,
           w_out, norm2_w, w_router, b_router, w1, b1, w2, b2):
    import concourse.bacc as bacc
    from concourse.bass_utils import run_bass_kernel_spmd as run

    def rows(a):
        return np.broadcast_to(np.asarray(a).reshape(1, -1), (P, np.asarray(a).size))

    ramp = np.arange(64, dtype=np.float32) * np.float32(1 / 63)
    inv_ret = (10000.0 ** (-ramp.astype(np.float64))).astype(np.float32)
    inv_diff = (500000.0 ** (-np.arange(0, ROT, 2) / ROT)).astype(np.float32)
    par = np.concatenate([
        np.asarray(norm1_w).reshape(KD, P).T, np.asarray(norm2_w).reshape(KD, P).T,
        np.asarray(ret_norm_w).reshape(HEADS, P).T, np.asarray(diff_norm_w).reshape(1, P).T,
        np.concatenate([inv_ret, inv_ret]).reshape(P, 1), rows(inv_diff),
        rows(ret_log_decay_fwd), rows(ret_log_decay_bwd), rows(q_norm_w), rows(k_norm_w),
        rows(lambda_q1), rows(lambda_k1), rows(lambda_q2), rows(lambda_k2), rows(b_router)], axis=1)
    pos = np.concatenate([rows(positions), np.asarray(positions).reshape(NB, P).T], axis=1)
    b1t = np.asarray(b1).reshape(NE, 2, 4, 2, P).transpose(4, 0, 2, 1, 3).reshape(P, NE * 16)
    arrays = {"x": x, "w_in": w_in, "w_out": w_out, "w_router": w_router, "w1": w1, "w2": w2, "b1t": b1t, "b2": b2,
              "par": par, "pos": pos}
    arrays = {n: np.ascontiguousarray(a) for n, a in arrays.items()}
    nc = bacc.Bacc("TRN2", target_bir_lowering=False, num_devices=1, dynamic_dma_scratch_size=4096)
    aps = {n: nc.dram_tensor(f"in_{n}", a.shape, mybir.dt.from_np(a.dtype), kind="ExternalInput").ap()
           for n, a in arrays.items()}
    out = nc.dram_tensor("out", (1, T, D), mybir.dt.float32, kind="ExternalOutput").ap()
    h2_rows = nc.dram_tensor("h2_rows", (T, D), mybir.dt.float32, kind="Internal").ap()
    y_rows = nc.dram_tensor("y_rows", (ASSIGNED + CAP, D), mybir.dt.float32, kind="Internal").ap()
    build_layer(nc, out=out, h2_rows=h2_rows, y_rows=y_rows, **aps)
    r = run(nc, [{f"in_{n}": a for n, a in arrays.items()}], core_ids=[0])
    return r.results[0]["out"]
```

```python
from contextlib import ExitStack

import concourse.bass as bass
from concourse import mybir
import numpy as np

P = 128
D = 1024
T = 512
NB = T // P
KD = D // P
HEADS = 4
DV = 128
DH = 64
ROT = DH // 4
NF8 = ROT // 2
NE = 32
TOPK = 4
W = 512
EPS = 1e-6
LIMIT = 7.0
ALPHA = 1.702
LAMBDA_INIT = 0.2
RING = 12
SLOT = 2048
CAP = 96
MAX_CHUNK = -(-T // CAP)
MAX_OVER = 24
CHUNKS = 6
W1_COLS = [0, D, W, D + W]
ORDER = [0, 3, 5, 4, 1, 2]
FRONT_LOADS = [2, 3, 3, 0, 0, 0]
SLICES = 4
DIST = 896

PK = {}
_at = 0
for _n, _w in (("n1w", KD), ("n2w", KD), ("retw", HEADS), ("diffw", 1), ("invcol", 1), ("inv8", NF8), ("ldf", HEADS),
               ("ldb", HEADS), ("qw", DH), ("kw", DH), ("lam", 4 * DH), ("brt", NE)):
    PK[_n] = (_at, _at + _w)
    _at += _w
NPAR = _at

GROUPS = [("Qd", 2048), ("Kd", 2560), ("Vd", 3072), ("Vr", 1024), ("G", 1536), ("Qr", 0), ("Kr", 512)]

TWO_PI = 2 * np.pi
C1 = 6.28125
C2 = float(np.float32(np.round((TWO_PI - C1) * 2**17) / 2**17))
C3 = float(np.float32(TWO_PI - C1 - C2))
MAGIC = 1.5 * 2.0**23
PI_LOW = 3.1415925


def build_layer(nc, x, w_in, w_out, w_router, w1, b1t, w2, b2, par, pos, h2_rows, sums, out):
    f32, i32, u32 = mybir.dt.float32, mybir.dt.int32, mybir.dt.uint32
    f32r, bf16 = mybir.dt.float32r, mybir.dt.bfloat16
    ALU, ACT, AX = mybir.AluOpType, mybir.ActivationFunctionType, mybir.AxisListType

    ctx = ExitStack()
    with ctx:
        def sb(name, shape, dt=f32):
            return ctx.enter_context(nc.sbuf_tensor(name, shape, dt))

        def sem(name):
            return ctx.enter_context(nc.semaphore(name))

        ring = sb("ring", [P, RING, SLOT])
        X = sb("X", [P, NB, D])
        HT = sb("HT", [P, KD * T])
        hT = HT[:, :].rearrange("p (k t) -> p k t", k=KD)
        h2 = HT[:, :].rearrange("p (b d) -> p b d", b=NB)
        par_sb = sb("par_sb", [P, NPAR])
        ident = sb("ident", [P, P])
        before = sb("before", [P, P], bf16)
        ones = sb("ones", [P, P], bf16)
        mask = sb("mask", [P, NB, NE], bf16)
        iota_s = sb("iota_s", [P, P])
        small = sb("small", [P, 592])
        small_used = [0]

        def tiny(*shape):
            n = int(np.prod(shape))
            a = small[:, small_used[0]:small_used[0] + n]
            small_used[0] += n
            if len(shape) == 2:
                a = a.rearrange("p (a b) -> p a b", a=shape[0])
            if len(shape) == 3:
                a = a.rearrange("p (a b c) -> p a b c", a=shape[0], b=shape[1])
            return a

        ssx, msx, rsx = tiny(2 * NB), tiny(2 * NB), tiny(2 * NB)
        ssq, msq, rsq = tiny(2, 32), tiny(2, 32), tiny(2, 32)
        negmax, rowsum, rowinv, lamc = tiny(32), tiny(32), tiny(32), tiny(16)
        sso, mso, rso = tiny(2, 16), tiny(2, 16), tiny(2, 16)
        lamt, lam2, neglam, dw = tiny(2), tiny(2), tiny(1), tiny(1)
        top8, topf, ev, gate4, esum = tiny(NB, 8), tiny(NB, 8), tiny(NB, TOPK), tiny(NB, TOPK), tiny(NB)
        idx8 = sb("idx8", [P, NB, 8], u32)
        gate_at = tiny(2)
        place_id, vacant = tiny(1), tiny(1)
        over_top = tiny(MAX_OVER)
        over_n = tiny(1)
        over_some = tiny(MAX_OVER)
        over_at = sb("over_at", [P, MAX_OVER + 1], i32)
        over_e = sb("over_e", [P, MAX_OVER], i32)
        place_idx, place_row = sb("place_idx", [P, 2], u32), sb("place_row", [P, 2], u32)

        arena = sb("arena", [P, 15872])

        def cut(at, n, *split):
            a = arena[:, at:at + n]
            if len(split) == 2:
                return a.rearrange("p (a b) -> p a b", a=split[0])
            if len(split) == 3:
                return a.rearrange("p (a b c) -> p a b c", a=split[0], b=split[1])
            return a

        def slots(s, n, parts):
            return ring[:, s:s + n, :].rearrange("p s c -> p (s c)").rearrange("p (a b) -> p a b", a=parts)

        NANG = T + NB * NF8
        rq, rk = cut(0, 2048, NB, W), cut(2048, 2048, NB, W)
        qrT, krT = cut(0, 2048, HEADS, T), cut(2048, 2048, HEADS, T)
        decay = cut(4096, HEADS * DIST, HEADS, DIST)
        h2T = cut(4096, 2048, 2, D)
        cosT, sinT = cut(7680, W), cut(8192, W)
        xs = cut(8704, 2048, 2, D)
        prob = cut(8704, 2048, 4, W)
        yrow = cut(8704, 2048, NB, W)
        ang, turns, red = cut(10752, NANG), cut(10752 + NANG, NANG), cut(10752 + 2 * NANG, 2 * NANG, 2, NANG)
        dist = cut(10752 + 4 * NANG, DIST)
        dtmp = cut(10752 + 4 * NANG + DIST, DIST)
        pos_sb = cut(4096, T + NB).bitcast(i32)
        ropet = cut(10752, 1024, 4, NB * 8 * NF8)
        amix = cut(10752, 1024, 2, W)
        std = cut(10752, 1024, 2, W)
        aT = cut(11776, 1024, 2, W)
        qsb = cut(12800, 1024, 2, W)
        roped = cut(13824, 1024, 2, W)
        sig = cut(12800, 2048)
        sqs = cut(14848, 1024)
        cs_row = sb("cs_row", [P, 2, NB * NF8])
        orow = slots(6, 1, NB)
        qdT = slots(7, 1, HEADS)
        kdT = slots(8, 1, HEADS)
        vd = slots(9, 1, NB)
        mixT = slots(8, 2, KD)
        vr = slots(10, 1, NB)
        gg = slots(11, 1, NB)
        posm = cut(0, MAX_CHUNK * NE * NB, MAX_CHUNK, NE, NB)
        b1_sb = cut(768, NE * 16, NE, 16)
        gatesT = arena[:, 1280:1280 + T]
        logits, rank = cut(1792, NB * NE, NB, NE), cut(1920, NB * NE, NB, NE)
        gts = cut(2176, NB * NE, NB, NE)
        over_key = cut(2816, (MAX_CHUNK - 1) * NE, MAX_CHUNK - 1, NE)
        ub, sg = cut(2304, 8 * CAP, 2, 4 * CAP), cut(3072, 4 * CAP, 2, 2 * CAP)
        actT = cut(3456, KD * CAP, KD, CAP)
        b2_sb = arena[:, 6144:6144 + D]
        wr_sb = cut(7168, KD * NE, KD, NE)
        htE = cut(7168, 2 * KD * CAP, 2, KD * CAP)
        onehot = cut(8704, NB * CAP, NB, CAP)
        tokens = arena[:, 10112:10112 + NE * NB * 3].rearrange("p (e b c) -> p e b c", e=NE, b=NB)
        chose = cut(2304, TOPK * NB * NE, TOPK, NB * NE)
        gated = cut(2816, TOPK * NB * NE, TOPK, NB * NE)
        yrows = arena[0:CAP, 9088:9088 + D]
        hrow = HT[0:CAP, 0:2 * D].rearrange("p (q d) -> p q d", q=2)
        act_hi, act_lo = sb("act_hi", [P, KD, CAP], f32r), sb("act_lo", [P, KD, CAP], f32r)
        w_hi, w_lo = sb("w_hi", [P, SLICES, W], f32r), sb("w_lo", [P, SLICES, W], f32r)
        ps = ctx.enter_context(nc.psum_tensor("ps", [P, 8, W], f32))

        x_in = [sem(f"x_in{b}") for b in range(NB)]
        par_in, pos_in, wr_in, b_in = sem("par_in"), sem("pos_in"), sem("wr_in"), sem("b_in")
        first_in = [sem(f"first_in{i}") for i in range(KD // 2)]
        ring_in = [sem(f"ring_in{s}") for s in range(RING)]
        consts, filled = sem("consts"), sem("filled")
        dve_chain = sem("dve_chain")
        sq_x, ms_x, sd_x, rs_x, xs_ready, xT_done, hT_ready = (sem(n) for n in (
            "sq_x", "ms_x", "sd_x", "rs_x", "xs_ready", "xT_done", "hT_ready"))
        red_ready, trig_ready, dexp_in, dexp_ready, lam_in, lam_exp = (sem(n) for n in (
            "red_ready", "trig_ready", "dexp_in", "dexp_ready", "lam_in", "lam_exp"))
        proj_done, proj_evac, sq_used, ms_q, sd_q, qk_ready = (sem(n) for n in (
            "proj_done", "proj_evac", "sq_used", "ms_q", "sd_q", "qk_ready"))
        qkT_done, qkT_evac, rope_done = (sem(n) for n in ("qkT_done", "qkT_evac", "rope_done"))
        sc_done, max_ready, exp_done, comb_done, aT_done, aT_evac, av_done, o_evac, o_sq = (sem(n) for n in (
            "sc_done", "max_ready", "exp_done", "comb_done", "aT_done", "aT_evac", "av_done", "o_evac", "o_sq"))
        ms_o, sd_o, o_ready, mixT_done, mixT_ready = (sem(n) for n in ("ms_o", "sd_o", "o_ready", "mixT_done", "mixT_ready"))
        sig_g, st_done, std_ready, yv_done, y_evac, y_sq = (sem(n) for n in (
            "sig_g", "st_done", "std_ready", "yv_done", "y_evac", "y_sq"))
        op_done, res_ready, h2_ready, h2T_done, h2T_ready, lg_done, lg_ready = (sem(n) for n in (
            "op_done", "res_ready", "h2_ready", "h2T_done", "h2T_ready", "lg_done", "lg_ready"))
        ev_in, ev_ready, mask_ready, rank_done, h2_stored = (sem(n) for n in (
            "ev_in", "ev_ready", "mask_ready", "rank_done", "h2_stored"))
        over_ready = sem("over_ready")
        fetches = sem("fetches")
        y_stored = [sem(f"y_stored{q}") for q in range(2)]
        gts_ready, gT_done, gT_ready, bias_done, bias_added = (sem(n) for n in (
            "gts_ready", "gT_done", "gT_ready", "bias_done", "bias_added"))
        pads = sem("pads")
        all_stored, vacant_ready = sem("all_stored"), sem("vacant_ready")
        sums_begun, table_ready = sem("sums_begun"), sem("table_ready")
        row_in = [sem(f"row_in{q}") for q in range(2)]
        (hot_ready, idx_done, idx_ready, hrT_done, htE_ready, up_done, ub_ready, glu_ready, lin_ready, gl_ready,
         sg_ready, act_ready, acthi_ready, actlo_ready, whi_ready, wlo_ready, slice_used, chunk_used, y_ready, out_done) = (sem(n) for n in (
             "hot_ready", "idx_done", "idx_ready", "hrT_done", "htE_ready", "up_done", "ub_ready", "glu_ready",
             "lin_ready", "gl_ready", "sg_ready", "act_ready", "acthi_ready", "actlo_ready", "whi_ready", "wlo_ready",
             "slice_used", "chunk_used", "y_ready", "out_done"))

        def pcols(name):
            a, b = PK[name]
            return par_sb[:, a:b]

        def bank(b, a=0, n=W):
            return ps[:, b, a:a + n]

        def wide(b):
            return ps[:, b:b + 2, :]

        def spread(ap, n):
            return ap.unsqueeze(len(ap.shape)).to_broadcast(list(ap.shape) + [n])

        x_v = x.rearrange("a (b p) d -> (a b) p d", p=P)
        out_v = out.rearrange("a (b p) d -> (a b) p d", p=P)
        w_in_v = w_in.rearrange("a (k p) n -> p (a k) n", p=P)
        w_out_v = w_out.rearrange("a (k p) n -> p (a k) n", p=P)
        w1_v = w1.rearrange("a e (k p) n -> (a e) p k n", p=P)
        w2_v = w2.rearrange("a e (k p) n -> (a e) p k n", p=P)
        h2_v = h2_rows.rearrange("(b p) d -> b p d", p=P)

        def pair(s):
            return ring[:, s:s + 2, :].rearrange("p s (k n) -> p (s k) n", n=W)

        def over_count(eng):
            return eng.value_load(over_at[0:1, MAX_OVER:MAX_OVER + 1], min_val=0, max_val=MAX_OVER)

        def further(eng, one_pass):
            eng.wait_ge(over_ready, 1)
            n_over = over_count(eng)
            with eng.If(n_over > 0):
                with eng.Fori(0, n_over) as j:
                    at = eng.value_load(over_at[0:1, bass.ds(j, 1)], min_val=0, max_val=MAX_CHUNK * NE - 1)
                    e = eng.value_load(over_e[0:1, bass.ds(j, 1)], min_val=0, max_val=NE - 1)
                    one_pass(j + NE, e, at)

        block = ctx.enter_context(nc.Block())

        @block.sync
        def _(sp):
            for b in range(NB):
                sp.dma_start(X[:, b, :], x_v[b]).then_inc(x_in[b], 16)
            for g, (_, c) in enumerate(GROUPS):
                if g >= 3:
                    sp.wait_ge(proj_done, 4 * (g - 2))
                if g == 0:
                    for i in range(KD // 2):
                        sp.dma_start(pair(0)[:, 2 * i:2 * i + 2, :], w_in_v[:, 2 * i:2 * i + 2, c:c + W]
                                     ).then_inc(first_in[i], 16)
                else:
                    sp.dma_start(pair(2 * (g % 3)), w_in_v[:, :, c:c + W]).then_inc(ring_in[2 * (g % 3)], 16)
            for n in range(2):
                sp.wait_ge(proj_done, 4 * (5 + n))
                sp.dma_start(pair(2 + 2 * n), w_out_v[:, :, n * W:(n + 1) * W]).then_inc(ring_in[2 + 2 * n], 16)

            def load(e, c):
                if c < 4:
                    src = w1_v[bass.ds(e, 1), :, :, W1_COLS[c]:W1_COLS[c] + W]
                else:
                    src = w2_v[bass.ds(e, 1), :, :, (c - 4) * W:(c - 3) * W]
                sp.dma_start(pair(2 * ORDER[c]), src.rearrange("a p k n -> p (a k) n")).then_inc(ring_in[2 * ORDER[c]], 16)

            for c in range(CHUNKS):
                s = ORDER[c]
                if c == 0:
                    sp.wait_ge(proj_done, 4 * 7)
                if s == 3:
                    sp.wait_ge(mixT_done, NB)
                    sp.wait_ge(sc_done, 2 * NB * HEADS)
                if s == 4:
                    sp.wait_ge(op_done, 2 * NB)
                    sp.wait_ge(h2_stored, 16 * NB)
                if s == 5:
                    sp.wait_ge(yv_done, NB * HEADS)
                    sp.wait_ge(o_ready, 2)
                if s == 1:
                    sp.wait_ge(op_done, 2 * NB)
                    sp.wait_ge(row_in[0], 16)
                load(0, c)

            for b in range(NB):
                sp.wait_ge(bias_added, 2 * (b + 1))
                sp.dma_start(sums[b * P:(b + 1) * P, :], X[:, b, :]).then_inc(sums_begun, 16)
            sp.dma_start(sums[T:T + CAP, :], X[0:CAP, 0, :]).then_inc(sums_begun, 16)

            def weights(n, e):
                for c in range(CHUNKS):
                    if c in (0, 2):
                        sp.wait_ge(chunk_used, 2 * n + (c // 2 - 1))
                    elif c < 4:
                        sp.wait_ge(up_done, 4 * n + (c - 3))
                    else:
                        sp.wait_ge(wlo_ready, 2 * KD * n + KD * (c - 5))
                    load(e, c)

            with sp.Fori(1, NE) as n:
                weights(n, n)
            further(sp, lambda n, e, at: weights(n, e))
            sp.wait_ge(all_stored, 1)
            for b in range(NB):
                sp.dma_start(out_v[b], sums[b * P:(b + 1) * P, :]).then_inc(out_done, 16)
            sp.wait_ge(out_done, 16 * NB)

        @block.gpsimd
        def _(pool):
            nc.gpsimd.memset(ident[:, :], 0.0).then_inc(filled, 1)
            nc.gpsimd.memset(before[:, :], 1.0).then_inc(filled, 1)
            nc.gpsimd.memset(ones[:, :], 1.0).then_inc(filled, 1)
            pool.wait_ge(filled, 3)
            nc.gpsimd.affine_select(out=ident[:, :], in_=ident[:, :], compare_op=ALU.not_equal, fill=1.0, base=0,
                                    pattern=[[-1, P]], channel_multiplier=1).then_inc(consts, 1)
            nc.gpsimd.affine_select(out=before[:, :], in_=before[:, :], compare_op=ALU.is_gt, fill=0.0, base=0,
                                    pattern=[[1, P]], channel_multiplier=-1).then_inc(consts, 1)
            nc.gpsimd.iota(iota_s[:, :], pattern=[[1, P]], base=0, channel_multiplier=0,
                           allow_small_or_imprecise_dtypes=True).then_inc(consts, 1)
            nc.gpsimd.iota(dist, pattern=[[1, DIST]], base=-(T - P), channel_multiplier=-1,
                           allow_small_or_imprecise_dtypes=True).then_inc(consts, 1)
            nc.gpsimd.iota(place_id, pattern=[[0, 1]], base=0, channel_multiplier=1,
                           allow_small_or_imprecise_dtypes=True).then_inc(consts, 1)
            pool.wait_ge(yv_done, NB * HEADS)
            pool.wait_ge(consts, 5)
            nc.gpsimd.memset(gatesT, 0.0).then_inc(pads, 1)
            pool.wait_ge(pads, 1)
            nc.gpsimd.memset(b2_sb, 0.0).then_inc(pads, 1)
            pool.wait_ge(pads, 2)
            pool.wait_ge(mixT_done, 2 * NB)
            nc.gpsimd.iota(tokens[:, :, :, 1], pattern=[[0, NE], [P, NB]], base=-T, channel_multiplier=1,
                           allow_small_or_imprecise_dtypes=True).then_inc(consts, 1)
            pool.wait_ge(consts, 6)
            nc.gpsimd.iota(tokens[:, :, :, 0], pattern=[[0, NE], [P, NB]], base=0, channel_multiplier=1,
                           allow_small_or_imprecise_dtypes=True).then_inc(consts, 1)

            def fetch(n, q):
                pool.wait_ge(idx_ready, n + 1)
                pool.sem_inc(fetches, 1)
                nc.gpsimd.indirect_dma_start(hrow[:, q, :], None, h2_rows,
                                             bass.IndirectOffsetOnAxis(ap=place_idx[0:CAP, q:q + 1], axis=0)
                                             ).then_inc(row_in[q], 16)

            def put(n, q):
                pool.wait_ge(y_ready, n + 1)
                pool.sem_inc(fetches, 1)
                nc.gpsimd.indirect_dma_start(sums, bass.IndirectOffsetOnAxis(ap=place_row[0:CAP, q:q + 1], axis=0),
                                             yrows, None, compute_op=ALU.add).then_inc(y_stored[q], 16)

            pool.wait_ge(h2_stored, 16 * NB)
            fetch(0, 0)
            fetch(1, 1)
            pool.wait_ge(sums_begun, 16 * (NB + 1))
            with pool.Fori(0, NE // 2 - 1) as i:
                put(2 * i, 0)
                fetch(2 * i + 2, 0)
                put(2 * i + 1, 1)
                fetch(2 * i + 3, 1)
            put(NE - 2, 0)
            put(NE - 1, 1)

            def over_pass(n, e, at):
                fetch(n, 0)
                put(n, 0)

            further(pool, over_pass)
            n_over = over_count(pool)
            pool.wait_ge(y_stored[0], 16 * n_over + 8 * NE)
            pool.wait_ge(y_stored[1], 8 * NE)
            pool.sem_inc(all_stored, 1)

        @block.scalar
        def _(act):
            act.dma_start(par_sb[:, :], par).then_inc(par_in, 16)
            act.dma_start(pos_sb, pos).then_inc(pos_in, 16)
            for b in range(NB):
                act.wait_ge(x_in[b], 16)
                nc.scalar.activation(sqs, X[:, b, :], ACT.Square, accum_out=ssx[:, b:b + 1]).then_inc(sq_x, 1)
                act.wait_ge(sq_x, b + 1)
                act.wait_ge(ms_x, b + 1)
                nc.scalar.activation(msx[:, b:b + 1], msx[:, b:b + 1], ACT.Sqrt).then_inc(sd_x, 1)
                act.wait_ge(rs_x, b + 1)
                if b >= 2:
                    act.wait_ge(xT_done, b - 1)
                nc.scalar.activation(xs[:, b % 2, :], X[:, b, :], ACT.Copy, scale=rsx[:, b:b + 1]).then_inc(xs_ready, 1)

            def evac(j):
                g, i = divmod(j, 4)
                name = GROUPS[g][0]
                act.wait_ge(proj_done, j + 1)
                src = bank(j % 2)
                if name in ("Qd", "Kd"):
                    if j >= 2:
                        act.wait_ge(sq_used, j - 1)
                    nc.scalar.activation((rq if name == "Qd" else rk)[:, i, :], src, ACT.Copy)
                    nc.scalar.activation(sqs[:, (j % 2) * W:(j % 2 + 1) * W], src, ACT.Square).then_inc(proj_evac, 1)
                elif name in ("Qr", "Kr"):
                    r = j - 20
                    if r >= 2:
                        act.wait_ge(rope_done, r - 1)
                    nc.scalar.activation(qsb[:, j % 2, :], src, ACT.Copy,
                                         scale=1.0 if name == "Qr" else P ** -0.5).then_inc(proj_evac, 1)
                else:
                    dst = {"Vd": vd, "Vr": vr, "G": gg}[name]
                    nc.scalar.activation(dst[:, i, :], src, ACT.Copy).then_inc(proj_evac, 1)

            evac(0)
            act.wait_ge(red_ready, 1)
            nc.scalar.activation(sinT, red[:, 0, 0:T], ACT.Sin)
            nc.scalar.activation(cosT, red[:, 1, 0:T], ACT.Sin)
            nc.scalar.activation(cs_row[:, :, :], red[:, :, T:NANG], ACT.Sin).then_inc(trig_ready, 1)
            for j in range(1, 8):
                evac(j)
            act.wait_ge(ms_q, 1)
            nc.scalar.activation(msq[:, 0, :], msq[:, 0, :], ACT.Sqrt).then_inc(sd_q, 1)
            act.wait_ge(ms_q, 2)
            nc.scalar.activation(msq[:, 1, :], msq[:, 1, :], ACT.Sqrt).then_inc(sd_q, 1)
            for j in range(8, 12):
                evac(j)
            for g, dst in enumerate((qdT, kdT)):
                for i in range(NB):
                    act.wait_ge(qkT_done, 4 * g + i + 1)
                    nc.scalar.activation(dst[:, :, i * P:(i + 1) * P],
                                         bank(3 + i).rearrange("p (h t) -> p h t", h=HEADS), ACT.Copy,
                                         scale=DH ** -0.5 if g == 0 else 1.0).then_inc(qkT_evac, 1)

            act.wait_ge(lam_in, 1)
            nc.scalar.activation(lam2, lamt, ACT.Exp).then_inc(lam_exp, 1)

            def a_out(u):
                act.wait_ge(aT_done, u + 1)
                if u >= 2:
                    act.wait_ge(av_done, u - 1)
                nc.scalar.activation(aT[:, u % 2, :], bank(7), ACT.Copy).then_inc(aT_evac, 1)

            def o_out(i):
                act.wait_ge(av_done, HEADS * (i + 1))
                nc.scalar.activation(orow[:, i, :], bank(2), ACT.Copy)
                if i >= 1:
                    act.wait_ge(o_sq, i)
                nc.scalar.activation(sqs[:, 0:W], bank(2), ACT.Square).then_inc(o_evac, 1)

            for u in range(NB * HEADS):
                for s in range(2):
                    k = 2 * u + s
                    act.wait_ge(max_ready, k + 1)
                    if u >= 2:
                        act.wait_ge(comb_done, u - 1)
                    nc.scalar.activation(prob[:, 2 * (u % 2) + s, :], bank(3 + 2 * (u % 2) + s), ACT.Exp,
                                         bias=negmax[:, k:k + 1], accum_out=rowsum[:, k:k + 1]).then_inc(exp_done, 1)
                evac(12 + u)
                if u >= 1:
                    a_out(u - 1)
                if u >= 5 and u % 4 == 1:
                    o_out(u // 4 - 1)
                if 1 <= u <= HEADS:
                    act.wait_ge(dexp_in, u)
                    nc.scalar.activation(decay[:, u - 1, :], decay[:, u - 1, :], ACT.Exp).then_inc(dexp_ready, 1)
            a_out(15)
            o_out(3)
            act.wait_ge(rope_done, 8)
            nc.scalar.activation(sig, gg, ACT.Sigmoid).then_inc(sig_g, 1)
            act.wait_ge(ms_o, 1)
            nc.scalar.activation(mso[:, 0, :], mso[:, 0, :], ACT.Sqrt).then_inc(sd_o, 1)
            for i in range(NB):
                act.wait_ge(yv_done, NB * HEADS)
                if i == 0:
                    act.wait_ge(comb_done, NB * HEADS)
                nc.scalar.activation(yrow[:, i, :], bank(2 + i), ACT.Copy)
                if i >= 2:
                    act.wait_ge(y_sq, i - 1)
                nc.scalar.activation(sqs[:, (i % 2) * W:(i % 2 + 1) * W], bank(2 + i), ACT.Square).then_inc(y_evac, 1)
            act.wait_ge(ms_o, 2)
            nc.scalar.activation(mso[:, 1, :], mso[:, 1, :], ACT.Sqrt).then_inc(sd_o, 1)
            act.dma_start(b1_sb, b1t.rearrange("p (e n) -> p e n", e=NE)).then_inc(b_in, 16)
            act.dma_start(wr_sb, w_router.rearrange("a (k p) e -> p (a k) e", p=P)).then_inc(wr_in, 16)
            act.wait_ge(pads, 2)
            act.dma_start(b2_sb[0:NE], b2.rearrange("a e d -> (a e) d")).then_inc(b_in, 16)
            for b in range(NB):
                act.wait_ge(res_ready, 2 * (b + 1))
                nc.scalar.activation(sqs, X[:, b, :], ACT.Square, accum_out=ssx[:, NB + b:NB + b + 1]).then_inc(sq_x, 1)
                act.wait_ge(sq_x, NB + b + 1)
                act.wait_ge(ms_x, NB + b + 1)
                nc.scalar.activation(msx[:, NB + b:NB + b + 1], msx[:, NB + b:NB + b + 1], ACT.Sqrt).then_inc(sd_x, 1)
                act.wait_ge(rs_x, NB + b + 1)
                nc.scalar.activation(h2[:, b, :], X[:, b, :], ACT.Copy, scale=rsx[:, NB + b:NB + b + 1]).then_inc(h2_ready, 1)
                act.wait_ge(h2_ready, b + 1)
                act.dma_start(h2_v[b], h2[:, b, :]).then_inc(h2_stored, 16)
            act.wait_ge(ev_in, 1)
            nc.scalar.activation(ev, ev, ACT.Exp).then_inc(ev_ready, 1)

            def gate_sigmoid(n, t):
                act.wait_ge(glu_ready, 4 * n + (t + 1))
                nc.scalar.activation(sg[:, t % 2, :], ub[:, t % 2, 0:2 * CAP], ACT.Sigmoid, scale=ALPHA).then_inc(sg_ready, 1)

            def y_out(n, q, q_before, before):
                act.wait_ge(slice_used, 2 * KD * (n + 1))
                if before is not None:
                    act.wait_ge(y_stored[q_before], before)
                nc.scalar.activation(yrows, ps[0:CAP, 4:6, :], ACT.Copy, scale=gate_at[0:CAP, q:q + 1]
                                     ).then_inc(y_ready, 1)

            def act_high(n, t):
                act.wait_ge(act_ready, 4 * n + (t + 1))
                nc.scalar.activation(act_hi[:, 2 * t:2 * t + 2, :], actT[:, 2 * t:2 * t + 2, :], ACT.Copy
                                     ).then_inc(acthi_ready, 1)

            def w_high(n, j, first=False):
                s, k = divmod(j, KD)
                if k == 0:
                    act.wait_ge(ring_in[2 * ORDER[4 + s]], 16 * n + 16 * (FRONT_LOADS[ORDER[4 + s]] + 1))
                if j >= SLICES or not first:
                    act.wait_ge(slice_used, 2 * KD * n + (j + 1 - SLICES))
                nc.scalar.activation(w_hi[:, j % SLICES, :], pair(2 * ORDER[4 + s])[:, k, :], ACT.Copy).then_inc(whi_ready, 1)

            def one_pass(n, first=False):
                for t in range(3):
                    gate_sigmoid(n, t)
                    if t:
                        act_high(n, t - 1)
                for j in range(SLICES):
                    w_high(n, j, first)
                act_high(n, 2)
                w_high(n, SLICES)
                gate_sigmoid(n, 3)
                w_high(n, SLICES + 1)
                w_high(n, SLICES + 2)
                act_high(n, 3)
                for j in range(SLICES + 3, 2 * KD):
                    w_high(n, j)

            def over_pass(n, e, at):
                one_pass(n)
                act.wait_ge(y_stored[1], 8 * NE)
                y_out(n, 0, 0, 16 * n - 8 * NE)

            act.wait_ge(gT_done, 1)
            nc.scalar.activation(gatesT[0:NE], ps[0:NE, 2, :], ACT.Copy).then_inc(gT_ready, 1)
            one_pass(0, first=True)
            y_out(0, 0, 1, None)
            with act.Fori(0, NE // 2 - 1) as i:
                one_pass(2 * i + 1)
                y_out(2 * i + 1, 1, 0, 16 * i + 16)
                one_pass(2 * i + 2)
                y_out(2 * i + 2, 0, 1, 16 * i + 16)
            one_pass(NE - 1)
            y_out(NE - 1, 1, 0, 8 * NE)
            further(act, over_pass)

        @block.vector
        def _(v):
            links = [0]

            def link(ins):
                links[0] += 1
                ins.then_inc(dve_chain, 1)
                v.wait_ge(dve_chain, links[0])

            TS, TT, STT = nc.vector.tensor_scalar, nc.vector.tensor_tensor, nc.vector.scalar_tensor_tensor

            def norm_x(b, k):
                v.wait_ge(sq_x, k + 1)
                TS(msx[:, k:k + 1], ssx[:, k:k + 1], 1.0 / D, EPS, ALU.mult, ALU.add).then_inc(ms_x, 1)
                v.wait_ge(sd_x, k + 1)
                nc.vector.reciprocal(rsx[:, k:k + 1], msx[:, k:k + 1]).then_inc(rs_x, 1)

            def norm_T(b):
                v.wait_ge(xT_done, b + 1)
                if b == 0:
                    v.wait_ge(par_in, 16)
                TT(hT[:, :, b * P:(b + 1) * P], wide(2 * b).rearrange("p s (k t) -> p (s k) t", t=P),
                   spread(pcols("n1w"), P), ALU.mult).then_inc(hT_ready, 1)

            for b in range(NB):
                norm_x(b, b)
                if b >= 1:
                    norm_T(b - 1)
            v.wait_ge(pos_in, 16)
            v.wait_ge(consts, 4)
            link(nc.vector.tensor_copy(ang[:, 0:T], pos_sb[:, 0:T]))
            link(nc.vector.tensor_copy(esum, pos_sb[:, T:T + NB]))
            link(TS(ang[:, 0:T], ang[:, 0:T], pcols("invcol"), None, ALU.mult))
            for b in range(NB):
                link(TS(ang[:, T + b * NF8:T + (b + 1) * NF8], pcols("inv8"), esum[:, b:b + 1], None, ALU.mult))
            for s, shift in enumerate((0.0, 0.25)):
                r = red[:, s, :]
                link(TS(turns, ang, 1.0 / TWO_PI, shift, ALU.mult, ALU.add))
                link(TS(turns, turns, MAGIC, MAGIC, ALU.add, ALU.subtract))
                link(STT(r, turns, -C1, ang, ALU.mult, ALU.add))
                link(STT(r, turns, -C2, r, ALU.mult, ALU.add))
                link(STT(r, turns, -C3, r, ALU.mult, ALU.add))
                if s:
                    link(TS(r, r, float(np.pi / 2), None, ALU.add))
                ins = TS(r, r, PI_LOW, -PI_LOW, ALU.min, ALU.max)
                if s:
                    ins.then_inc(red_ready, 1)
                else:
                    link(ins)
                    norm_T(NB - 1)
            lam = pcols("lam").rearrange("p (a b c) -> p a b c", a=2, b=2)
            prod = turns[:, 0:2 * DH].rearrange("p (a c) -> p a c", a=2)
            link(TT(prod, lam[:, :, 0, :], lam[:, :, 1, :], ALU.mult))
            nc.vector.reduce_sum(lamt, prod, AX.X).then_inc(lam_in, 1)
            def qk_sums(g):
                for i in range(NB):
                    j = 4 * g + i
                    v.wait_ge(proj_evac, j + 1)
                    nc.vector.reduce_sum(ssq[:, g, 8 * i:8 * i + 8],
                                         sqs[:, (j % 2) * W:(j % 2 + 1) * W].rearrange("p (a c) -> p a c", a=8),
                                         AX.X).then_inc(sq_used, 1)
                v.wait_ge(sq_used, 4 * g + 4)
                TS(msq[:, g, :], ssq[:, g, :], 1.0 / DH, EPS, ALU.mult, ALU.add).then_inc(ms_q, 1)

            def qk_rest(g):
                r, w = (rq, pcols("qw")) if g == 0 else (rk, pcols("kw"))
                v.wait_ge(sd_q, g + 1)
                link(nc.vector.reciprocal(rsq[:, g, :], msq[:, g, :]))
                for i in range(NB):
                    cell = r[:, i, :].rearrange("p (a c) -> p a c", a=8)
                    link(TT(cell, cell, spread(rsq[:, g, 8 * i:8 * i + 8], DH), ALU.mult))
                    link(TT(cell, cell, w.unsqueeze(1).to_broadcast([P, 8, DH]), ALU.mult))
                cells = r.rearrange("p b (a c) -> p b a c", a=8)
                x1, x2 = cells[:, :, :, 0:NF8], cells[:, :, :, NF8:ROT]
                s, c = (cs_row[:, k, :].rearrange("p (b f) -> p b f", b=NB).unsqueeze(2).to_broadcast([P, NB, 8, NF8])
                        for k in range(2))
                t = [ropet[:, k, :].rearrange("p (b a f) -> p b a f", b=NB, a=8) for k in range(4)]
                if g == 0:
                    v.wait_ge(trig_ready, 1)
                link(TT(t[0], x1, c, ALU.mult))
                link(TT(t[1], x2, s, ALU.mult))
                link(TT(t[2], x2, c, ALU.mult))
                link(TT(t[3], x1, s, ALU.mult))
                link(TT(x1, t[0], t[1], ALU.subtract))
                TT(x2, t[2], t[3], ALU.add).then_inc(qk_ready, 1)
                v.wait_ge(qk_ready, g + 1)

            qk_sums(0)
            qk_sums(1)
            qk_rest(0)
            qk_rest(1)
            v.wait_ge(lam_exp, 1)
            link(TT(neglam, lam2[:, 1:2], lam2[:, 0:1], ALU.subtract))
            link(TS(neglam, neglam, LAMBDA_INIT, None, ALU.subtract))
            link(TS(dw, pcols("diffw"), 1.0 - LAMBDA_INIT, None, ALU.mult))

            def decay_exponents(h):
                link(TS(dtmp, dist, 0.0, pcols("ldb")[:, h:h + 1], ALU.min, ALU.mult))
                link(TS(decay[:, h, :], dist, 0.0, pcols("ldf")[:, h:h + 1], ALU.max, ALU.mult))
                TT(decay[:, h, :], decay[:, h, :], dtmp, ALU.subtract).then_inc(dexp_in, 1)
                v.wait_ge(dexp_in, h + 1)

            link(TS(sinT[DH:P], sinT[DH:P], -1.0, None, ALU.mult))

            def comb(u):
                v.wait_ge(exp_done, 2 * u + 2)
                link(nc.vector.reciprocal(rowinv[:, 2 * u:2 * u + 2], rowsum[:, 2 * u:2 * u + 2]))
                link(TT(lamc[:, u:u + 1], rowinv[:, 2 * u + 1:2 * u + 2], neglam, ALU.mult))
                p1, p2 = prob[:, 2 * (u % 2), :], prob[:, 2 * (u % 2) + 1, :]
                if u >= 2:
                    v.wait_ge(aT_done, u - 1)
                link(TS(amix[:, u % 2, :], p2, lamc[:, u:u + 1], None, ALU.mult))
                STT(amix[:, u % 2, :], p1, rowinv[:, 2 * u:2 * u + 1], amix[:, u % 2, :], ALU.mult, ALU.add
                    ).then_inc(comb_done, 1)

            def rope(r):
                q = r % 2
                dst = (qrT if r < 4 else krT)[:, r % 4, :]
                v.wait_ge(proj_evac, 20 + r + 1)
                if r == 0:
                    v.wait_ge(qkT_done, 8)
                TT(roped[:, 0, :], qsb[:, q, :], cosT, ALU.mult)
                TT(roped[0:DH, 1, :], qsb[DH:P, q, :], sinT[DH:P], ALU.mult)
                link(TT(roped[DH:P, 1, :], qsb[0:DH, q, :], sinT[0:DH], ALU.mult))
                TT(dst, roped[:, 0, :], roped[:, 1, :], ALU.add).then_inc(rope_done, 1)
                v.wait_ge(rope_done, r + 1)

            def o_sum(i):
                v.wait_ge(o_evac, i + 1)
                nc.vector.reduce_sum(sso[:, 0, 4 * i:4 * i + 4], sqs[:, 0:W].rearrange("p (h c) -> p h c", h=HEADS),
                                     AX.X).then_inc(o_sq, 1)

            for u in range(NB * HEADS):
                for s in range(2):
                    v.wait_ge(sc_done, 2 * u + s + 1)
                    nc.vector.tensor_reduce(negmax[:, 2 * u + s:2 * u + s + 1], bank(3 + 2 * (u % 2) + s), AX.X, ALU.max,
                                            negate=True).then_inc(max_ready, 1)
                comb(u)
                if u >= 9:
                    rope(u - 9)
                if u >= 5 and u % 4 == 1:
                    o_sum(u // 4 - 1)
                if u < HEADS:
                    decay_exponents(u)
            rope(7)
            o_sum(3)

            def mean_squares(k):
                v.wait_ge(o_sq if k == 0 else y_sq, NB)
                TS(mso[:, k, :], sso[:, k, :], 1.0 / DV, EPS, ALU.mult, ALU.add).then_inc(ms_o, 1)

            def finish_heads(k, rows):
                v.wait_ge(sd_o, k + 1)
                link(nc.vector.reciprocal(rso[:, k, :], mso[:, k, :]))
                flat = rows.rearrange("p b (h c) -> p (b h) c", h=HEADS)
                return TT(flat, flat, spread(rso[:, k, :], DV), ALU.mult)

            mean_squares(0)
            v.wait_ge(dexp_ready, HEADS)
            for q in range(NB * HEADS):
                h, m = divmod(q, NB)
                v.wait_ge(st_done, q + 1)
                if q >= 2:
                    v.wait_ge(yv_done, q - 1)
                a = (T - P) - P * m
                TT(std[:, q % 2, :], bank((6, 7, 0, 1)[q % 4]), decay[:, h, a:a + T], ALU.mult).then_inc(std_ready, 1)
                if q == NB:
                    finish_heads(0, orow).then_inc(o_ready, 1)
            v.wait_ge(sig_g, 1)
            gflat = gg.rearrange("p b c -> p (b c)")
            link(TT(gflat, gflat, sig, ALU.mult))
            def mix_columns(k, i):
                t = 4 * k + i
                v.wait_ge(mixT_done, t + 1)
                src = bank(6 + t % 2).rearrange("p (h t) -> p h t", h=HEADS)
                if k == 0:
                    TS(mixT[:, 4:8, i * P:(i + 1) * P], src, dw, None, ALU.mult).then_inc(mixT_ready, 1)
                else:
                    TT(mixT[:, 0:4, i * P:(i + 1) * P], src, spread(pcols("retw"), P), ALU.mult).then_inc(mixT_ready, 1)

            for i in range(NB):
                mix_columns(0, i)
            for i in range(NB):
                v.wait_ge(y_evac, i + 1)
                nc.vector.reduce_sum(sso[:, 1, 4 * i:4 * i + 4],
                                     sqs[:, (i % 2) * W:(i % 2 + 1) * W].rearrange("p (h c) -> p h c", h=HEADS),
                                     AX.X).then_inc(y_sq, 1)
            mean_squares(1)
            link(finish_heads(1, yrow))
            TT(yrow, yrow, gg, ALU.mult).then_inc(o_ready, 1)
            for i in range(NB):
                mix_columns(1, i)

            def h2_T(b):
                v.wait_ge(h2T_done, b + 1)
                if b >= 2:
                    v.wait_ge(lg_done, b - 1)
                TT(h2T[:, b % 2, :].rearrange("p (k t) -> p k t", k=KD),
                   wide(4 + 2 * (b % 2)).rearrange("p s (k t) -> p (s k) t", t=P),
                   spread(pcols("n2w"), P), ALU.mult).then_inc(h2T_ready, 1)

            def choose(b):
                v.wait_ge(lg_done, b + 1)
                TT(logits[:, b, :], bank(2 + b % 2, 0, NE), pcols("brt"), ALU.add).then_inc(lg_ready, 1)
                v.wait_ge(lg_ready, b + 1)
                link(nc.vector.max(top8[:, b, :], logits[:, b, :]))
                link(nc.vector.max_index(idx8[:, b, :], top8[:, b, :], logits[:, b, :]))

            for b in range(NB):
                for s in range(2):
                    w = 2 * b + s
                    v.wait_ge(op_done, w + 1)
                    cell = X[:, b, s * W:(s + 1) * W]
                    TT(cell, bank(w if w < 4 else w % 2), cell, ALU.add).then_inc(res_ready, 1)
                norm_x(b, NB + b)
                if b >= 1:
                    h2_T(b - 1)
            choose(0)
            choose(1)
            h2_T(NB - 1)
            choose(2)
            choose(3)
            link(TT(ev, top8[:, :, 0:TOPK], top8[:, :, 0:1].to_broadcast([P, NB, TOPK]), ALU.subtract))
            nc.vector.tensor_copy(topf, idx8[:, :, :]).then_inc(ev_in, 1)
            v.wait_ge(ev_in, 1)
            for k in range(TOPK):
                ins = TT(chose[:, k, :].rearrange("p (b e) -> p b e", b=NB),
                         iota_s[:, 0:NE].unsqueeze(1).to_broadcast([P, NB, NE]),
                         topf[:, :, k:k + 1].to_broadcast([P, NB, NE]), ALU.is_equal)
            link(ins)
            pairs = gated[:, 0:2, :]
            link(TT(pairs, chose[:, 0:2, :], chose[:, 2:4, :], ALU.add))
            TT(mask[:, :, :].rearrange("p b e -> p (b e)"), gated[:, 0, :], gated[:, 1, :], ALU.add).then_inc(mask_ready, 1)
            v.wait_ge(mask_ready, 1)
            v.wait_ge(ev_ready, 1)
            link(nc.vector.reduce_sum(esum, ev, AX.X))
            link(nc.vector.reciprocal(esum, esum))
            link(TT(gate4, ev, spread(esum, TOPK), ALU.mult))
            for k in range(TOPK):
                ins = TT(gated[:, k, :].rearrange("p (b e) -> p b e", b=NB),
                         chose[:, k, :].rearrange("p (b e) -> p b e", b=NB),
                         gate4[:, :, k:k + 1].to_broadcast([P, NB, NE]), ALU.mult)
            link(ins)
            link(TT(pairs, gated[:, 0:2, :], gated[:, 2:4, :], ALU.add))
            TT(gts.rearrange("p b e -> p (b e)"), gated[:, 0, :], gated[:, 1, :], ALU.add).then_inc(gts_ready, 1)
            v.wait_ge(gts_ready, 1)
            v.wait_ge(consts, 7)
            nc.vector.tensor_copy(tokens[:, :, :, 2], gts.rearrange("p b e -> p e b")).then_inc(table_ready, 1)
            v.wait_ge(rank_done, 1)
            link(STT(rank, bank(1, 0, NB * NE).rearrange("p (b e) -> p b e", b=NB), 1.0, mask[:, :, :], ALU.add, ALU.mult))

            def chunk_places(c):
                return TS(posm[:, c, :, :], rank.rearrange("p b e -> p e b"), -1.0 - CAP * c, None, ALU.add)

            link(chunk_places(0))

            def hot(n, at):
                TT(onehot, iota_s[:, 0:CAP].unsqueeze(1).to_broadcast([P, NB, CAP]),
                   spread(posm.rearrange("p c e b -> p (c e) b")[:, bass.ds(at, 1), :].rearrange("p a b -> p (a b)"), CAP), ALU.is_equal
                   ).then_inc(hot_ready, 1)

            def places(n, q, stored=None):
                v.wait_ge(idx_done, n + 1)
                if stored is not None:
                    v.wait_ge(y_stored[q], stored)
                nc.vector.tensor_copy(place_idx[0:CAP, q:q + 1], ps[0:CAP, 6, 0:1])
                nc.vector.tensor_copy(gate_at[0:CAP, q:q + 1], ps[0:CAP, 6, 2:3])
                at = ps[0:CAP, 6, 1:2]
                STT(vacant[0:CAP], at, 0.0, place_id[0:CAP], ALU.is_ge, ALU.mult).then_inc(vacant_ready, 1)
                v.wait_ge(vacant_ready, n + 1)
                STT(place_row[0:CAP, q:q + 1], at, float(T), vacant[0:CAP], ALU.add, ALU.add).then_inc(idx_ready, 1)

            def columns(n, q):
                v.wait_ge(hrT_done, n + 1)
                TT(htE[:, q, :].rearrange("p (k t) -> p k t", k=KD),
                   ps[:, 6:8, CAP:5 * CAP].rearrange("p s (k t) -> p s k t", t=CAP),
                   spread(pcols("n2w").rearrange("p (s k) -> p s k", s=2), CAP), ALU.mult).then_inc(htE_ready, 1)

            def swiglu(n, e, t, first=False):
                v.wait_ge(up_done, 4 * n + (t + 1))
                if t >= 2 or not first:
                    v.wait_ge(act_ready, 4 * n + (t - 1))
                TT(ub[:, t % 2, :].rearrange("p (m t) -> p m t", t=CAP), ps[:, t, 0:4 * CAP].rearrange("p (m t) -> p m t", t=CAP),
                   spread(b1_sb[:, bass.ds(e, 1), 4 * t:4 * t + 4].rearrange("p a m -> p (a m)"), CAP), ALU.add
                   ).then_inc(ub_ready, 1)
                glu, lin = ub[:, t % 2, 0:2 * CAP], ub[:, t % 2, 2 * CAP:4 * CAP]
                v.wait_ge(ub_ready, 4 * n + (t + 1))
                TS(glu, glu, LIMIT, None, ALU.min).then_inc(glu_ready, 1)
                TS(lin, lin, LIMIT, -LIMIT, ALU.min, ALU.max).then_inc(lin_ready, 1)
                v.wait_ge(lin_ready, 4 * n + (t + 1))
                STT(lin, lin, 1.0, glu, ALU.add, ALU.mult).then_inc(gl_ready, 1)

            def swiglu_end(n, t):
                lin = ub[:, t % 2, 2 * CAP:4 * CAP]
                v.wait_ge(gl_ready, 4 * n + (t + 1))
                v.wait_ge(sg_ready, 4 * n + (t + 1))
                TT(actT[:, 2 * t:2 * t + 2, :], lin.rearrange("p (m t) -> p m t", t=CAP),
                   sg[:, t % 2, :].rearrange("p (m t) -> p m t", t=CAP), ALU.mult).then_inc(act_ready, 1)

            def act_low(n, t):
                v.wait_ge(acthi_ready, 4 * n + (t + 1))
                TT(act_lo[:, 2 * t:2 * t + 2, :], actT[:, 2 * t:2 * t + 2, :], act_hi[:, 2 * t:2 * t + 2, :].bitcast(f32),
                   ALU.subtract).then_inc(actlo_ready, 1)

            def w_low(n, j):
                s, k = divmod(j, KD)
                v.wait_ge(whi_ready, 2 * KD * n + (j + 1))
                TT(w_lo[:, j % SLICES, :], pair(2 * ORDER[4 + s])[:, k, :], w_hi[:, j % SLICES, :].bitcast(f32),
                   ALU.subtract).then_inc(wlo_ready, 1)

            def later_half(n, e, first=False, next_rows=None):
                swiglu(n, e, 2, first)
                swiglu_end(n, 2)
                act_low(n, 1)
                if next_rows is not None:
                    columns(n + 1, next_rows)
                for j in range(SLICES):
                    w_low(n, j)
                act_low(n, 2)
                swiglu(n, e, 3, first)
                w_low(n, SLICES)
                swiglu_end(n, 3)
                w_low(n, SLICES + 1)
                act_low(n, 3)

            def expert(n, q, stored=None, first=False, last=False):
                if not last:
                    v.wait_ge(idx_done, n + 1)
                    hot(n + 1, n + 1)
                swiglu(n, n, 0, first)
                swiglu_end(n, 0)
                if not last:
                    places(n + 1, 1 - q, stored)
                swiglu(n, n, 1, first)
                swiglu_end(n, 1)
                act_low(n, 0)
                later_half(n, n, first, None if last else 1 - q)
                for j in range(SLICES + 2, 2 * KD):
                    w_low(n, j)

            v.wait_ge(b_in, 32)
            hot(0, 0)
            places(0, 0)
            for c in range(1, MAX_CHUNK):
                ins = chunk_places(c)
            link(ins)
            for c in range(1, MAX_CHUNK):
                key = over_key[:, c - 1, :]
                link(TS(key, iota_s[:, 0:NE], 1.0 + NE * c, None, ALU.add))
                link(STT(key, bank(1, NB * NE, NE), float(CAP * c), key, ALU.is_gt, ALU.mult))
            keys = over_key.rearrange("p c e -> p (c e)")
            for i in range(MAX_OVER // 8):
                top = over_top[:, 8 * i:8 * i + 8]
                link(nc.vector.max(top, keys))
                if i < MAX_OVER // 8 - 1:
                    link(nc.vector.match_replace(out=keys, in_to_replace=top, in_values=keys, imm_value=0.0))
            link(TS(over_some, over_top, 0.0, None, ALU.is_gt))
            link(nc.vector.reduce_sum(over_n, over_some, AX.X))
            link(nc.vector.tensor_copy(over_at[:, MAX_OVER:MAX_OVER + 1], over_n))
            link(TS(over_at[:, 0:MAX_OVER], over_top, -1.0, None, ALU.add))
            TS(over_e[:, :], over_at[:, 0:MAX_OVER], NE - 1, None, ALU.bitwise_and).then_inc(over_ready, 1)
            for w in range(2 * NB):
                v.wait_ge(bias_done, w + 1)
                cell = X[:, w // 2, w % 2 * W:(w % 2 + 1) * W]
                TT(cell, bank((3, 4, 5, 0)[w % 4]), cell, ALU.add).then_inc(bias_added, 1)
            columns(0, 0)
            expert(0, 0, first=True)
            with v.Fori(0, NE // 2 - 1) as i:
                expert(2 * i + 1, 1, 16 * i + 16)
                expert(2 * i + 2, 0, 16 * i + 16)
            expert(NE - 1, 1, last=True)

            def over_pass(n, e, at):
                v.wait_ge(idx_done, n)
                hot(n, at)
                places(n, 0, 16 * n - 8 * NE)
                columns(n, 0)
                for t in range(2):
                    swiglu(n, e, t)
                    swiglu_end(n, t)
                act_low(n, 0)
                later_half(n, e)
                for j in range(SLICES + 2, 2 * KD):
                    w_low(n, j)

            further(v, over_pass)

        @block.tensor
        def _(pe):
            MM, TR = nc.tensor.matmul, nc.tensor.transpose
            pe.wait_ge(consts, 4)

            def turn_x(b):
                pe.wait_ge(xs_ready, b + 1)
                for k in range(KD):
                    t = TR(bank(2 * b + k // 4, (k % 4) * P, P), xs[:, b % 2, k * P:(k + 1) * P], ident[:, :])
                t.then_inc(xT_done, 1)

            def project(j):
                g, i = divmod(j, 4)
                if g == 0:
                    pe.wait_ge(hT_ready, i + 1)
                if i == 0 and g:
                    pe.wait_ge(ring_in[2 * (g % 3)], 16 * (g // 3 + (g % 3 > 0)))
                if j >= 2:
                    pe.wait_ge(proj_evac, j - 1)
                wt = pair(2 * (g % 3))
                for k in range(KD):
                    if j == 0 and k % 2 == 0:
                        pe.wait_ge(first_in[k // 2], 16)
                    if g < 5:
                        lhs, rhs = hT[:, k, i * P:(i + 1) * P], wt[:, k, :]
                    else:
                        lhs, rhs = wt[:, k, i * P:(i + 1) * P], hT[:, k, :]
                    m = MM(bank(j % 2), lhs, rhs, start=k == 0, stop=k == KD - 1)
                m.then_inc(proj_done, 1)

            turn_x(0)
            turn_x(1)
            project(0)
            turn_x(2)
            turn_x(3)
            for j in range(1, 12):
                project(j)
            for g, r in enumerate((rq, rk)):
                pe.wait_ge(qk_ready, g + 1)
                for i in range(NB):
                    if g == 1:
                        pe.wait_ge(qkT_evac, i + 1)
                    for h in range(HEADS):
                        t = TR(bank(3 + i, h * P, P), r[:, i, h * P:(h + 1) * P], ident[:, :])
                    t.then_inc(qkT_done, 1)

            def scores(u):
                i, h = divmod(u, HEADS)
                if u == 0:
                    pe.wait_ge(qkT_evac, 8)
                if u >= 2:
                    pe.wait_ge(exp_done, 2 * u - 2)
                for s in range(2):
                    MM(bank(3 + 2 * (u % 2) + s), qdT[s * DH:(s + 1) * DH, h, i * P:(i + 1) * P],
                       kdT[s * DH:(s + 1) * DH, h, :], start=True, stop=True).then_inc(sc_done, 1)

            def turn(u):
                pe.wait_ge(comb_done, u + 1)
                if u >= 1:
                    pe.wait_ge(aT_evac, u)
                for k in range(NB):
                    t = TR(bank(7, k * P, P), amix[:, u % 2, k * P:(k + 1) * P], ident[:, :])
                t.then_inc(aT_done, 1)

            def values(u):
                i, h = divmod(u, HEADS)
                pe.wait_ge(aT_evac, u + 1)
                if h == 0 and i >= 1:
                    pe.wait_ge(o_evac, i)
                for k in range(NB):
                    m = MM(bank(2, h * DV, DV), aT[:, u % 2, k * P:(k + 1) * P], vd[:, k, h * DV:(h + 1) * DV],
                           start=k == 0, stop=k == NB - 1)
                m.then_inc(av_done, 1)

            for u in range(NB * HEADS):
                scores(u)
                project(12 + u)
                if u >= 1:
                    turn(u - 1)
                if u >= 2:
                    values(u - 2)
            turn(15)
            values(14)
            values(15)

            def ret_scores(q):
                h, m = divmod(q, NB)
                if m == 0:
                    pe.wait_ge(rope_done, HEADS + 1 + h)
                if q == 0:
                    pe.wait_ge(exp_done, 32)
                    pe.wait_ge(aT_evac, 16)
                if q == 2:
                    pe.wait_ge(proj_evac, 28)
                if q >= 4:
                    pe.wait_ge(std_ready, q - 3)
                MM(bank((6, 7, 0, 1)[q % 4]), krT[:, h, m * P:(m + 1) * P], qrT[:, h, :], start=True, stop=True
                   ).then_inc(st_done, 1)

            def ret_values(q):
                h, m = divmod(q, NB)
                if q == 0:
                    pe.wait_ge(o_evac, NB)
                pe.wait_ge(std_ready, q + 1)
                for i in range(NB):
                    t = MM(bank(2 + i, h * DV, DV), std[:, q % 2, i * P:(i + 1) * P], vr[:, m, h * DV:(h + 1) * DV],
                           start=m == 0, stop=m == NB - 1)
                t.then_inc(yv_done, 1)

            ret_scores(0)
            ret_scores(1)
            for q in range(NB * HEADS):
                if q + 2 < NB * HEADS:
                    ret_scores(q + 2)
                ret_values(q)

            def turn_mix(k, rows):
                pe.wait_ge(o_ready, k + 1)
                for i in range(NB):
                    t = 4 * k + i
                    if t == 0:
                        pe.wait_ge(std_ready, NB * HEADS)
                    if t >= 2:
                        pe.wait_ge(mixT_ready, t - 1)
                    for h in range(HEADS):
                        m = TR(bank(6 + t % 2, h * P, P), rows[:, i, h * P:(h + 1) * P], ident[:, :])
                    m.then_inc(mixT_done, 1)

            def out_project(w, half):
                b, s = divmod(w, 2)
                if half and b == 0:
                    pe.wait_ge(ring_in[2 + 2 * s], 16 * 3)
                if half and w in (2, 3):
                    pe.wait_ge(y_evac, w - 1)
                if w >= 4 and half:
                    pe.wait_ge(res_ready, (1, 2, 5, 6)[w - 4])
                pe.wait_ge(mixT_ready, b + 1 if half else NB + b + 1)
                for k in range(4 * half, 4 * half + 4):
                    m = MM(bank(w if w < 4 else w % 2), mixT[:, k, b * P:(b + 1) * P], pair(2 + 2 * s)[:, k, :],
                           start=k == 4, stop=k == 3)
                if not half:
                    m.then_inc(op_done, 1)

            turn_mix(0, orow)
            for w in range(4):
                out_project(w, 1)
            turn_mix(1, yrow)

            def h2_turn(b):
                pe.wait_ge(h2_ready, b + 1)
                if b == 0:
                    pe.wait_ge(mixT_ready, 8)
                if b >= 2:
                    pe.wait_ge(h2T_ready, b - 1)
                for k in range(KD):
                    m = TR(bank(4 + 2 * (b % 2) + k // 4, (k % 4) * P, P), h2[:, b, k * P:(k + 1) * P], ident[:, :])
                m.then_inc(h2T_done, 1)

            def route(b):
                pe.wait_ge(h2T_ready, b + 1)
                if b == 0:
                    pe.wait_ge(wr_in, 16)
                if b >= 2:
                    pe.wait_ge(lg_ready, b - 1)
                for k in range(KD):
                    m = MM(bank(2 + b % 2, 0, NE), h2T[:, b % 2, k * P:(k + 1) * P], wr_sb[:, k, :],
                           start=k == 0, stop=k == KD - 1)
                m.then_inc(lg_done, 1)

            for b in range(NB):
                for w in (2 * b, 2 * b + 1):
                    if b >= 2:
                        out_project(w, 1)
                    out_project(w, 0)
                    if w == 6:
                        route(0)
                if b >= 1:
                    h2_turn(b - 1)
            route(1)
            h2_turn(NB - 1)
            route(2)
            route(NB - 1)
            pe.wait_ge(lg_ready, NB)
            pe.wait_ge(mask_ready, 1)
            for b in range(NB):
                for c in range(b + 1):
                    m = MM(bank(1, b * NE, NE), (before if c == b else ones)[:, :], mask[:, c, :],
                           start=c == 0, stop=c == b)
            for c in range(NB):
                m = MM(bank(1, NB * NE, NE), ones[:, :], mask[:, c, :], start=c == 0, stop=c == NB - 1)
            m.then_inc(rank_done, 1)

            def index(n, e):
                pe.wait_ge(hot_ready, n + 1)
                for b in range(NB):
                    m = MM(ps[0:CAP, 6, 0:3], onehot[:, b, :],
                           tokens[:, bass.ds(e, 1), b, :].rearrange("p a c -> p (a c)"), start=b == 0, stop=b == NB - 1)
                m.then_inc(idx_done, 1)

            def turn_rows(n, q, k_th):
                pe.wait_ge(row_in[q], k_th)
                for k in range(KD):
                    m = TR(bank(6 + k // 4, (k % 4 + 1) * CAP, CAP), hrow[:, q, k * P:(k + 1) * P], ident[0:CAP, 0:CAP])
                m.then_inc(hrT_done, 1)

            def weights(n, c):
                s = ORDER[c]
                pe.wait_ge(ring_in[2 * s], 16 * n + 16 * (FRONT_LOADS[s] + 1))

            def up(n, q, r):
                t, j = divmod(r, 4)
                c = 2 * (t // 2) + j // 2
                if r % 8 == 0:
                    weights(n, c)
                    if r == 0:
                        pe.wait_ge(htE_ready, n + 1)
                if r % 8 == 2:
                    weights(n, c)
                col = (2 * (t % 2) + j % 2) * P
                for k in range(KD):
                    m = MM(bank(t, j * CAP, CAP), pair(2 * ORDER[c])[:, k, col:col + P],
                           htE[:, q, k * CAP:(k + 1) * CAP], start=k == 0, stop=k == KD - 1)
                if j == 3:
                    m.then_inc(up_done, 1)
                elif r % 8 == 5:
                    m.then_inc(chunk_used, 1)

            def down(n):
                for j in range(2 * KD):
                    s, k = divmod(j, KD)
                    if s == 0 and k % 2 == 0:
                        pe.wait_ge(actlo_ready, 4 * n + (k // 2 + 1))
                    pe.wait_ge(wlo_ready, 2 * KD * n + (j + 1))
                    out, hi = ps[0:CAP, 4 + s, :], w_hi[:, j % SLICES, :]
                    MM(out, act_hi[:, k, :], hi, start=k == 0, stop=False)
                    MM(out, act_hi[:, k, :], w_lo[:, j % SLICES, :], start=False, stop=False)
                    MM(out, act_lo[:, k, :], hi, start=False, stop=k == KD - 1).then_inc(slice_used, 1)

            def expert(n, q, rows_next, first=False, last=False):
                for r in range(4):
                    up(n, q, r)
                if not last:
                    index(n + 1, n + 1)
                for r in range(4, 12):
                    up(n, q, r)
                if not last:
                    turn_rows(n + 1, 1 - q, rows_next)
                for r in range(12, 16):
                    up(n, q, r)
                if not first:
                    pe.wait_ge(y_ready, n)
                down(n)

            def gate_biases():
                for w in range(2 * NB):
                    if w >= 4:
                        pe.wait_ge(bias_added, w - 3)
                    MM(bank((3, 4, 5, 0)[w % 4]), gatesT[:, w // 2 * P:(w // 2 + 1) * P], b2_sb[:, w % 2 * W:(w % 2 + 1) * W],
                       start=True, stop=True).then_inc(bias_done, 1)

            pe.wait_ge(table_ready, 1)
            index(0, 0)
            pe.wait_ge(gts_ready, 1)
            for b in range(NB):
                m = TR(ps[0:NE, 2, b * P:(b + 1) * P], gts[:, b, :], ident[:, :])
            m.then_inc(gT_done, 1)
            pe.wait_ge(gT_ready, 1)
            pe.wait_ge(b_in, 32)
            gate_biases()
            turn_rows(0, 0, 16)
            pe.wait_ge(bias_added, 2 * NB)
            expert(0, 0, 16, first=True)
            with pe.Fori(0, NE // 2 - 1) as i:
                expert(2 * i + 1, 1, 16 * i + 32)
                expert(2 * i + 2, 0, 16 * i + 32)
            expert(NE - 1, 1, None, last=True)

            def over_pass(n, e, at):
                index(n, e)
                turn_rows(n, 0, 16 * n + (16 - 16 * (NE // 2)))
                for r in range(16):
                    up(n, 0, r)
                pe.wait_ge(y_ready, n)
                down(n)

            further(pe, over_pass)


def kernel(x, positions, norm1_w, w_in, ret_log_decay_fwd, ret_log_decay_bwd, ret_norm_w,
           q_norm_w, k_norm_w, lambda_q1, lambda_k1, lambda_q2, lambda_k2, diff_norm_w,
           w_out, norm2_w, w_router, b_router, w1, b1, w2, b2):
    import concourse.bacc as bacc
    from concourse.bass_utils import run_bass_kernel_spmd as run

    def rows(a):
        return np.broadcast_to(np.asarray(a).reshape(1, -1), (P, np.asarray(a).size))

    ramp = np.arange(64, dtype=np.float32) * np.float32(1 / 63)
    inv_ret = (10000.0 ** (-ramp.astype(np.float64))).astype(np.float32)
    inv_diff = (500000.0 ** (-np.arange(0, ROT, 2) / ROT)).astype(np.float32)
    par = np.concatenate([
        np.asarray(norm1_w).reshape(KD, P).T, np.asarray(norm2_w).reshape(KD, P).T,
        np.asarray(ret_norm_w).reshape(HEADS, P).T, np.asarray(diff_norm_w).reshape(1, P).T,
        np.concatenate([inv_ret, inv_ret]).reshape(P, 1), rows(inv_diff),
        rows(ret_log_decay_fwd), rows(ret_log_decay_bwd), rows(q_norm_w), rows(k_norm_w),
        rows(lambda_q1), rows(lambda_k1), rows(lambda_q2), rows(lambda_k2), rows(b_router)], axis=1)
    pos = np.concatenate([rows(positions), np.asarray(positions).reshape(NB, P).T], axis=1)
    b1t = np.asarray(b1).reshape(NE, 2, 4, 2, P).transpose(4, 0, 2, 1, 3).reshape(P, NE * 16)
    arrays = {"x": x, "w_in": w_in, "w_out": w_out, "w_router": w_router, "w1": w1, "w2": w2, "b1t": b1t, "b2": b2,
              "par": par, "pos": pos}
    arrays = {n: np.ascontiguousarray(a) for n, a in arrays.items()}
    nc = bacc.Bacc("TRN2", target_bir_lowering=False, num_devices=1, dynamic_dma_scratch_size=4096)
    aps = {n: nc.dram_tensor(f"in_{n}", a.shape, mybir.dt.from_np(a.dtype), kind="ExternalInput").ap()
           for n, a in arrays.items()}
    out = nc.dram_tensor("out", (1, T, D), mybir.dt.float32, kind="ExternalOutput").ap()
    h2_rows = nc.dram_tensor("h2_rows", (T, D), mybir.dt.float32, kind="Internal").ap()
    sums = nc.dram_tensor("sums", (T + CAP, D), mybir.dt.float32, kind="Internal").ap()
    build_layer(nc, out=out, h2_rows=h2_rows, sums=sums, **aps)
    r = run(nc, [{f"in_{n}": a for n, a in arrays.items()}], core_ids=[0])
    return r.results[0]["out"]
```
